# Optimizing a Trainium2 kernel written in Bass

```python
import math
import jax
import jax.numpy as jnp
from jax import lax
import numpy as np

D_MODEL = 1024
BATCH = 1
SEQ = 512
DEPTH = 2

HEAD_DIM = 64
A_HEADS = 8
A_WIDTH = A_HEADS * HEAD_DIM
DECAY_LORA = 64
ICLR_LORA = 64
VRES_LORA = 32
GATE_LORA = 128
GN_EPS = 64e-5
B_HEADS = 8
B_WIDTH = B_HEADS * HEAD_DIM
KV_RANK = 128
IDX_HEADS = 8
IDX_DIM = 64
IDX_TOPK_MAX = 256
C_HEADS = 16
C_WIDTH = C_HEADS * HEAD_DIM
N_GROUPS = 4
EXPERTS_PER_GROUP = 8
N_EXPERTS = N_GROUPS * EXPERTS_PER_GROUP
EXPERT_FF = 512
TOP_K_EXPERTS = 2
MOE_BLOCK = 128
Q_BLOCK = 128
RMS_EPS = 1e-6
N_EVEN = (DEPTH + 1) // 2
N_ODD = DEPTH // 2
EVEN_SPLIT_SIZES = (A_WIDTH, A_WIDTH, A_WIDTH, B_WIDTH, KV_RANK, IDX_HEADS * IDX_DIM, IDX_DIM, IDX_HEADS)
IN_EVEN = sum(EVEN_SPLIT_SIZES)

kernel_name = "hybrid_rwkv7_dsa_stickbreak_hmoe"

def rmsnorm(x, g):
    xf = x.astype(jnp.float32)
    y = xf * lax.rsqrt(jnp.mean(xf * xf, axis=-1, keepdims=True) + RMS_EPS)
    return (y * g.astype(jnp.float32)).astype(x.dtype)

def token_shift(z):
    return jnp.concatenate([jnp.zeros_like(z[:, :1]), z[:, :-1]], axis=1)

def rwkv7_scan(r, w, k, v, kk, a):
    b, t, h, n = r.shape

    def step(state, inp):
        r_t, w_t, k_t, v_t, kk_t, a_t = inp
        s_kk = jnp.einsum('bhvk,bhk->bhv', state, kk_t)
        state = (state * w_t[:, :, None, :]
                 - s_kk[..., None] * (kk_t * a_t)[:, :, None, :]
                 + v_t[..., None] * k_t[:, :, None, :])
        return state, jnp.einsum('bhvk,bhk->bhv', state, r_t)

    xs = tuple(jnp.moveaxis(z, 1, 0) for z in (r, w, k, v, kk, a))
    _, ys = lax.scan(step, jnp.zeros((b, h, n, n), jnp.float32), xs)
    return jnp.moveaxis(ys, 0, 1)

def rwkv7_time_mix(h, r, k, v, mu_rkv, mu_lora, w0, w1, w2, a0, a1, a2, g1, g2,
                   k_k, k_a, r_k, ln_g, ln_b, vres):
    f32 = jnp.float32
    b, t, _ = h.shape
    rkv = jnp.stack([r, k, v], axis=2)
    rkv = rkv + (token_shift(rkv) - rkv) * mu_rkv
    r, k, v = rkv[:, :, 0], rkv[:, :, 1], rkv[:, :, 2]
    dh = token_shift(h) - h
    xw = h + dh * mu_lora[0]
    xa = h + dh * mu_lora[1]
    xg = h + dh * mu_lora[2]
    decay = jnp.exp(-math.exp(-0.5) * jax.nn.sigmoid((w0 + jnp.tanh(xw @ w1) @ w2).astype(f32)))
    iclr = jax.nn.sigmoid((a0 + (xa @ a1) @ a2).astype(f32))
    gate = jax.nn.sigmoid(xg @ g1) @ g2
    if vres is not None:
        v_first, mu_v, v0, v1, v2 = vres
        xv = h + dh * mu_v
        v = v + (v_first - v) * jax.nn.sigmoid(v0 + (xv @ v1) @ v2)

    def heads(z):
        return z.astype(f32).reshape(b, t, A_HEADS, HEAD_DIM)

    kk = heads(k * k_k)
    kk = kk * lax.rsqrt(jnp.maximum(jnp.sum(kk * kk, axis=-1, keepdims=True), 1e-12))
    k_mod = k.astype(f32) * (1.0 + (iclr - 1.0) * k_a)
    r_h, k_h, v_h = heads(r), heads(k_mod), heads(v)
    y = rwkv7_scan(r_h, heads(decay), k_h, v_h, kk, heads(iclr))
    yc = y - jnp.mean(y, axis=-1, keepdims=True)
    y = yc * lax.rsqrt(jnp.mean(yc * yc, axis=-1, keepdims=True) + GN_EPS)
    bonus = jnp.sum(r_h * k_h * r_k, axis=-1, keepdims=True) * v_h
    y = y.reshape(b, t, A_WIDTH) * ln_g + ln_b + bonus.reshape(b, t, A_WIDTH)
    return (y * gate).astype(h.dtype), v

def dsa_sparse_attention(q, c_kv, q_idx, k_idx, w_idx, kv_norm, w_kv_up, idx_k_norm):
    b, t = q.shape[0], q.shape[1]
    n_blk = t // Q_BLOCK
    topk = min(IDX_TOPK_MAX, t // 4)
    kv = (rmsnorm(c_kv, kv_norm) @ w_kv_up).reshape(b, t, 2, B_HEADS, HEAD_DIM)
    k_i = rmsnorm(k_idx, idx_k_norm)
    q_blk = q.reshape(b, n_blk, Q_BLOCK, B_HEADS, HEAD_DIM).swapaxes(0, 1)
    qi_blk = q_idx.reshape(b, n_blk, Q_BLOCK, IDX_HEADS, IDX_DIM).swapaxes(0, 1)
    wi_blk = w_idx.reshape(b, n_blk, Q_BLOCK, IDX_HEADS).swapaxes(0, 1)
    key_pos = jnp.arange(t)

    def one_block(args):
        blk, qb, qib, wib = args
        q_pos = blk * Q_BLOCK + jnp.arange(Q_BLOCK)
        dots = jnp.einsum('bqhd,bsd->bqhs', qib, k_i).astype(jnp.float32) * IDX_DIM ** -0.5
        score = jnp.einsum('bqhs,bqh->bqs', jax.nn.relu(dots), wib.astype(jnp.float32)) * IDX_HEADS ** -0.5
        causal = key_pos[None, :] <= q_pos[:, None]
        score = jnp.where(causal[None], score, -jnp.inf)
        _, sel = lax.top_k(score, topk)
        valid = sel <= q_pos[None, :, None]
        kv_sel = jax.vmap(lambda kv_b, sel_b: kv_b[sel_b])(kv, sel)
        logits = jnp.einsum('bqhd,bqkhd->bhqk', qb, kv_sel[:, :, :, 0]).astype(jnp.float32) * HEAD_DIM ** -0.5
        logits = jnp.where(valid[:, None], logits, -jnp.inf)
        p = jax.nn.softmax(logits, axis=-1).astype(kv.dtype)
        return jnp.einsum('bhqk,bqkhd->bqhd', p, kv_sel[:, :, :, 1])

    o = lax.map(one_block, (jnp.arange(n_blk), q_blk, qi_blk, wi_blk))
    return o.swapaxes(0, 1).reshape(b, t, B_WIDTH)

def stick_breaking_attention(q, k, v):
    b, t, _, _ = q.shape
    n_blk = t // Q_BLOCK
    q_blk = q.reshape(b, n_blk, Q_BLOCK, C_HEADS, HEAD_DIM).swapaxes(0, 1)
    key_pos = jnp.arange(t)

    def one_block(args):
        blk, qb = args
        q_pos = blk * Q_BLOCK + jnp.arange(Q_BLOCK)
        z = jnp.einsum('bqhd,bshd->bhqs', qb, k).astype(jnp.float32) * HEAD_DIM ** -0.5
        before = key_pos[None, :] < q_pos[:, None]
        log_keep = jnp.where(before, jax.nn.log_sigmoid(-z), 0.0)
        log_tail = lax.cumsum(log_keep, axis=3, reverse=True) - log_keep
        weight = jnp.where(before, jnp.exp(jax.nn.log_sigmoid(z) + log_tail), 0.0)
        return jnp.einsum('bhqs,bshd->bqhd', weight.astype(v.dtype), v)

    o = lax.map(one_block, (jnp.arange(n_blk), q_blk))
    return o.swapaxes(0, 1).reshape(b, t, C_WIDTH)

def routed_experts(xf, expert_idx, gates, w1, w3, w2):
    n_tok, d = xf.shape
    n_asg = n_tok * TOP_K_EXPERTS
    flat_e = expert_idx.reshape(n_asg)
    order = jnp.argsort(flat_e)
    sorted_e = flat_e[order]
    counts = jnp.zeros((N_EXPERTS,), jnp.int32).at[flat_e].add(1)
    padded = (counts + MOE_BLOCK - 1) // MOE_BLOCK * MOE_BLOCK
    seg_start = jnp.cumsum(counts) - counts
    pad_end = jnp.cumsum(padded)
    pad_start = pad_end - padded
    dest = pad_start[sorted_e] + (jnp.arange(n_asg) - seg_start[sorted_e])
    n_blocks = (n_asg + MOE_BLOCK - 1) // MOE_BLOCK + N_EXPERTS
    n_rows = n_blocks * MOE_BLOCK
    x_rows = jnp.zeros((n_rows, d), xf.dtype).at[dest].set(xf[order // TOP_K_EXPERTS])
    blk_expert = jnp.minimum(jnp.searchsorted(pad_end, jnp.arange(n_blocks) * MOE_BLOCK, side='right'), N_EXPERTS - 1)

    def expert_block(args):
        xb, e = args
        return (jax.nn.silu(xb @ w1[e]) * (xb @ w3[e])) @ w2[e]

    y_rows = lax.map(expert_block, (x_rows.reshape(n_blocks, MOE_BLOCK, d), blk_expert)).reshape(n_rows, d)
    y_asg = jnp.zeros((n_asg, d), y_rows.dtype).at[order].set(y_rows[dest])
    y = jnp.sum(y_asg.reshape(n_tok, TOP_K_EXPERTS, d).astype(jnp.float32) * gates[..., None], axis=1)
    return y.astype(xf.dtype)

def hierarchical_moe(h, router_group, router_expert, w1, w3, w2):
    b, t, d = h.shape
    xf = h.reshape(b * t, d)
    g_logits = (xf @ router_group).astype(jnp.float32)
    g_prob = jax.nn.softmax(g_logits, axis=-1)
    g_sel = jnp.argmax(g_logits, axis=-1)
    g_gate = jnp.take_along_axis(g_prob, g_sel[:, None], axis=1)
    e_logits = jnp.einsum('nd,gde->nge', xf, router_expert).astype(jnp.float32)
    e_logits = jnp.take_along_axis(e_logits, g_sel[:, None, None], axis=1)[:, 0]
    top_p, top_i = lax.top_k(jax.nn.softmax(e_logits, axis=-1), TOP_K_EXPERTS)
    gates = g_gate * top_p / jnp.sum(top_p, axis=-1, keepdims=True)
    expert_idx = g_sel[:, None].astype(jnp.int32) * EXPERTS_PER_GROUP + top_i.astype(jnp.int32)
    return routed_experts(xf, expert_idx, gates, w1, w3, w2).reshape(b, t, d)

def setup_inputs(seed: int = 0) -> dict:
    key = jax.random.key(seed)
    ks = iter(jax.random.split(key, 48))
    D = D_MODEL
    NE, NO = N_EVEN, N_ODD
    res_scale = (2.0 * DEPTH) ** -0.5

    def nrm(shape, scale):
        return jax.random.normal(next(ks), shape, jnp.float32) * scale

    def gain(shape):
        return 1.0 + nrm(shape, 0.02)

    def unif(shape):
        return jax.random.uniform(next(ks), shape, jnp.float32, 0.0, 1.0)

    return {
        'x': nrm((BATCH, SEQ, D), 1.0),
        'ev_norm': gain((NE, D)),
        'ev_w_in': nrm((NE, D, IN_EVEN), D ** -0.5),
        'ev_w_out': nrm((NE, A_WIDTH + B_WIDTH, D), (A_WIDTH + B_WIDTH) ** -0.5 * res_scale),
        'a_mu_rkv': unif((NE, 3, A_WIDTH)),
        'a_mu_lora': unif((NE, 3, D)),
        'a_w0': nrm((NE, A_WIDTH), 0.5),
        'a_w1': nrm((NE, D, DECAY_LORA), D ** -0.5),
        'a_w2': nrm((NE, DECAY_LORA, A_WIDTH), 0.5 * DECAY_LORA ** -0.5),
        'a_a0': nrm((NE, A_WIDTH), 0.1),
        'a_a1': nrm((NE, D, ICLR_LORA), D ** -0.5),
        'a_a2': nrm((NE, ICLR_LORA, A_WIDTH), 0.5 * ICLR_LORA ** -0.5),
        'a_g1': nrm((NE, D, GATE_LORA), D ** -0.5),
        'a_g2': nrm((NE, GATE_LORA, A_WIDTH), GATE_LORA ** -0.5),
        'a_k_k': 0.85 + nrm((NE, A_WIDTH), 0.02),
        'a_k_a': 1.0 + nrm((NE, A_WIDTH), 0.02),
        'a_r_k': nrm((NE, A_HEADS, HEAD_DIM), 0.1),
        'a_ln_g': gain((NE, A_WIDTH)),
        'a_ln_b': nrm((NE, A_WIDTH), 0.02),
        'a_mu_vres': unif((NE - 1, D)),
        'a_v0': nrm((NE - 1, A_WIDTH), 0.5),
        'a_v1': nrm((NE - 1, D, VRES_LORA), D ** -0.5),
        'a_v2': nrm((NE - 1, VRES_LORA, A_WIDTH), 0.5 * VRES_LORA ** -0.5),
        'b_kv_norm': gain((NE, KV_RANK)),
        'b_w_kv_up': nrm((NE, KV_RANK, 2 * B_WIDTH), KV_RANK ** -0.5),
        'b_idx_k_norm': gain((NE, IDX_DIM)),
        'od_norm': gain((NO, D)),
        'od_w_qkv': nrm((NO, D, 3 * C_WIDTH), D ** -0.5),
        'od_w_out': nrm((NO, C_WIDTH, D), C_WIDTH ** -0.5 * res_scale),
        'moe_norm': gain((DEPTH, D)),
        'moe_router_group': nrm((DEPTH, D, N_GROUPS), D ** -0.5),
        'moe_router_expert': nrm((DEPTH, N_GROUPS, D, EXPERTS_PER_GROUP), D ** -0.5),
        'moe_w1': nrm((DEPTH, N_EXPERTS, D, EXPERT_FF), D ** -0.5),
        'moe_w3': nrm((DEPTH, N_EXPERTS, D, EXPERT_FF), D ** -0.5),
        'moe_w2': nrm((DEPTH, N_EXPERTS, EXPERT_FF, D), EXPERT_FF ** -0.5 * res_scale),
        'final_norm': gain((D,)),
    }

def reference(x, ev_norm, ev_w_in, ev_w_out, a_mu_rkv, a_mu_lora, a_w0, a_w1, a_w2,
              a_a0, a_a1, a_a2, a_g1, a_g2, a_k_k, a_k_a, a_r_k, a_ln_g, a_ln_b,
              a_mu_vres, a_v0, a_v1, a_v2, b_kv_norm, b_w_kv_up, b_idx_k_norm,
              od_norm, od_w_qkv, od_w_out, moe_norm, moe_router_group, moe_router_expert,
              moe_w1, moe_w3, moe_w2, final_norm):
    b, t, _ = x.shape
    split_points = [int(s) for s in np.cumsum(EVEN_SPLIT_SIZES)[:-1]]
    v_first = None
    for i in range(DEPTH):
        if i % 2 == 0:
            e = i // 2
            h = rmsnorm(x, ev_norm[e])
            r, k, v, q_b, c_kv, q_idx, k_idx, w_idx = jnp.split(h @ ev_w_in[e], split_points, axis=-1)
            vres = None if e == 0 else (v_first, a_mu_vres[e - 1], a_v0[e - 1], a_v1[e - 1], a_v2[e - 1])
            y_a, v_used = rwkv7_time_mix(h, r, k, v, a_mu_rkv[e], a_mu_lora[e], a_w0[e], a_w1[e], a_w2[e],
                                         a_a0[e], a_a1[e], a_a2[e], a_g1[e], a_g2[e], a_k_k[e], a_k_a[e],
                                         a_r_k[e], a_ln_g[e], a_ln_b[e], vres)
            if e == 0:
                v_first = v_used
            y_b = dsa_sparse_attention(q_b.reshape(b, t, B_HEADS, HEAD_DIM), c_kv,
                                       q_idx.reshape(b, t, IDX_HEADS, IDX_DIM), k_idx, w_idx,
                                       b_kv_norm[e], b_w_kv_up[e], b_idx_k_norm[e])
            x = x + jnp.concatenate([y_a, y_b], axis=-1) @ ev_w_out[e]
        else:
            o = i // 2
            h = rmsnorm(x, od_norm[o])
            q, k, v = jnp.split((h @ od_w_qkv[o]).reshape(b, t, 3, C_HEADS, HEAD_DIM), 3, axis=2)
            y_c = stick_breaking_attention(q[:, :, 0], k[:, :, 0], v[:, :, 0])
            x = x + y_c @ od_w_out[o]
        x = x + hierarchical_moe(rmsnorm(x, moe_norm[i]), moe_router_group[i], moe_router_expert[i],
                                 moe_w1[i], moe_w3[i], moe_w2[i])
    return rmsnorm(x, final_norm)


_drawn_inputs = setup_inputs


def setup_inputs(seed=0):
    import zlib

    import numpy as np

    out = dict(_drawn_inputs(seed))
    spreads = {}
    factors = {'ev_norm': 3.03,
     'a_w1': 2.77,
     'a_w2': 3.161,
     'a_a0': 2.866,
     'a_k_k': 64.0,
     'a_k_a': 5.023,
     'a_ln_g': 41.613,
     'a_ln_b': 39.926,
     'b_kv_norm': 8.0,
     'b_idx_k_norm': 5.717,
     'od_norm': 4.868,
     'final_norm': 8.689,
     'moe_norm': 8.0}
    for name, (base, spread) in spreads.items():
        noise = np.random.default_rng([zlib.crc32(name.encode()), seed]).standard_normal(out[name].shape)
        drawn = base * np.exp(spread * noise) if base else spread * noise
        out[name] = jnp.asarray(drawn.astype(out[name].dtype))
    for name, factor in factors.items():
        out[name] = (out[name] * factor).astype(out[name].dtype)
    return out
```

```python
import math
from contextlib import ExitStack

import concourse.bass as bass
from concourse import mybir

F32 = mybir.dt.float32
I32 = mybir.dt.int32
U32 = mybir.dt.uint32
ALU = mybir.AluOpType
ACT = mybir.ActivationFunctionType
AX = mybir.AxisListType

P = 128
BANK = 512
D = 1024
T = 512
TT = T // P
KD = D // P
HD = 64
RMS_EPS = 1e-6
NEG = -1e30
TAKEN = -3e38

N_EXP = 32
N_GRP = 4
EPG = N_EXP // N_GRP
FF = 512
KF = FF // P
MB = 64
N_ASG = 2 * T
N_ROWS = N_ASG + MB


class Core:

    def __init__(self, nc, ctx):
        self.nc, self.ctx, self.made, self.of_stage = nc, ctx, 0, []

    def sb(self, name, shape, dt=F32, ctx=None):
        self.made += 1
        return (ctx or self.ctx).enter_context(self.nc.sbuf_tensor(f"{name}_{self.made}", shape, dt))

    def sem(self, name):
        self.made += 1
        s = self.nc.alloc_semaphore(name=f"{name}_{self.made}")
        self.of_stage.append(s)
        return s

    def end_stage(self):
        if self.of_stage:
            self.nc.clear_and_free_semaphores(self.of_stage)
            self.nc.all_engine_barrier()
        self.of_stage = []


def stage(f):
    def run(nc, c, *args):
        f(nc, c, *args)
        c.end_stage()
    return run


def chain(eng, sem):
    done = [0]

    def link(ins):
        done[0] += 1
        ins.then_inc(sem, 1)
        eng.wait_ge(sem, done[0])

    return link


@stage
def constants(nc, c):
    c.ident = c.sb("ident", [P, P])
    c.ones = c.sb("ones", [P, P])
    c.tri = c.sb("tri", [P, P])
    c.half = c.sb("half", [P, P], mybir.dt.bfloat16)
    c.headones = c.sb("headones", [P, P])
    c.count32 = c.sb("count32", [P, N_EXP])
    c.eps = c.sb("eps", [P, 4])
    made = c.sem("const_made")
    with nc.Block() as block:

        @block.gpsimd
        def _(pool):
            link = chain(pool, made)
            link(nc.gpsimd.memset(c.ones[:, :], 1.0))
            link(nc.gpsimd.memset(c.ident[:, :], 0.0))
            link(nc.gpsimd.affine_select(out=c.ident[:, :], in_=c.ident[:, :], compare_op=ALU.not_equal,
                                         fill=1.0, base=0, pattern=[[-1, P]], channel_multiplier=1))
            link(nc.gpsimd.affine_select(out=c.tri[:, :], in_=c.ones[:, :], compare_op=ALU.is_gt,
                                         fill=0.0, base=0, pattern=[[1, P]], channel_multiplier=-1))
            link(nc.gpsimd.memset(c.half[:, :], 0.0))
            link(nc.gpsimd.memset(c.headones[:, :], 0.0))
            link(nc.gpsimd.memset(c.headones[0:HD, 0:HD], 1.0))
            link(nc.gpsimd.memset(c.headones[HD:P, HD:P], 1.0))
            link(nc.gpsimd.memset(c.eps[:, :], 0.0))
            link(nc.gpsimd.memset(c.eps[:, 0:1], RMS_EPS))
            link(nc.gpsimd.memset(c.eps[:, 1:2], 64e-5))
            link(nc.gpsimd.iota(c.count32[:, :], [[1, N_EXP]], base=0, channel_multiplier=0,
                                allow_small_or_imprecise_dtypes=True))


def rms_scale(nc, c, x, xn, ss, rstd, sem_ss, sem_std, block):

    @block.scalar
    def _(act):
        for t in range(TT):
            nc.scalar.activation(xn[:, t, :], x[:, t, :], ACT.Square,
                                 accum_out=ss[:, t:t + 1]).then_inc(sem_ss, 1)
        act.wait_ge(sem_ss, TT)
        nc.scalar.activation(ss[:, TT:2 * TT], ss[:, 0:TT], ACT.Sqrt, scale=1.0 / D,
                             bias=c.eps[:, 0:1]).then_inc(sem_std, 1)


@stage
def norm_transpose(nc, c, ctx, ps, x, xn, hT, gain_dram):
    g = c.sb("gain", [P, KD], ctx=ctx)
    ss = c.sb("ss", [P, 2 * TT], ctx=ctx)
    rstd = c.sb("rstd", [P, TT], ctx=ctx)
    gain_in, ss_done, std_done, dve_own = c.sem("gain_in"), c.sem("ss_done"), c.sem("std_done"), c.sem("dve_own")
    xn_done, turned = c.sem("xn_done"), c.sem("turned")
    with nc.Block() as block:

        @block.sync
        def _(sp):
            sp.dma_start(g[:, :], gain_dram.rearrange("(p k) -> p k", k=KD)).then_inc(gain_in, 16)

        rms_scale(nc, c, x, xn, ss, rstd, ss_done, std_done, block)

        def evacuate(k, op):
            return op(hT[:, k, 1:T + 1], ps[k][:, :], g[:, k:k + 1])

        @block.vector
        def _(dve):
            link = chain(dve, dve_own)
            dve.wait_ge(std_done, 1)
            link(nc.vector.reciprocal(rstd[:, :], ss[:, TT:2 * TT]))
            link(nc.vector.memset(hT[:, :, 0:1], 0.0))
            for t in range(TT):
                nc.vector.tensor_scalar(xn[:, t, :], x[:, t, :], rstd[:, t:t + 1], None,
                                        ALU.mult).then_inc(xn_done, 1)
            dve.wait_ge(gain_in, 16)
            for k in range(0, KD, 2):
                dve.wait_ge(turned, k + 1)
                nc.vector.tensor_scalar(hT[:, k, 1:T + 1], ps[k][:, :], g[:, k:k + 1], None, ALU.mult)

        @block.tensor
        def _(pe):
            pe.wait_ge(xn_done, TT)
            for k in range(KD):
                for t in range(TT):
                    last = nc.tensor.transpose(ps[k][:, t * P:(t + 1) * P], xn[:, t, k::KD], c.ident[:, :])
                last.then_inc(turned, 1)

        @block.scalar
        def _(act):
            act.wait_ge(gain_in, 16)
            for k in range(1, KD, 2):
                act.wait_ge(turned, k + 1)
                nc.scalar.activation(hT[:, k, 1:T + 1], ps[k][:, :], ACT.Copy, scale=g[:, k:k + 1])


@stage
def router(nc, c, ctx, ps, hT, xn, w_group, w_expert, xrows, r):
    wr = c.sb("w_router", [P, KD, N_GRP + N_EXP], ctx=ctx)
    NL = N_GRP + N_EXP
    lgT = c.sb("logitsT", [NL, T], ctx=ctx)
    lg = c.sb("logits", [P, TT, NL], ctx=ctx)
    g8 = c.sb("group8", [P, TT, 8], ctx=ctx)
    e8 = c.sb("expert8", [P, TT, EPG], ctx=ctx)
    best = c.sb("best", [P, 2, TT, 8], ctx=ctx)
    besti = c.sb("best_index", [P, 2, TT, 8], U32, ctx=ctx)
    bestf = c.sb("best_index_f", [P, 2, TT, 8], ctx=ctx)
    prod = c.sb("prod", [P, TT, N_EXP], ctx=ctx)
    small = c.sb("small", [P, 12, TT], ctx=ctx)
    gex = c.sb("group_exp", [P, TT, N_GRP], ctx=ctx)
    hot = c.sb("hot", [P, 3, TT, N_EXP], ctx=ctx)
    pos = c.sb("pos", [P, TT, N_EXP], ctx=ctx)
    tab = c.sb("tab", [P, 8, N_EXP], ctx=ctx)
    zero = c.sb("zero_rows", [MB, D], ctx=ctx)
    w_in, cleared, scattered = c.sem("router_w_in"), c.sem("rows_cleared"), c.sem("rows_scattered")
    logitsT_done, logitsT_out, logits_done = c.sem("logitsT_done"), c.sem("logitsT_out"), c.sem("logits_done")
    own, sub_done, exp_done = c.sem("dve_own"), c.sem("sub_done"), c.sem("exp_done")
    hot_done, pos_done, dest_done, zeroed = c.sem("hot_done"), c.sem("pos_done"), c.sem("dest_done"), c.sem("zeroed")

    def col(t):
        return t[:, :, :]

    def wide(ap, n):
        return ap.rearrange("p (t o) -> p t o", o=1).to_broadcast([P, TT, n])

    with nc.Block() as block:

        @block.sync
        def _(sp):
            sp.dma_start(wr[:, :, 0:N_GRP], w_group.rearrange("(p k) n -> p k n", k=KD)).then_inc(w_in, 16)
            for g in range(N_GRP):
                lo = N_GRP + g * EPG
                sp.dma_start(wr[:, :, lo:lo + EPG],
                             w_expert[g].rearrange("(p k) n -> p k n", k=KD)).then_inc(w_in, 16)
            sp.wait_ge(zeroed, 1)
            sp.dma_start(xrows[N_ASG:N_ROWS, :], zero[:, :]).then_inc(cleared, 16)
            sp.wait_ge(cleared, 16)

        @block.tensor
        def _(pe):
            pe.wait_ge(w_in, 16 * (1 + N_GRP))
            for k in range(KD):
                last = nc.tensor.matmul(ps[0][0:NL, :], wr[:, k, :], hT[:, k, 1:T + 1],
                                        start=k == 0, stop=k == KD - 1)
            last.then_inc(logitsT_done, 1)
            pe.wait_ge(logitsT_out, 1)
            for t in range(TT):
                last = nc.tensor.transpose(ps[1][:, t * NL:(t + 1) * NL], lgT[:, t * P:(t + 1) * P],
                                           c.ident[0:NL, 0:NL])
            last.then_inc(logits_done, 1)
            pe.wait_ge(hot_done, 1)
            nc.tensor.matmul(ps[2][:, 0:P], c.tri[:, :], hot[:, 2, :, :].rearrange("p t e -> p (t e)"),
                             start=True, stop=True)
            nc.tensor.matmul(ps[3][:, 0:P], c.ones[:, :], hot[:, 2, :, :].rearrange("p t e -> p (t e)"),
                             start=True, stop=True).then_inc(pos_done, 1)

        @block.scalar
        def _(act):
            act.wait_ge(sub_done, 1)
            nc.scalar.activation(gex[:, :, :], gex[:, :, :], ACT.Exp).then_inc(exp_done, 1)
            act.wait_ge(sub_done, 2)
            nc.scalar.activation(small[:, 3, :], small[:, 2, :], ACT.Exp).then_inc(exp_done, 1)

        @block.vector
        def _(dve):
            link = chain(dve, own)
            V = nc.vector
            V.memset(zero[:, :], 0.0).then_inc(zeroed, 1)
            link(V.memset(g8[:, :, :], NEG))
            dve.wait_ge(logitsT_done, 1)
            V.tensor_copy(lgT[:, :], ps[0][0:NL, :]).then_inc(logitsT_out, 1)
            dve.wait_ge(logits_done, 1)
            link(V.tensor_copy(lg[:, :, :], ps[1][:, 0:TT * NL].rearrange("p (t n) -> p t n", n=NL)))
            link(V.tensor_copy(g8[:, :, 0:N_GRP], lg[:, :, 0:N_GRP]))
            for t in range(TT):
                link(V.max(best[:, 0, t, :], g8[:, t, :]))
                link(V.max_index(besti[:, 0, t, :], best[:, 0, t, :], g8[:, t, :]))
            link(V.tensor_copy(bestf[:, 0, :, :], besti[:, 0, :, :]))
            V.tensor_tensor(gex[:, :, :], lg[:, :, 0:N_GRP], best[:, 0, :, 0:1].to_broadcast([P, TT, N_GRP]),
                            ALU.subtract).then_inc(sub_done, 1)
            link(V.tensor_tensor(pos[:, :, 0:N_GRP], c.count32[:, 0:N_GRP].rearrange("p (o g) -> p o g", o=1)
                                 .to_broadcast([P, TT, N_GRP]),
                                 bestf[:, 0, :, 0:1].to_broadcast([P, TT, N_GRP]), ALU.is_equal))
            for t in range(TT):
                link(V.tensor_tensor(prod[:, t, :].rearrange("p (g e) -> p g e", e=EPG),
                                     lg[:, t, N_GRP:NL].rearrange("p (g e) -> p g e", e=EPG),
                                     pos[:, t, 0:N_GRP].rearrange("p (g o) -> p g o", o=1)
                                     .to_broadcast([P, N_GRP, EPG]), ALU.mult))
                link(V.tensor_reduce(e8[:, t, :], prod[:, t, :].rearrange("p (g e) -> p e g", e=EPG), AX.X, ALU.add))
                link(V.max(best[:, 1, t, :], e8[:, t, :]))
                link(V.max_index(besti[:, 1, t, :], best[:, 1, t, :], e8[:, t, :]))
            link(V.tensor_copy(bestf[:, 1, :, :], besti[:, 1, :, :]))
            V.tensor_tensor(small[:, 2, :], best[:, 1, :, 1], best[:, 1, :, 0], ALU.subtract).then_inc(sub_done, 1)
            for j in range(2):
                link(V.scalar_tensor_tensor(out=small[:, 4 + j, :], in0=bestf[:, 0, :, 0], scalar=float(EPG),
                                            in1=bestf[:, 1, :, j], op0=ALU.mult, op1=ALU.add))
                link(V.tensor_tensor(hot[:, j, :, :], c.count32[:, :].rearrange("p (o e) -> p o e", o=1)
                                     .to_broadcast([P, TT, N_EXP]), wide(small[:, 4 + j, :], N_EXP), ALU.is_equal))
            V.tensor_tensor(hot[:, 2, :, :], hot[:, 0, :, :], hot[:, 1, :, :], ALU.add).then_inc(hot_done, 1)
            dve.wait_ge(exp_done, 2)
            link(V.tensor_reduce(small[:, 6, :], gex[:, :, :], AX.X, ALU.add))
            link(V.tensor_scalar(small[:, 7, :], small[:, 3, :], 1.0, None, ALU.add))
            link(V.tensor_tensor(small[:, 8, :], small[:, 6, :], small[:, 7, :], ALU.mult))
            link(V.reciprocal(r.gate[:, 0, :], small[:, 8, :]))
            link(V.tensor_tensor(r.gate[:, 1, :], r.gate[:, 0, :], small[:, 3, :], ALU.mult))
            dve.wait_ge(pos_done, 1)
            total = ps[3][:, 0:P].rearrange("p (t e) -> p t e", e=N_EXP)
            link(V.memset(tab[:, 0, :], 0.0))
            for t in range(TT):
                link(V.tensor_tensor(tab[:, t + 1, :], total[:, t, :], tab[:, t, :], ALU.add))
            link(V.tensor_tensor_scan(tab[:, 5, :], c.ones[:, 0:N_EXP], tab[:, TT, :], 0.0, ALU.mult, ALU.add))
            link(V.tensor_tensor(tab[:, 6, :], tab[:, 5, :], tab[:, TT, :], ALU.subtract))
            link(V.tensor_tensor(pos[:, :, :], ps[2][:, 0:P].rearrange("p (t e) -> p t e", e=N_EXP),
                                 tab[:, 0:TT, :], ALU.add))
            link(V.tensor_tensor(pos[:, :, :], pos[:, :, :], tab[:, 6:7, :].to_broadcast([P, TT, N_EXP]), ALU.add))
            for j in range(2):
                link(V.tensor_tensor(prod[:, :, :], pos[:, :, :], hot[:, j, :, :], ALU.mult))
                link(V.tensor_reduce(small[:, 9, :], prod[:, :, :], AX.X, ALU.add))
                link(V.tensor_copy(r.dest[:, j, :], small[:, 9, :]))
            link(V.memset(tab[:, 7, :], 0.0))
            for b in range(1, T // MB):
                link(V.tensor_scalar(tab[:, 3, :], tab[:, TT, :], float(b * MB), None, ALU.is_gt))
                link(V.tensor_tensor(tab[:, 7, :], tab[:, 7, :], tab[:, 3, :], ALU.add))
            link(V.tensor_tensor_scan(tab[:, 0, :], c.ones[:, 0:N_EXP], tab[:, 7, :], 0.0, ALU.mult, ALU.add))
            link(V.tensor_tensor(tab[:, 1, :], tab[:, 0, :], tab[:, 7, :], ALU.subtract))
            link(V.tensor_copy(r.start[:, :], tab[0:1, 6, :]))
            link(V.tensor_copy(r.end[:, :], tab[0:1, 5, :]))
            link(V.tensor_copy(r.extra_before[:, :], tab[0:1, 1, :]))
            link(V.tensor_copy(r.extra_total[:, :], tab[0:1, 0, N_EXP - 1:N_EXP]))
            V.tensor_scalar(r.blocks[:, :], tab[0:1, 7, :], 1.0, None, ALU.add).then_inc(dest_done, 1)

        @block.gpsimd
        def _(pool):
            pool.wait_ge(dest_done, 1)
            for j in range(2):
                for t in range(TT):
                    nc.gpsimd.indirect_dma_start(
                        out=xrows[0:N_ASG, :], out_offset=bass.IndirectOffsetOnAxis(ap=r.dest[:, j, t:t + 1], axis=0),
                        in_=xn[:, t, :], in_offset=None).then_inc(scattered, 16)
            pool.wait_ge(scattered, 16 * 2 * TT)


@stage
def experts(nc, c, ctx, ps, xrows, yrows, r, gain_dram, w1, w3, w2):
    x_rows = [c.sb(f"x_rows{j}", [MB, D], ctx=ctx) for j in range(2)]
    w1_sb = [c.sb(f"w1_{j}", [P, KD, FF], ctx=ctx) for j in range(2)]
    w3_sb = [c.sb(f"w3_{j}", [P, KD, FF], ctx=ctx) for j in range(2)]
    w2_sb = [c.sb(f"w2_{j}", [P, KF, D], ctx=ctx) for j in range(2)]
    y_sb = [c.sb(f"y_{j}", [P, FF], ctx=ctx) for j in range(2)]
    xT = c.sb("xT", [P, KD, MB], ctx=ctx)
    gate_act = c.sb("gate_act", [MB, FF], ctx=ctx)
    hid = c.sb("hid", [MB, FF], ctx=ctx)
    hidT = c.sb("hidT", [P, KF, MB], ctx=ctx)
    g = c.sb("gain", [P, KD], ctx=ctx)
    ps_x, ps_1, ps_3, ps_h, ps_y0, ps_y1 = ps[0], ps[1], ps[2], ps[3], ps[4], ps[5]

    gain_in = c.sem("gain_in")
    rows_in = [c.sem(f"rows_in{j}") for j in range(2)]
    up_in = [c.sem(f"up_in{j}") for j in range(2)]
    down_in = [c.sem(f"down_in{j}") for j in range(2)]
    stored = [c.sem(f"stored{j}") for j in range(2)]
    xT_done, xT_out = c.sem("xT_done"), c.sem("xT_out")
    up_done, silu_done, hid_done = c.sem("up_done"), c.sem("silu_done"), c.sem("hid_done")
    hidT_done, hidT_out = c.sem("hidT_done"), c.sem("hidT_out")
    down_done, y0_out, y1_out = c.sem("down_done"), c.sem("y0_out"), c.sem("y1_out")

    def expert(w, e, k):
        return w[bass.ds(e, 1)].rearrange("o (p k) n -> p (o k) n", k=k)

    def load(sp, j, n, e, row, first=False):
        if not first:
            sp.wait_ge(xT_done, n - 1)
        sp.dma_start(x_rows[j][:, :], xrows[bass.ds(row, MB), :]).then_inc(rows_in[j], 16)
        if not first:
            sp.wait_ge(up_done, n - 1)
        sp.dma_start(w1_sb[j][:, :, :], expert(w1, e, KD)).then_inc(up_in[j], 16)
        sp.dma_start(w3_sb[j][:, :, :], expert(w3, e, KD)).then_inc(up_in[j], 16)
        if not first:
            sp.wait_ge(down_done, n - 1)
        sp.dma_start(w2_sb[j][:, :, :], expert(w2, e, KF)).then_inc(down_in[j], 16)

    def pe_step(pe, j, n, u):
        pe.wait_ge(rows_in[j], 16 * u + 16)
        nc.tensor.ldweights(c.half[:, :], tile_position=(0, 0))
        for k in range(KD):
            last = nc.tensor.transpose(ps_x[:, k * MB:(k + 1) * MB], x_rows[j][:, k::KD], c.ident[0:MB, 0:MB])
        last.then_inc(xT_done, 1)
        pe.wait_ge(xT_out, n + 1)
        pe.wait_ge(up_in[j], 32 * u + 32)
        for k in range(KD):
            nc.tensor.matmul(ps_1[0:MB, :], xT[:, k, :], w1_sb[j][:, k, :], start=k == 0, stop=k == KD - 1)
            last = nc.tensor.matmul(ps_3[MB:P, :], xT[:, k, :], w3_sb[j][:, k, :], start=k == 0, stop=k == KD - 1)
        last.then_inc(up_done, 1)
        pe.wait_ge(hid_done, n + 1)
        nc.tensor.ldweights(c.half[:, :], tile_position=(0, 0))
        for k in range(KF):
            last = nc.tensor.transpose(ps_h[:, k * MB:(k + 1) * MB], hid[:, k::KF], c.ident[0:MB, 0:MB])
        last.then_inc(hidT_done, 1)
        pe.wait_ge(hidT_out, n + 1)
        pe.wait_ge(down_in[j], 16 * u + 16)
        pe.wait_ge(y0_out, n + 1)
        pe.wait_ge(y1_out, n + 1)
        for k in range(KF):
            nc.tensor.matmul(ps_y0[0:MB, :], hidT[:, k, :], w2_sb[j][:, k, 0:FF], start=k == 0, stop=k == KF - 1)
            last = nc.tensor.matmul(ps_y1[MB:P, :], hidT[:, k, :], w2_sb[j][:, k, FF:D], start=k == 0, stop=k == KF - 1)
        last.then_inc(down_done, 1)

    def dve_step(dve, j, n, u):
        dve.wait_ge(xT_done, n + 1)
        nc.vector.tensor_tensor(xT[:, :, :], ps_x[:, :].rearrange("p (k m) -> p k m", m=MB),
                                g[:, :].rearrange("p (k o) -> p k o", o=1).to_broadcast([P, KD, MB]),
                                ALU.mult).then_inc(xT_out, 1)
        dve.wait_ge(silu_done, n + 1)
        nc.vector.tensor_tensor(hid[:, :], gate_act[:, :], ps_3[MB:P, :], ALU.mult).then_inc(hid_done, 1)
        dve.wait_ge(down_done, n + 1)
        dve.wait_ge(stored[j], 32 * u + 32)
        nc.vector.tensor_copy(y_sb[j][MB:P, :], ps_y1[MB:P, :]).then_inc(y1_out, 1)

    def act_step(act, j, n, u, row, before):
        act.wait_ge(up_done, n + 1)
        nc.scalar.activation(gate_act[:, :], ps_1[0:MB, :], ACT.Silu).then_inc(silu_done, 1)
        act.wait_ge(hidT_done, n + 1)
        nc.scalar.activation(hidT[:, :, :], ps_h[:, 0:KF * MB].rearrange("p (k m) -> p k m", m=MB),
                             ACT.Copy).then_inc(hidT_out, 1)
        act.wait_ge(down_done, n + 1)
        act.wait_ge(stored[j], 32 * u + 32)
        nc.scalar.activation(y_sb[j][0:MB, :], ps_y0[0:MB, :], ACT.Copy).then_inc(y0_out, 1)
        act.wait_ge(y0_out, n + 2)
        act.wait_ge(y1_out, n + 2)
        before(act)
        for h in range(2):
            act.dma_start(yrows[bass.ds(row, MB), h * FF:(h + 1) * FF],
                          y_sb[j][h * MB:(h + 1) * MB, :]).then_inc(stored[j], 16)

    N_MAIN = N_EXP
    U_MAIN = N_EXP // 2

    def further(eng, step):
        more = eng.value_load(r.extra_total[0:1, 0:1], min_val=0, max_val=N_ASG // MB)
        with eng.If(more > 0):
            with eng.Fori(0, N_EXP) as e:
                blocks = eng.value_load(r.blocks[0:1, bass.ds(e, 1)], min_val=1, max_val=T // MB)
                done = eng.value_load(r.extra_before[0:1, bass.ds(e, 1)], min_val=0, max_val=N_ASG // MB)
                with eng.If(blocks > 1):
                    end = eng.value_load(r.end[0:1, bass.ds(e, 1)], min_val=MB, max_val=N_ASG)
                    with eng.Fori(1, blocks) as b:
                        step(e, eng.snap(done + b - 1), nc.s_assert_within(eng.snap(end - b * MB), 0, N_ASG - MB, skip_runtime_bounds_check_because="further blocks lie inside the expert's rows"))
                eng.nop()
            eng.nop()
        eng.nop()

    with nc.Block() as block:

        @block.sync
        def _(sp):
            sp.dma_start(g[:, :], gain_dram.rearrange("(p k) -> p k", k=KD)).then_inc(gain_in, 16)
            for j in range(2):
                row = sp.value_load(r.start[0:1, j:j + 1], min_val=0, max_val=N_ASG)
                load(sp, j, j, j, row, first=True)
            with sp.Fori(1, U_MAIN) as i:
                for j in range(2):
                    row = sp.value_load(r.start[0:1, bass.ds(2 * i + j, 1)], min_val=0, max_val=N_ASG)
                    load(sp, j, 2 * i + j, 2 * i + j, row)

            def more(e, m, row):
                sp.wait_ge(down_done, m + N_MAIN)
                load(sp, 0, m + N_MAIN, e, row, first=True)

            further(sp, more)

        @block.tensor
        def _(pe):
            pe.wait_ge(gain_in, 16)
            with pe.Fori(0, U_MAIN) as i:
                for j in range(2):
                    pe_step(pe, j, 2 * i + j, i)
            further(pe, lambda e, m, row: pe_step(pe, 0, m + N_MAIN, m + U_MAIN))

        @block.vector
        def _(dve):
            dve.wait_ge(gain_in, 16)
            dve.sem_inc(y1_out, 1)
            with dve.Fori(0, U_MAIN) as i:
                for j in range(2):
                    dve_step(dve, j, 2 * i + j, i)
            further(dve, lambda e, m, row: dve_step(dve, 0, m + N_MAIN, m + U_MAIN))

        @block.scalar
        def _(act):
            act.sem_inc(y0_out, 1)
            act.sem_inc(stored[0], 32)
            act.sem_inc(stored[1], 32)
            with act.Fori(0, U_MAIN) as i:
                for j in range(2):
                    row = act.value_load(r.start[0:1, bass.ds(2 * i + j, 1)], min_val=0, max_val=N_ASG)
                    act_step(act, j, 2 * i + j, i, row,
                             lambda a: a.wait_ge(stored[1 - j], 32 * i + 32 + 32 * j))

            def more(e, m, row):
                act_step(act, 0, m + N_MAIN, m + U_MAIN, row, lambda a: a.wait_ge(stored[1], 32 * U_MAIN + 32))
                act.wait_ge(stored[0], 32 * m + 32 * U_MAIN + 64)

            further(act, more)
            act.wait_ge(stored[0], 32 * U_MAIN + 32)
            act.wait_ge(stored[1], 32 * U_MAIN + 32)


@stage
def combine(nc, c, ctx, x, yrows, r):
    got = c.sb("got", [P, 2, TT, D], ctx=ctx)
    gathered = [[c.sem(f"gathered{j}{t}") for t in range(TT)] for j in range(2)]
    own = c.sem("dve_own")
    with nc.Block() as block:

        @block.gpsimd
        def _(pool):
            for t in range(TT):
                for j in range(2):
                    nc.gpsimd.indirect_dma_start(
                        out=got[:, j, t, :], out_offset=None, in_=yrows[0:N_ASG, :],
                        in_offset=bass.IndirectOffsetOnAxis(ap=r.dest[:, j, t:t + 1], axis=0)
                    ).then_inc(gathered[j][t], 16)

        @block.vector
        def _(dve):
            link = chain(dve, own)
            for t in range(TT):
                for j in range(2):
                    dve.wait_ge(gathered[j][t], 16)
                    link(nc.vector.scalar_tensor_tensor(out=x[:, t, :], in0=got[:, j, t, :],
                                                        scalar=r.gate[:, j, t:t + 1], in1=x[:, t, :],
                                                        op0=ALU.mult, op1=ALU.add))


class Routes:

    def __init__(self, c, ctx):
        self.gate = c.sb("gate", [P, 2, TT], ctx=ctx)
        self.dest = c.sb("dest", [P, 2, TT], U32, ctx=ctx)
        self.start = c.sb("start", [1, N_EXP], I32, ctx=ctx)
        self.end = c.sb("end", [1, N_EXP], I32, ctx=ctx)
        self.blocks = c.sb("blocks", [1, N_EXP], I32, ctx=ctx)
        self.extra_before = c.sb("extra_before", [1, N_EXP], I32, ctx=ctx)
        self.extra_total = c.sb("extra_total", [1, 1], I32, ctx=ctx)


def moe(nc, c, ps, x, xrows, yrows, gain, w_group, w_expert, w1, w3, w2):
    with ExitStack() as outer:
        r = Routes(c, outer)
        with ExitStack() as ctx:
            xn = c.sb("xn", [P, TT, D], ctx=ctx)
            hT = c.sb("hT", [P, KD, T + 1], ctx=ctx)
            norm_transpose(nc, c, ctx, ps, x, xn, hT, gain)
            router(nc, c, ctx, ps, hT, xn, w_group, w_expert, xrows, r)
        with ExitStack() as ctx:
            experts(nc, c, ctx, ps, xrows, yrows, r, gain, w1, w3, w2)
        with ExitStack() as ctx:
            combine(nc, c, ctx, x, yrows, r)


class Bank:

    def __init__(self, ps, filled, emptied):
        self.ps, self.filled, self.emptied, self.n = ps, filled, emptied, 0

    def open(self, pe):
        if self.n:
            pe.wait_ge(self.emptied, self.n)
        return self.ps

    def close(self, last):
        last.then_inc(self.filled, 1)
        self.n += 1

    def copied(self, pe):
        pe.wait_ge(self.emptied, self.n)

    def read(self, eng):
        self.n += 1
        eng.wait_ge(self.filled, self.n)
        return self.ps

    def empty(self, ins):
        ins.then_inc(self.emptied, 1)


def bank_sems(c, what):
    return [(c.sem(f"{what}_filled{b}"), c.sem(f"{what}_emptied{b}")) for b in range(8)]


def bank_set(ps, sems):
    return [Bank(ps[b], *sems[b]) for b in range(8)]


@stage
def out_project(nc, c, ctx, ps, x, yT, w_dram):
    w = c.sb("w_out", [P, KD, D], ctx=ctx)
    w_in = [c.sem(f"w_out_in{f}") for f in range(2)]
    done = c.sem("out_done")
    with nc.Block() as block:

        @block.sync
        def _(sp):
            for h in range(2):
                sp.dma_start(w[:, :, h * BANK:(h + 1) * BANK],
                             w_dram.rearrange("(f p) n -> p f n", p=P)[:, :, h * BANK:(h + 1) * BANK]
                             ).then_inc(w_in[h], 16)

        @block.tensor
        def _(pe):
            for h in range(2):
                pe.wait_ge(w_in[h], 16)
                for t in range(TT):
                    for f in range(KD):
                        last = nc.tensor.matmul(ps[h * TT + t][:, :], yT[:, f, t * P:(t + 1) * P],
                                                w[:, f, h * BANK:(h + 1) * BANK], start=f == 0, stop=f == KD - 1)
                    last.then_inc(done, 1)

        @block.vector
        def _(dve):
            for h in range(2):
                for t in range(TT):
                    dve.wait_ge(done, h * TT + t + 1)
                    xs = x[:, t, h * BANK:(h + 1) * BANK]
                    nc.vector.tensor_tensor(xs, ps[h * TT + t][:, :], xs, ALU.add)


C_HEADS = 16
LAG_T, LAG_PV = 3, 4


@stage
def odd_project(nc, c, ctx, ps, hT, w_dram, qT, kT, v):
    NG, SLOTS = 6, 3
    w = [c.sb(f"w_qkv{s}", [P, KD, BANK], ctx=ctx) for s in range(SLOTS)]
    w_in = [c.sem(f"w_qkv_in{s}") for s in range(SLOTS)]
    used = c.sem("w_qkv_used")
    sems = bank_sems(c, "qkv")

    def dest(g, s):
        if g < 2:
            return qT[:, 4 * g + s, :]
        if g < 4:
            return kT[:, 4 * (g - 2) + s, :]
        return v[:, s, (g - 4) * BANK:(g - 3) * BANK]

    with nc.Block() as block:

        @block.sync
        def _(sp):
            for g in range(NG):
                if g >= SLOTS:
                    sp.wait_ge(used, g - SLOTS + 1)
                sp.dma_start(w[g % SLOTS][:, :, :],
                             w_dram.rearrange("(p k) n -> p k n", k=KD)[:, :, g * BANK:(g + 1) * BANK]
                             ).then_inc(w_in[g % SLOTS], 16)

        @block.tensor
        def _(pe):
            banks = bank_set(ps, sems)
            for g in range(NG):
                pe.wait_ge(w_in[g % SLOTS], 16 * (g // SLOTS + 1))
                for s in range(4):
                    b = banks[(4 * g + s) % 8]
                    out = b.open(pe)
                    for k in range(KD):
                        wk = w[g % SLOTS][:, k, :]
                        if g < 4:
                            last = nc.tensor.matmul(out[:, :], wk[:, s * P:(s + 1) * P], hT[:, k, 1:T + 1],
                                                    start=k == 0, stop=k == KD - 1)
                        else:
                            last = nc.tensor.matmul(out[:, :], hT[:, k, 1 + s * P:1 + (s + 1) * P], wk,
                                                    start=k == 0, stop=k == KD - 1)
                    b.close(last)
                pe.wait_ge(b.filled, b.n)
                pe.sem_inc(used, 1)

        @block.vector
        def _(dve):
            banks = bank_set(ps, sems)
            for g in range(NG):
                for s in range(0, 4, 2):
                    b = banks[(4 * g + s) % 8]
                    b.empty(nc.vector.tensor_scalar(dest(g, s), b.read(dve)[:, :],
                                                    HD ** -0.5 if g < 2 else 1.0, None, ALU.mult))

        @block.scalar
        def _(act):
            banks = bank_set(ps, sems)
            for g in range(NG):
                for s in range(1, 4, 2):
                    b = banks[(4 * g + s) % 8]
                    b.empty(nc.scalar.activation(dest(g, s), b.read(act)[:, :], ACT.Copy,
                                                 scale=HD ** -0.5 if g < 2 else 1.0))


@stage
def stick_breaking(nc, c, ctx, ps, qT, kT, v, yT):
    units = [(h, t) for h in range(C_HEADS) for t in range(TT)]
    N = len(units)
    keep = [c.sb(f"keep{i}", [P, T], ctx=ctx) for i in range(4)]
    beta = [c.sb(f"beta{i}", [P, T], ctx=ctx) for i in range(4)]
    tail = [c.sb(f"tail{t}", [P, T + 1], ctx=ctx) for t in range(TT)]
    wT = [c.sb(f"wT{i}", [P, T], ctx=ctx) for i in range(2)]
    zero = c.sb("zero", [P, T], ctx=ctx)
    z_done, beta_done, masked = c.sem("z_done"), c.sem("beta_done"), c.sem("masked")
    scanned, weighted = c.sem("scanned"), c.sem("weighted")
    turned, wT_out, pv_done, y_out, ready = (c.sem("turned"), c.sem("wT_out"), c.sem("pv_done"),
                                             c.sem("y_out"), c.sem("stick_ready"))
    ps_z, ps_t, ps_y = ps[0:3], ps[3:5], ps[5:7]

    with nc.Block() as block:

        @block.tensor
        def _(pe):
            def scores(u):
                h, t = units[u]
                q = HD * (h % 2)
                if u >= 3:
                    pe.wait_ge(beta_done, 2 * (u - 3) + 2)
                nc.tensor.matmul(ps_z[u % 3][:, 0:(t + 1) * P], qT[q:q + HD, h // 2, t * P:(t + 1) * P],
                                 kT[q:q + HD, h // 2, 0:(t + 1) * P], start=True, stop=True).then_inc(z_done, 1)

            def turn(u):
                h, t = units[u]
                pe.wait_ge(weighted, u + 1)
                if u >= 2:
                    pe.wait_ge(wT_out, u - 1)
                for b in range(t + 1):
                    last = nc.tensor.transpose(ps_t[u % 2][:, b * P:(b + 1) * P], beta[u % 4][:, b * P:(b + 1) * P],
                                               c.ident[:, :])
                last.then_inc(turned, 1)

            def weigh(u):
                h, t = units[u]
                q = HD * (h % 2)
                pair = h // 2
                pe.wait_ge(wT_out, u + 1)
                if h % 2 == 0 and t == 0 and pair >= 2:
                    pe.wait_ge(y_out, pair - 1)
                for b in range(t + 1):
                    last = nc.tensor.matmul(ps_y[pair % 2][q:q + HD, t * P:(t + 1) * P],
                                            v[:, b, h * HD:(h + 1) * HD], wT[u % 2][:, b * P:(b + 1) * P],
                                            start=b == 0, stop=b == t)
                last.then_inc(pv_done, 1)

            for i in range(N + LAG_PV):
                if i < N:
                    scores(i)
                if 0 <= i - LAG_T < N:
                    turn(i - LAG_T)
                if 0 <= i - LAG_PV < N:
                    weigh(i - LAG_PV)

        @block.scalar
        def _(act):
            for i in range(N + LAG_T):
                if i < N:
                    h, t = units[i]
                    L = (t + 1) * P
                    act.wait_ge(z_done, i + 1)
                    if i >= 4:
                        act.wait_ge(scanned, i - 3)
                        act.wait_ge(turned, i - 3)
                    nc.scalar.activation(keep[i % 4][:, 0:L], ps_z[i % 3][:, 0:L], ACT.Sigmoid,
                                         scale=-1.0).then_inc(beta_done, 1)
                    nc.scalar.activation(beta[i % 4][:, 0:L], ps_z[i % 3][:, 0:L],
                                         ACT.Sigmoid).then_inc(beta_done, 1)
                u = i - LAG_T
                if u >= 0:
                    L = (units[u][1] + 1) * P
                    act.wait_ge(turned, u + 1)
                    if u >= 2:
                        act.wait_ge(pv_done, u - 1)
                    nc.scalar.activation(wT[u % 2][:, 0:L], ps_t[u % 2][:, 0:L], ACT.Copy).then_inc(wT_out, 1)

        @block.gpsimd
        def _(pool):
            for i, (h, t) in enumerate(units):
                pool.wait_ge(beta_done, 2 * i + 2)
                lo, hi = t * P, (t + 1) * P
                for buf, fill in ((keep, 1.0), (beta, 0.0)):
                    last = nc.gpsimd.affine_select(out=buf[i % 4][:, lo:hi], in_=buf[i % 4][:, lo:hi],
                                                   compare_op=ALU.is_gt, fill=fill, base=0, pattern=[[-1, P]],
                                                   channel_multiplier=1)
                last.then_inc(masked, 1)

        @block.vector
        def _(dve):
            nc.vector.memset(zero[:, :], 0.0).then_inc(ready, 1)
            for t in range(TT):
                L = (t + 1) * P
                nc.vector.memset(tail[t][:, L:L + 1], 1.0).then_inc(ready, 1)
            dve.wait_ge(ready, 1 + TT)
            for i, (h, t) in enumerate(units):
                L = (t + 1) * P
                dve.wait_ge(masked, i + 1)
                if i >= 4:
                    dve.wait_ge(weighted, i - 3)
                nc.vector.tensor_tensor_scan(tail[t][:, L - 1::-1] if L == T + 1 else tail[t][:, 0:L][:, ::-1],
                                             keep[i % 4][:, 0:L][:, ::-1], zero[:, 0:L], 1.0,
                                             ALU.mult, ALU.add).then_inc(scanned, 1)
                dve.wait_ge(scanned, i + 1)
                nc.vector.tensor_tensor(beta[i % 4][:, 0:L], beta[i % 4][:, 0:L], tail[t][:, 1:L + 1],
                                        ALU.mult).then_inc(weighted, 1)
                if h % 2 == 1 and t == 1 and h >= 3:
                    pair = h // 2 - 1
                    dve.wait_ge(pv_done, 8 * (pair + 1))
                    nc.vector.tensor_copy(yT[:, pair, :], ps_y[pair % 2][:, :]).then_inc(y_out, 1)
            pair = C_HEADS // 2 - 1
            dve.wait_ge(pv_done, N)
            nc.vector.tensor_copy(yT[:, pair, :], ps_y[pair % 2][:, :]).then_inc(y_out, 1)


def odd_mixer(nc, c, ps, x, gain, w_qkv, w_out):
    with ExitStack() as ctx:
        yT = c.sb("yT", [P, KD, T], ctx=ctx)
        with ExitStack() as inner:
            qT = c.sb("qT", [P, KD, T], ctx=inner)
            kT = c.sb("kT", [P, KD, T], ctx=inner)
            v = c.sb("v", [P, TT, D], ctx=inner)
            with ExitStack() as proj:
                xn = c.sb("xn", [P, TT, D], ctx=proj)
                hT = c.sb("hT", [P, KD, T + 1], ctx=proj)
                norm_transpose(nc, c, proj, ps, x, xn, hT, gain)
                odd_project(nc, c, proj, ps, hT, w_qkv, qT, kT, v)
            stick_breaking(nc, c, inner, ps, qT, kT, v, yT)
        out_project(nc, c, ctx, ps, x, yT, w_out)


A_HEADS, A_WIDTH = 8, 512
B_HEADS, B_WIDTH = 8, 512
KV_RANK = 128
IDX_HEADS = 8
TOPK = min(256, T // 4)
FT = A_WIDTH // P
CH = 64
NCH = T // CH
DECAY = math.exp(-0.5)
COLS = dict(r=0, k=512, v=1024, qb=1536, ckv=2048, qi=2176, ki=2688, wi=2752)


@stage
def even_project(nc, c, ctx, ps, hT, w_dram, m, prm):
    SLOTS = 3
    w = [c.sb(f"w_in{s}", [P, KD, BANK], ctx=ctx) for s in range(SLOTS)]
    wda = c.sb("w_da", [P, 2, KD, P], ctx=ctx)
    wg = c.sb("w_g", [P, 2, KD, P], ctx=ctx)
    mu = c.sb("mu_lora", [P, 3, KD], ctx=ctx)
    less = c.sb("one_less_mu", [P, 3, FT], ctx=ctx)
    raw = [c.sb(f"raw{i}", [P, T + 1], ctx=ctx) for i in range(2)]
    w_in = [c.sem(f"w_in{s}") for s in range(SLOTS)]
    used, own, prm_in, lora_w = c.sem("w_used"), c.sem("dve_own"), c.sem("prm_in"), c.sem("lora_w_ready")
    raw_out, raw_read, raw_zero = c.sem("raw_out"), c.sem("raw_read"), c.sem("raw_zero")
    sems = bank_sems(c, "proj")
    groups = ["r", "k", "v", "qb", "qi", "misc"]
    wv = w_dram.rearrange("(p k) n -> p k n", k=KD)
    with nc.Block() as block:

        @block.sync
        def _(sp):
            def group(g):
                s, name = g % SLOTS, groups[g]
                if name != "misc":
                    sp.dma_start(w[s][:, :, :], wv[:, :, COLS[name]:COLS[name] + BANK]).then_inc(w_in[s], 16)
                    return
                for lo, col, n in ((0, COLS["ckv"], KV_RANK), (P, COLS["ki"], HD), (P + HD, COLS["ki"], HD),
                                   (2 * P, COLS["wi"], IDX_HEADS)):
                    sp.dma_start(w[s][:, :, lo:lo + n], wv[:, :, col:col + n]).then_inc(w_in[s], 16)

            group(0)
            sp.dma_start(mu[:, :, :], prm["mu_lora"].rearrange("m (p k) -> p m k", k=KD)).then_inc(prm_in, 16)
            for i in range(3):
                sp.dma_start(m.mu[:, i, :], prm["mu_rkv"][i].rearrange("(f p) -> p f", p=P),
                             allow_slow_non_contiguous=True).then_inc(prm_in, 16)
            sp.dma_start(wda[:, 0, :, 0:HD], prm["w1"].rearrange("(p k) n -> p k n", k=KD)).then_inc(prm_in, 16)
            sp.dma_start(wda[:, 0, :, HD:P], prm["a1"].rearrange("(p k) n -> p k n", k=KD)).then_inc(prm_in, 16)
            sp.dma_start(wg[:, 0, :, :], prm["g1"].rearrange("(p k) n -> p k n", k=KD)).then_inc(prm_in, 16)
            for g in range(1, len(groups)):
                if g >= SLOTS:
                    sp.wait_ge(used, g - SLOTS + 1)
                group(g)

        @block.tensor
        def _(pe):
            banks = bank_set(ps, sems)
            jobs = [0]

            def project(lhsT, rhs, rows=P, steps=1):
                b = banks[jobs[0] % 8]
                jobs[0] += 1
                out = b.open(pe)
                for s in range(steps):
                    for k in range(KD):
                        last = nc.tensor.matmul(out[0:rows, :], lhsT(s, k), rhs(s, k),
                                                start=s == 0 and k == 0, stop=s == steps - 1 and k == KD - 1)
                b.close(last)
                return b

            for g, name in enumerate(groups):
                s = g % SLOTS
                pe.wait_ge(w_in[s], 16 * (g // SLOTS + (1 if name != "misc" else 4)))
                for f in range(FT if name != "misc" else 2):
                    b = project(lambda _, k: w[s][:, k, f * P:(f + 1) * P], lambda _, k: hT[:, k, 1:T + 1])
                if name == "misc":
                    b = project(lambda _, k: w[s][:, k, 2 * P:2 * P + IDX_HEADS], lambda _, k: hT[:, k, 1:T + 1],
                                rows=IDX_HEADS)
                pe.wait_ge(b.filled, b.n)
                pe.sem_inc(used, 1)
            pe.wait_ge(lora_w, 1)
            for wl in (wda, wg):
                project(lambda s, k: wl[:, s, k, :], lambda s, k: hT[:, k, 1 - s:T + 1 - s], steps=2)

        @block.scalar
        def _(act):
            banks = bank_set(ps, sems)
            act.wait_ge(raw_zero, 1)
            jobs = [0]

            def take():
                b = banks[jobs[0] % 8]
                jobs[0] += 1
                return b, b.read(act)

            for n in range(3 * FT):
                b, out = take()
                if n >= 2:
                    act.wait_ge(raw_read, n - 1)
                ins = nc.scalar.activation(raw[n % 2][:, 1:T + 1], out[:, :], ACT.Copy)
                b.empty(ins)
                act.wait_ge(b.emptied, b.n)
                act.sem_inc(raw_out, 1)
            for dest, scale in ((m.qb, HD ** -0.5), (m.qi, HD ** -0.5)):
                for f in range(FT):
                    b, out = take()
                    b.empty(nc.scalar.activation(dest[:, f, :], out[:, :], ACT.Copy, scale=scale))
            for dest in (m.ck, m.ki):
                b, out = take()
                b.empty(nc.scalar.activation(dest[:, :], out[:, :], ACT.Copy))
            b, out = take()
            b.empty(nc.scalar.activation(m.wiT[:, :], out[0:IDX_HEADS, :], ACT.Copy, scale=IDX_HEADS ** -0.5))
            b, out = take()
            nc.scalar.activation(m.lo_da[0:HD, :], out[0:HD, :], ACT.Tanh)
            b.empty(nc.scalar.activation(m.lo_da[HD:P, :], out[HD:P, :], ACT.Copy))
            b, out = take()
            b.empty(nc.scalar.activation(m.lo_g[:, :], out[:, :], ACT.Sigmoid))

        @block.vector
        def _(dve):
            link = chain(dve, own)
            link(nc.vector.memset(raw[0][:, 0:1], 0.0))
            nc.vector.memset(raw[1][:, 0:1], 0.0).then_inc(raw_zero, 1)
            dve.wait_ge(prm_in, 16 * 7)
            link(nc.vector.tensor_scalar(less[:, :, :], m.mu[:, :, :], -1.0, 1.0, ALU.mult, ALU.add))
            for wl, lo, i in ((wda, 0, 0), (wda, HD, 1), (wg, 0, 2)):
                n = HD if wl is wda else P
                mub = mu[:, i, :].rearrange("p (k o) -> p k o", o=1).to_broadcast([P, KD, n])
                link(nc.vector.tensor_tensor(wl[:, 1, :, lo:lo + n], wl[:, 0, :, lo:lo + n], mub, ALU.mult))
                link(nc.vector.tensor_tensor(wl[:, 0, :, lo:lo + n], wl[:, 0, :, lo:lo + n], wl[:, 1, :, lo:lo + n],
                                             ALU.subtract))
            dve.sem_inc(lora_w, 1)
            for n in range(3 * FT):
                i, f = n // FT, n % FT
                z = m.rkv[i][:, f, :]
                dve.wait_ge(raw_out, n + 1)
                link(nc.vector.tensor_scalar(z, raw[n % 2][:, 1:T + 1], less[:, i, f:f + 1], None, ALU.mult))
                nc.vector.scalar_tensor_tensor(out=z, in0=raw[n % 2][:, 0:T], scalar=m.mu[:, i, f:f + 1], in1=z,
                                               op0=ALU.mult, op1=ALU.add).then_inc(raw_read, 1)


@stage
def rwkv_prepare(nc, c, ctx, ps, m, prm):
    R, K, V = m.rkv
    w2a2 = c.sb("w2a2", [P, A_WIDTH], ctx=ctx)
    g2 = c.sb("g2", [P, A_WIDTH], ctx=ctx)
    vec = c.sb("vec", [P, 5, FT], ctx=ctx)
    dec, rn, sq, rw = (c.sb(n, [P, FT, T], ctx=ctx) for n in ("decay", "rnorm", "square", "rW"))
    zero = c.sb("zero", [P, CH], ctx=ctx)
    lora_in, vec_in, own = c.sem("lora_in"), c.sem("vec_in"), c.sem("dve_own")
    kk0, sq_done, clamped, root, dec_done, own_act = (c.sem("kk0"), c.sem("sq_done"), c.sem("clamped"), c.sem("root"),
                                                      c.sem("dec_done"), c.sem("act_own"))
    km_done, bonus_in, pool_own, W_done = c.sem("km_done"), c.sem("bonus_in"), c.sem("pool_own"), c.sem("W_done")
    sems = bank_sems(c, "prep")
    V_ = nc.vector

    with nc.Block() as block:

        @block.sync
        def _(sp):
            for i, name in enumerate(("w0", "a0", "k_k", "k_a", "r_k")):
                sp.dma_start(vec[:, i, :], prm[name].rearrange("(f p) -> p f", p=P),
                             allow_slow_non_contiguous=True).then_inc(vec_in, 16)
            sp.dma_start(w2a2[0:HD, :], prm["w2"]).then_inc(lora_in, 16)
            sp.dma_start(w2a2[HD:P, :], prm["a2"]).then_inc(lora_in, 16)
            sp.dma_start(g2[:, :], prm["g2"]).then_inc(lora_in, 16)

        @block.tensor
        def _(pe):
            banks = bank_set(ps, sems)
            pe.wait_ge(lora_in, 48)
            n = 0
            for lhsT, rhs in ((w2a2[0:HD], m.lo_da[0:HD, :]), (w2a2[HD:P], m.lo_da[HD:P, :]), (g2[:], m.lo_g[:, :])):
                for f in range(FT):
                    b = banks[n % 4]
                    n += 1
                    b.open(pe)
                    b.close(nc.tensor.matmul(b.ps[:, :], lhsT[:, f * P:(f + 1) * P], rhs, start=True, stop=True))
            for f in range(FT):
                pe.wait_ge(sq_done, f + 1)
                b = banks[4 + f]
                b.open(pe)
                b.close(nc.tensor.matmul(b.ps[:, :], c.headones[:, :], sq[:, f, :], start=True, stop=True))
            for f in range(FT):
                pe.wait_ge(bonus_in, f + 1)
                b = banks[4 + f]
                b.open(pe)
                b.close(nc.tensor.matmul(b.ps[:, :], c.headones[:, :], m.bonus[:, f, :], start=True, stop=True))

        @block.scalar
        def _(act):
            banks = bank_set(ps, sems)
            act.wait_ge(vec_in, 16 * 5)
            n = 0
            for dest, i in ((dec, 0), (m.rate, 1), (m.gate, None)):
                for f in range(FT):
                    b = banks[n % 4]
                    n += 1
                    out = b.read(act)
                    if i is None:
                        b.empty(nc.scalar.activation(dest[:, f, :], out[:, :], ACT.Copy))
                    else:
                        b.empty(nc.scalar.activation(dest[:, f, :], out[:, :], ACT.Sigmoid, bias=vec[:, i, f:f + 1]))
            act.wait_ge(banks[3].emptied, banks[3].n)
            act.wait_ge(banks[2].emptied, banks[2].n)
            act.wait_ge(banks[1].emptied, banks[1].n)
            act.wait_ge(banks[0].emptied, banks[0].n)
            nc.scalar.activation(dec[:, :, :], dec[:, :, :], ACT.Exp, scale=-DECAY).then_inc(dec_done, 1)
            act.wait_ge(clamped, 1)
            nc.scalar.activation(rn[:, :, :], rn[:, :, :], ACT.Sqrt).then_inc(root, 1)

        @block.gpsimd
        def _(pool):
            link = chain(pool, pool_own)
            for f in range(FT):
                pool.wait_ge(kk0, f + 1)
                nc.gpsimd.tensor_tensor(sq[:, f, :], m.kk[:, f, :], m.kk[:, f, :], ALU.mult).then_inc(sq_done, 1)
            for f in range(FT):
                pool.wait_ge(km_done, f + 1)
                link(nc.gpsimd.tensor_tensor(m.bonus[:, f, :], R[:, f, :], m.kmod[:, f, :], ALU.mult))
                nc.gpsimd.tensor_scalar(m.bonus[:, f, :], m.bonus[:, f, :], vec[:, 4, f:f + 1], None,
                                        ALU.mult).then_inc(bonus_in, 1)
            pool.wait_ge(bonus_in, FT)
            pool.wait_ge(W_done, FT)
            for f in range(FT):
                nc.gpsimd.tensor_tensor(R[:, f, :], R[:, f, :], m.W[:, f, :], ALU.mult)

        @block.vector
        def _(dve):
            banks = bank_set(ps, sems)
            link = chain(dve, own)
            link(V_.memset(zero[:, :], 0.0))
            dve.wait_ge(vec_in, 16 * 5)
            for f in range(FT):
                V_.tensor_scalar(m.kk[:, f, :], K[:, f, :], vec[:, 2, f:f + 1], None, ALU.mult).then_inc(kk0, 1)
            dve.wait_ge(dec_done, 1)
            for f in range(FT):
                link(V_.tensor_scalar(m.kmod[:, f, :], m.rate[:, f, :], 1.0, vec[:, 3, f:f + 1], ALU.subtract, ALU.mult))
                V_.scalar_tensor_tensor(out=m.kmod[:, f, :], in0=m.kmod[:, f, :], scalar=1.0, in1=K[:, f, :],
                                        op0=ALU.add, op1=ALU.mult).then_inc(km_done, 1)
            for f in range(FT):
                out = banks[4 + f].read(dve)
                ins = V_.tensor_scalar(rn[:, f, :], out[:, :], 1e-12, None, ALU.max)
                banks[4 + f].empty(ins)
            for f in range(FT):
                dve.wait_ge(banks[4 + f].emptied, 1)
            dve.sem_inc(clamped, 1)
            for f in range(FT):
                for i in range(NCH):
                    part = slice(i * CH, (i + 1) * CH)
                    ins = V_.tensor_tensor_scan(m.W[:, f, part], dec[:, f, part], zero[:, :], 1.0, ALU.mult, ALU.add)
                link(ins)
                dve.sem_inc(W_done, 1)
            link(V_.reciprocal(rw[:, :, :], m.W[:, :, :]))
            dve.wait_ge(root, 1)
            link(V_.reciprocal(rn[:, :, :], rn[:, :, :]))
            link(V_.tensor_tensor(m.kk[:, :, :], m.kk[:, :, :], rn[:, :, :], ALU.mult))
            link(V_.tensor_tensor(m.rate[:, :, :], m.rate[:, :, :], m.kk[:, :, :], ALU.mult))
            link(V_.tensor_tensor(m.rate[:, :, :], m.rate[:, :, :], rw[:, :, :], ALU.mult))
            kkc = m.kk[:, :, :].rearrange("p f (c i) -> p (f c) i", i=CH)
            Wc = m.W[:, :, :].rearrange("p f (c i) -> p (f c) i", i=CH)
            link(V_.tensor_tensor(kkc[:, :, 1:CH], kkc[:, :, 1:CH], Wc[:, :, 0:CH - 1], ALU.mult))
            for f in range(FT):
                out = banks[4 + f].read(dve)
                link(V_.tensor_tensor(m.bonus[:, f, :], out[:, :], V[:, f, :], ALU.mult))
                banks[4 + f].empty(V_.tensor_tensor(m.kmod[:, f, :], m.kmod[:, f, :], rw[:, f, :], ALU.mult))


@stage
def rwkv_chunks(nc, c, ctx, ps, m, yA):
    al, be, ka, rho, V, W = m.kk, m.rate, m.kmod, m.rkv[0], m.rkv[2], m.W
    LEVELS = CH.bit_length() - 2
    mask = c.sb("mask", [P, 4, P], ctx=ctx)
    grams = ["AT", "QbT", "NT", "QkT", "A"]
    G = {g: c.sb(g, [P, 2, FT, P], ctx=ctx) for g in ("QbT", "NT", "QkT")}
    A = [c.sb(f"A{i}", [P, 2, FT, P], ctx=ctx) for i in range(2)]
    AT = [c.sb(f"AT{i}", [P, 2, FT, P], ctx=ctx) for i in range(2)]
    XT = c.sb("XT", [P, 2, FT, P], ctx=ctx)
    Cm = c.sb("Cm", [P, 2, FT, P], ctx=ctx)
    vt, kt, bt = (c.sb(n, [P, FT, P], ctx=ctx) for n in ("v_tok", "kappa_tok", "beta_tok"))
    U0, Wt, nU = (c.sb(n, [P, FT, P], ctx=ctx) for n in ("U0", "Walpha", "minusU"))
    WT = c.sb("WalphaT", [P, FT, P], ctx=ctx)
    S = c.sb("state", [P, FT, P], ctx=ctx)
    made, own, x_ready, mask_ready = c.sem("masks_made"), c.sem("dve_own"), c.sem("XT_ready"), c.sem("mask_ready")
    gram_out, s_ready, vt_out = c.sem("gram_out"), c.sem("state_ready"), c.sem("vt_out")
    sems = bank_sems(c, "chunk")

    def heads():
        return [(par, f) for par in range(2) for f in range(FT)]

    with nc.Block() as block:

        @block.gpsimd
        def _(pool):
            link = chain(pool, made)
            G_ = nc.gpsimd
            for i, (cmp, sign, chan) in enumerate(((ALU.is_gt, -1.0, -1), (ALU.is_gt, -1.0, 1),
                                                   (ALU.is_gt, 1.0, -1), (ALU.is_ge, 1.0, -1))):
                link(G_.memset(mask[:, i, :], sign))
                link(G_.affine_select(out=mask[:, i, :], in_=mask[:, i, :], compare_op=cmp, fill=0.0, base=0,
                                      pattern=[[-chan, P]], channel_multiplier=chan))
                link(G_.memset(mask[0:CH, i, CH:P], 0.0))
                link(G_.memset(mask[CH:P, i, 0:CH], 0.0))
            link(G_.memset(S[:, :, :], 0.0))
            pool.sem_inc(mask_ready, 1)
            for t in range(TT):
                for par in range(2):
                    pool.wait_ge(gram_out, 2 * t + par + 1)
                    G_.tensor_tensor(XT[:, par, :, :], AT[0][:, par, :, :],
                                     c.ident[:, :].rearrange("p (o n) -> p o n", o=1).to_broadcast([P, FT, P]),
                                     ALU.add).then_inc(x_ready, 1)

        @block.tensor
        def _(pe):
            B = bank_set(ps, sems)
            M = nc.tensor.matmul

            def four(b, one):
                out = b.open(pe)
                for f in range(FT):
                    last = one(out[:, f * P:(f + 1) * P], f)
                b.close(last)

            def mm(lhsT, rhs):
                return lambda out, f: M(out, lhsT(f), rhs(f), start=True, stop=True)

            pe.wait_ge(mask_ready, 1)
            for t in range(TT):
                tok = slice(t * P, (t + 1) * P)
                for b, src in ((B[0], V), (B[4], ka), (B[1], be), (B[5], al)):
                    four(b, lambda out, f: nc.tensor.transpose(out, src[:, f, tok], c.ident[:, :]))
                n = 0
                for par in range(2):
                    q = slice(par * HD, (par + 1) * HD)
                    for g in grams:
                        l, r = dict(AT=(be, al), QbT=(be, rho), NT=(ka, al), QkT=(ka, rho), A=(al, be))[g]
                        four(B[(2 + n) % 4], mm(lambda f: l[q, f, tok], lambda f: r[q, f, tok]))
                        n += 1
                for b in B[0:4]:
                    b.copied(pe)
                for lv in range(1, LEVELS + 1):
                    old, new = (lv - 1) % 2, lv % 2
                    for par in range(2):
                        four(B[4 + par], mm(lambda f: AT[old][:, par, f, :], lambda f: A[old][:, par, f, :]))
                        if lv < LEVELS:
                            four(B[6 + par], mm(lambda f: A[old][:, par, f, :], lambda f: AT[old][:, par, f, :]))
                    for par in range(2):
                        B[4 + par].copied(pe)
                        if lv == 1:
                            pe.wait_ge(x_ready, 2 * t + par + 1)
                        else:
                            B[par].copied(pe)
                        four(B[par], mm(lambda f: A[new][:, par, f, :], lambda f: XT[:, par, f, :]))
                        if lv < LEVELS:
                            B[6 + par].copied(pe)
                for par in range(2):
                    four(B[2 + par], mm(lambda f: G["NT"][:, par, f, :], lambda f: vt[:, f, :]))
                for par in range(2):
                    B[2 + par].copied(pe)
                    B[par].copied(pe)
                    B[5].copied(pe)
                    four(B[par], mm(lambda f: XT[:, par, f, :], lambda f: Cm[:, par, f, :]))
                B[0].copied(pe)
                B[1].copied(pe)
                four(B[4], lambda out, f: nc.tensor.transpose(out, Wt[:, f, :], c.ident[:, :]))
                B[4].copied(pe)
                y = B[5].open(pe)
                for s in range(2):
                    p = slice(s * CH, (s + 1) * CH)
                    cur = slice(t * P + s * CH, t * P + (s + 1) * CH)
                    if t or s:
                        B[3].copied(pe)
                    out = B[2].open(pe)
                    for f in range(FT):
                        last = M(out[p, f * P:(f + 1) * P], WT[:, f, p], S[:, f, :], start=True, stop=True)
                    B[2].close(last)
                    for f in range(FT):
                        M(y[:, f * P + s * CH:f * P + (s + 1) * CH], S[:, f, :], rho[:, f, cur],
                          start=s == 0 and f == 0, stop=False, skip_group_check=True)
                    if s == 0:
                        for par, f in heads():
                            q = slice(par * HD, (par + 1) * HD)
                            M(y[q, f * P:(f + 1) * P], vt[:, f, q], G["QkT"][:, par, f, :],
                              start=False, stop=False, skip_group_check=True)
                    out = B[3].open(pe)
                    B[2].copied(pe)
                    for f in range(FT):
                        M(out[:, f * P:(f + 1) * P], kt[p, f, :], vt[p, f, :], start=True, stop=False)
                        last = M(out[:, f * P:(f + 1) * P], bt[p, f, :], nU[p, f, :], start=False, stop=True)
                    B[3].close(last)
                for par, f in heads():
                    q = slice(par * HD, (par + 1) * HD)
                    last = M(y[q, f * P:(f + 1) * P], nU[:, f, q], G["QbT"][:, par, f, :],
                             start=False, stop=(par, f) == (1, FT - 1), skip_group_check=True)
                B[5].close(last)

        def view(out):
            return out[:, :].rearrange("p (f n) -> p f n", f=FT)

        @block.scalar
        def _(act):
            B = bank_set(ps, sems)
            cp = lambda out, in_: nc.scalar.activation(out, in_, ACT.Copy)
            for t in range(TT):
                o = view(B[4].read(act))
                B[4].empty(cp(kt[:, :, :], o))
                o = view(B[5].read(act))
                cp(Cm[:, 0, :, HD:P], o[:, :, 0:HD])
                B[5].empty(cp(Cm[:, 1, :, HD:P], o[:, :, HD:P]))
                for lv in range(1, LEVELS + 1):
                    for par in range(2):
                        B[4 + par].empty(cp(A[lv % 2][:, par, :, :], view(B[4 + par].read(act))))
                        if lv < LEVELS:
                            B[6 + par].empty(cp(AT[lv % 2][:, par, :, :], view(B[6 + par].read(act))))
                B[4].empty(cp(WT[:, :, :], view(B[4].read(act))))
                B[5].empty(cp(yA[:, :, t * P:(t + 1) * P], view(B[5].read(act))))

        @block.vector
        def _(dve):
            B = bank_set(ps, sems)
            link = chain(dve, own)
            V_ = nc.vector
            dve.wait_ge(mask_ready, 1)
            dest = dict(AT=(AT[0], 0), QbT=(G["QbT"], 3), NT=(G["NT"], 2), QkT=(G["QkT"], 3), A=(A[0], 1))
            for t in range(TT):
                B[0].empty(V_.tensor_copy(vt[:, :, :], view(B[0].read(dve))))
                B[1].empty(V_.tensor_copy(bt[:, :, :], view(B[1].read(dve))))
                n = 0
                for par in range(2):
                    for g in grams:
                        b = B[(2 + n) % 4]
                        n += 1
                        out, i = dest[g]
                        ins = V_.tensor_tensor(out[:, par, :, :], view(b.read(dve)),
                                               mask[:, i:i + 1, :].to_broadcast([P, FT, P]), ALU.mult)
                        b.empty(ins)
                        if g == "AT":
                            dve.wait_ge(b.emptied, b.n)
                            dve.sem_inc(gram_out, 1)
                for lv in range(1, LEVELS + 1):
                    for par in range(2):
                        B[par].empty(V_.tensor_tensor(XT[:, par, :, :], view(B[par].read(dve)), XT[:, par, :, :],
                                                      ALU.add))
                for par in range(2):
                    B[2 + par].empty(V_.tensor_copy(Cm[:, par, :, 0:HD],
                                                    view(B[2 + par].read(dve))[:, :, par * HD:(par + 1) * HD]))
                for par in range(2):
                    q = slice(par * HD, (par + 1) * HD)
                    o = view(B[par].read(dve))
                    V_.tensor_copy(U0[:, :, q], o[:, :, 0:HD])
                    B[par].empty(V_.tensor_copy(Wt[:, :, q], o[:, :, HD:P]))
                for par in range(2):
                    dve.wait_ge(B[par].emptied, B[par].n)
                for s in range(2):
                    p = slice(s * CH, (s + 1) * CH)
                    end = t * P + (s + 1) * CH - 1
                    o = view(B[2].read(dve))
                    B[2].empty(V_.scalar_tensor_tensor(out=nU[p, :, :], in0=o[p, :, :], scalar=-1.0, in1=U0[p, :, :],
                                                       op0=ALU.mult, op1=ALU.subtract))
                    o = view(B[3].read(dve))
                    for par in range(2):
                        q = slice(par * HD, (par + 1) * HD)
                        link(V_.tensor_tensor(S[q, :, q], o[q, :, q], S[q, :, q], ALU.add))
                        ins = V_.tensor_tensor(S[q, :, q], S[q, :, q],
                                               W[q, :, end:end + 1].to_broadcast([HD, FT, HD]), ALU.mult)
                        if par == 0:
                            link(ins)
                    B[3].empty(ins)
                    dve.wait_ge(B[3].emptied, B[3].n)


@stage
def rwkv_finish(nc, c, ctx, ps, m, yA, yT, prm):
    vec = c.sb("ln", [P, 2, FT], ctx=ctx)
    sq = c.sb("sq", [P, FT, T], ctx=ctx)
    vec_in, centred, sq_done, root, own = (c.sem("ln_in"), c.sem("centred"), c.sem("sq_done"), c.sem("root"),
                                           c.sem("dve_own"))
    sum_done, var_done = c.sem("sum_done"), c.sem("var_done")
    with nc.Block() as block:

        @block.sync
        def _(sp):
            for i, name in enumerate(("ln_g", "ln_b")):
                sp.dma_start(vec[:, i, :], prm[name].rearrange("(f p) -> p f", p=P),
                             allow_slow_non_contiguous=True).then_inc(vec_in, 16)

        @block.tensor
        def _(pe):
            for f in range(FT):
                nc.tensor.matmul(ps[f][:, :], c.headones[:, :], yA[:, f, :], start=True, stop=True).then_inc(sum_done, 1)
            for f in range(FT):
                pe.wait_ge(sq_done, f + 1)
                nc.tensor.matmul(ps[4 + f][:, :], c.headones[:, :], sq[:, f, :], start=True, stop=True
                                 ).then_inc(var_done, 1)

        @block.gpsimd
        def _(pool):
            for f in range(FT):
                pool.wait_ge(centred, f + 1)
                nc.gpsimd.tensor_tensor(sq[:, f, :], yA[:, f, :], yA[:, f, :], ALU.mult).then_inc(sq_done, 1)

        @block.scalar
        def _(act):
            for f in range(FT):
                act.wait_ge(var_done, f + 1)
                nc.scalar.activation(sq[:, f, :], ps[4 + f][:, :], ACT.Sqrt, scale=1.0 / HD,
                                     bias=c.eps[:, 1:2]).then_inc(root, 1)

        @block.vector
        def _(dve):
            link = chain(dve, own)
            V_ = nc.vector
            for f in range(FT):
                dve.wait_ge(sum_done, f + 1)
                V_.scalar_tensor_tensor(out=yA[:, f, :], in0=ps[f][:, :], scalar=-1.0 / HD, in1=yA[:, f, :],
                                        op0=ALU.mult, op1=ALU.add).then_inc(centred, 1)
            dve.wait_ge(vec_in, 32)
            dve.wait_ge(centred, FT)
            for f in range(FT):
                y = yA[:, f, :]
                dve.wait_ge(root, f + 1)
                link(V_.reciprocal(sq[:, f, :], sq[:, f, :]))
                link(V_.tensor_tensor(y, y, sq[:, f, :], ALU.mult))
                link(V_.tensor_scalar(y, y, vec[:, 0, f:f + 1], vec[:, 1, f:f + 1], ALU.mult, ALU.add))
                link(V_.tensor_tensor(y, y, m.bonus[:, f, :], ALU.add))
                link(V_.tensor_tensor(yT[:, f, :], y, m.gate[:, f, :], ALU.mult))


@stage
def sparse_prepare(nc, c, ctx, ps, m, prm):
    wkv = c.sb("w_kv_up", [P, 2 * B_WIDTH], ctx=ctx)
    gkv = c.sb("kv_gain", [P, 1], ctx=ctx)
    gki = c.sb("ki_gain", [P, 1], ctx=ctx)
    sq = c.sb("sq", [P, 2, T], ctx=ctx)
    w_in, sq_done, sum_done, root, own = (c.sem("wkv_in"), c.sem("sq_done"), c.sem("sum_done"), c.sem("root"),
                                          c.sem("dve_own"))
    normed, up_done, wi_done, up_out = c.sem("normed"), c.sem("up_done"), c.sem("wi_done"), c.sem("up_out")
    with nc.Block() as block:

        @block.sync
        def _(sp):
            sp.dma_start(wkv[:, :], prm["w_kv_up"]).then_inc(w_in, 16)
            sp.dma_start(gkv[:, :], prm["kv_norm"].rearrange("(p o) -> p o", o=1)).then_inc(w_in, 16)
            for i in range(2):
                sp.dma_start(gki[i * HD:(i + 1) * HD, :],
                             prm["idx_k_norm"].rearrange("(p o) -> p o", o=1)).then_inc(w_in, 16)

        @block.tensor
        def _(pe):
            for t in range(TT):
                last = nc.tensor.transpose(ps[2][:, t * IDX_HEADS:(t + 1) * IDX_HEADS],
                                           m.wiT[:, t * P:(t + 1) * P], c.ident[0:IDX_HEADS, 0:IDX_HEADS])
            last.then_inc(wi_done, 1)
            for i, mat in enumerate((c.ones, c.headones)):
                pe.wait_ge(sq_done, i + 1)
                nc.tensor.matmul(ps[i][:, :], mat[:, :], sq[:, i, :], start=True, stop=True).then_inc(sum_done, 1)
            pe.wait_ge(w_in, 64)
            pe.wait_ge(normed, 1)
            for f in range(FT):
                if f >= 1:
                    pass
                nc.tensor.matmul(ps[3 + f][:, :], wkv[:, f * P:(f + 1) * P], m.ck[:, :], start=True, stop=True
                                 ).then_inc(up_done, 1)
            for t in range(TT):
                pe.wait_ge(up_out, t + 1)
                nc.tensor.matmul(ps[3 + t][:, :], m.ck[:, t * P:(t + 1) * P], wkv[:, B_WIDTH:2 * B_WIDTH],
                                 start=True, stop=True).then_inc(up_done, 1)

        @block.scalar
        def _(act):
            for i, src in enumerate((m.ck, m.ki)):
                nc.scalar.activation(sq[:, i, :], src[:, :], ACT.Square).then_inc(sq_done, 1)
            for i, n in enumerate((KV_RANK, HD)):
                act.wait_ge(sum_done, i + 1)
                nc.scalar.activation(sq[:, i, :], ps[i][:, :], ACT.Sqrt, scale=1.0 / n,
                                     bias=c.eps[:, 0:1]).then_inc(root, 1)
            for n in range(2 * FT):
                act.wait_ge(up_done, n + 1)
                dest = m.kb[:, n, :] if n < FT else m.vb[:, n - FT, :]
                nc.scalar.activation(dest, ps[3 + n % FT][:, :], ACT.Copy).then_inc(up_out, 1)

        @block.vector
        def _(dve):
            link = chain(dve, own)
            V_ = nc.vector
            dve.wait_ge(w_in, 64)
            for i, (x, g) in enumerate(((m.ck, gkv), (m.ki, gki))):
                dve.wait_ge(root, i + 1)
                link(V_.reciprocal(sq[:, i, :], sq[:, i, :]))
                V_.scalar_tensor_tensor(out=x[:, :], in0=x[:, :], scalar=g[:, 0:1], in1=sq[:, i, :],
                                        op0=ALU.mult, op1=ALU.mult).then_inc(normed, 1)
            dve.wait_ge(wi_done, 1)
            V_.tensor_copy(m.wi[:, :, :], ps[2][:, 0:TT * IDX_HEADS].rearrange("p (t h) -> p t h", t=TT))


@stage
def index_select(nc, c, ctx, ps, m):
    score = [c.sb(f"score{t}", [P, T], ctx=ctx) for t in range(TT)]
    best = [c.sb(f"best{t}", [P, 8], ctx=ctx) for t in range(TT)]
    rl = [c.sb(f"relu{i}", [P, T], ctx=ctx) for i in range(4)]
    dots, relu, added, own = c.sem("dots"), c.sem("relu"), c.sem("added"), c.sem("dve_own")
    scored, masked, zeroed = c.sem("scored"), c.sem("masked"), c.sem("zeroed")
    tiles = [3, 2, 1]
    units = [(t, h) for t in tiles for h in range(IDX_HEADS)]
    with nc.Block() as block:

        @block.tensor
        def _(pe):
            for u, (t, h) in enumerate(units):
                q = slice((h % 2) * HD, (h % 2 + 1) * HD)
                if u >= 4:
                    pe.wait_ge(relu, u - 3)
                nc.tensor.matmul(ps[u % 4][:, 0:(t + 1) * P], m.qi[q, h // 2, t * P:(t + 1) * P],
                                 m.ki[q, 0:(t + 1) * P], start=True, stop=True).then_inc(dots, 1)

        @block.scalar
        def _(act):
            for u, (t, h) in enumerate(units):
                act.wait_ge(dots, u + 1)
                if u >= 4:
                    act.wait_ge(added, u - 3)
                nc.scalar.activation(rl[u % 4][:, 0:(t + 1) * P], ps[u % 4][:, 0:(t + 1) * P],
                                     ACT.Relu).then_inc(relu, 1)

        @block.gpsimd
        def _(pool):
            G_ = nc.gpsimd
            G_.memset(m.bias[:, 0, 0:P], 0.0).then_inc(zeroed, 1)
            pool.wait_ge(zeroed, 1)
            G_.affine_select(out=m.bias[:, 0, 0:P], in_=m.bias[:, 0, 0:P], compare_op=ALU.is_ge, fill=NEG, base=0,
                             pattern=[[-1, P]], channel_multiplier=1)
            for i, t in enumerate(tiles):
                pool.wait_ge(scored, i + 1)
                part = score[t][:, t * P:(t + 1) * P]
                G_.affine_select(out=part, in_=part, compare_op=ALU.is_ge, fill=NEG, base=0,
                                 pattern=[[-1, P]], channel_multiplier=1).then_inc(masked, 1)

        @block.vector
        def _(dve):
            link = chain(dve, own)
            V_ = nc.vector

            def scores(t):
                for u, (tu, h) in enumerate(units):
                    if tu != t:
                        continue
                    s, r = score[t][:, 0:(t + 1) * P], rl[u % 4][:, 0:(t + 1) * P]
                    dve.wait_ge(relu, u + 1)
                    if h == 0:
                        V_.tensor_scalar(s, r, m.wi[:, t, h:h + 1], None, ALU.mult).then_inc(added, 1)
                    else:
                        dve.wait_ge(added, u)
                        V_.scalar_tensor_tensor(out=s, in0=r, scalar=m.wi[:, t, h:h + 1], in1=s,
                                                op0=ALU.mult, op1=ALU.add).then_inc(added, 1)
                dve.wait_ge(added, u + 1 if t == tiles[-1] else (tiles.index(t) + 1) * IDX_HEADS)
                dve.sem_inc(scored, 1)

            def search(t):
                s = score[t][:, 0:(t + 1) * P]
                dve.wait_ge(masked, tiles.index(t) + 1)
                for _ in range(TOPK // 8):
                    link(V_.max(best[t][:, :], s))
                    link(V_.match_replace(s, best[t][:, :], s, TAKEN))
                V_.tensor_scalar(m.bias[:, t, 0:(t + 1) * P], s, TAKEN / 2, NEG, ALU.is_gt, ALU.mult)

            scores(3)
            scores(2)
            search(3)
            scores(1)
            search(2)
            search(1)


@stage
def sparse_attend(nc, c, ctx, ps, m, yT):
    units = [(h, t) for h in range(B_HEADS) for t in range(TT)]
    N = len(units)
    RING, LT, LP = 4, 3, 4
    lg = [c.sb(f"prob{i}", [P, T], ctx=ctx) for i in range(RING)]
    pT = [c.sb(f"probT{i}", [P, T], ctx=ctx) for i in range(2)]
    nmax = c.sb("minus_max", [P, N], ctx=ctx)
    tot = c.sb("total", [P, N], ctx=ctx)
    inv = c.sb("inverse", [P, N], ctx=ctx)
    qk, biased, maxed, exped, inverted, scaled, turned, pT_out, pv, y_out = (
        c.sem(n) for n in ("qk", "biased", "maxed", "exped", "inverted", "scaled", "turned", "pT_out", "pv", "y_out"))
    ps_z, ps_t, ps_y = ps[0:3], ps[3:5], ps[5:7]
    with nc.Block() as block:

        @block.tensor
        def _(pe):
            for i in range(N + LP):
                if i < N:
                    h, t = units[i]
                    q = slice((h % 2) * HD, (h % 2 + 1) * HD)
                    if i >= 3:
                        pe.wait_ge(biased, i - 2)
                    nc.tensor.matmul(ps_z[i % 3][:, 0:(t + 1) * P], m.qb[q, h // 2, t * P:(t + 1) * P],
                                     m.kb[q, h // 2, 0:(t + 1) * P], start=True, stop=True).then_inc(qk, 1)
                u = i - LT
                if 0 <= u < N:
                    pe.wait_ge(scaled, u + 1)
                    if u >= 2:
                        pe.wait_ge(pT_out, u - 1)
                    for b in range(units[u][1] + 1):
                        last = nc.tensor.transpose(ps_t[u % 2][:, b * P:(b + 1) * P],
                                                   lg[u % RING][:, b * P:(b + 1) * P], c.ident[:, :])
                    last.then_inc(turned, 1)
                u = i - LP
                if 0 <= u < N:
                    h, t = units[u]
                    q = slice((h % 2) * HD, (h % 2 + 1) * HD)
                    pair = h // 2
                    pe.wait_ge(pT_out, u + 1)
                    if h % 2 == 0 and t == 0 and pair >= 2:
                        pe.wait_ge(y_out, pair - 1)
                    for b in range(t + 1):
                        last = nc.tensor.matmul(ps_y[pair % 2][q, t * P:(t + 1) * P], m.vb[:, b, h * HD:(h + 1) * HD],
                                                pT[u % 2][:, b * P:(b + 1) * P], start=b == 0, stop=b == t)
                    last.then_inc(pv, 1)

        @block.vector
        def _(dve):
            V_ = nc.vector
            for i in range(N + 1):
                if i < N:
                    h, t = units[i]
                    L = (t + 1) * P
                    dve.wait_ge(qk, i + 1)
                    if i >= RING:
                        dve.wait_ge(turned, i - RING + 1)
                    V_.tensor_tensor(lg[i % RING][:, 0:L], ps_z[i % 3][:, 0:L], m.bias[:, t, 0:L],
                                     ALU.add).then_inc(biased, 1)
                    dve.wait_ge(biased, i + 1)
                    V_.tensor_reduce(nmax[:, i:i + 1], lg[i % RING][:, 0:L], AX.X, ALU.max,
                                     negate=True).then_inc(maxed, 1)
                if i >= 1:
                    dve.wait_ge(exped, i)
                    V_.reciprocal(inv[:, i - 1:i], tot[:, i - 1:i]).then_inc(inverted, 1)

        @block.scalar
        def _(act):
            for i in range(N + LT):
                if i < N:
                    L = (units[i][1] + 1) * P
                    act.wait_ge(maxed, i + 1)
                    nc.scalar.activation(lg[i % RING][:, 0:L], lg[i % RING][:, 0:L], ACT.Exp,
                                         bias=nmax[:, i:i + 1], accum_out=tot[:, i:i + 1]).then_inc(exped, 1)
                u = i - LT
                if u >= 0:
                    L = (units[u][1] + 1) * P
                    act.wait_ge(turned, u + 1)
                    if u >= 2:
                        act.wait_ge(pv, u - 1)
                    nc.scalar.activation(pT[u % 2][:, 0:L], ps_t[u % 2][:, 0:L], ACT.Copy).then_inc(pT_out, 1)
                    if u % 8 == 2 and u > 8:
                        pair = u // 8 - 1
                        act.wait_ge(pv, 8 * (pair + 1))
                        nc.scalar.activation(yT[:, FT + pair, :], ps_y[pair % 2][:, :], ACT.Copy).then_inc(y_out, 1)
            pair = B_HEADS // 2 - 1
            act.wait_ge(pv, N)
            nc.scalar.activation(yT[:, FT + pair, :], ps_y[pair % 2][:, :], ACT.Copy).then_inc(y_out, 1)

        @block.gpsimd
        def _(pool):
            for i, (h, t) in enumerate(units):
                L = (t + 1) * P
                pool.wait_ge(inverted, i + 1)
                nc.gpsimd.tensor_scalar(lg[i % RING][:, 0:L], lg[i % RING][:, 0:L], inv[:, i:i + 1], None,
                                        ALU.mult).then_inc(scaled, 1)


class Mixed:
    pass


def even_mixer(nc, c, ps, x, gain, w_in, w_out, prm):
    with ExitStack() as ctx:
        yT = c.sb("yT", [P, KD, T], ctx=ctx)
        with ExitStack() as mid:
            m = Mixed()
            m.qb, m.qi = (c.sb(n, [P, FT, T], ctx=mid) for n in ("q_b", "q_idx"))
            m.ck, m.ki = (c.sb(n, [P, T], ctx=mid) for n in ("c_kv", "k_idx"))
            m.wiT = c.sb("w_idxT", [IDX_HEADS, T], ctx=mid)
            with ExitStack() as rw:
                m.rkv = [c.sb(n, [P, FT, T], ctx=rw) for n in "rkv"]
                m.mu = c.sb("mu_rkv", [P, 3, FT], ctx=rw)
                m.lo_da, m.lo_g = c.sb("lora_da", [P, T], ctx=rw), c.sb("lora_g", [P, T], ctx=rw)
                with ExitStack() as proj:
                    xn = c.sb("xn", [P, TT, D], ctx=proj)
                    hT = c.sb("hT", [P, KD, T + 1], ctx=proj)
                    norm_transpose(nc, c, proj, ps, x, xn, hT, gain)
                    even_project(nc, c, proj, ps, hT, w_in, m, prm)
                m.rate, m.gate, m.kk, m.kmod, m.bonus, m.W = (
                    c.sb(n, [P, FT, T], ctx=rw) for n in ("rate", "gate", "kk", "k_mod", "bonus", "W"))
                with ExitStack() as prep:
                    rwkv_prepare(nc, c, prep, ps, m, prm)
                yA = c.sb("yA", [P, FT, T], ctx=rw)
                with ExitStack() as chunks:
                    rwkv_chunks(nc, c, chunks, ps, m, yA)
                with ExitStack() as fin:
                    rwkv_finish(nc, c, fin, ps, m, yA, yT, prm)
            with ExitStack() as sp:
                m.kb, m.vb, m.bias = (c.sb(n, [P, FT, T], ctx=sp) for n in ("k_b", "v_b", "bias"))
                m.wi = c.sb("w_idx", [P, TT, IDX_HEADS], ctx=sp)
                with ExitStack() as inner:
                    sparse_prepare(nc, c, inner, ps, m, prm)
                with ExitStack() as inner:
                    index_select(nc, c, inner, ps, m)
                with ExitStack() as inner:
                    sparse_attend(nc, c, inner, ps, m, yT)
        out_project(nc, c, ctx, ps, x, yT, w_out)


@stage
def load_x(nc, c, x, x_dram):
    x_in = c.sem("x_in")
    with nc.Block() as block:

        @block.sync
        def _(sp):
            sp.dma_start(x[:, :, :], x_dram.rearrange("(t p) d -> p t d", p=P)).then_inc(x_in, 16)
            sp.wait_ge(x_in, 16)


@stage
def final_norm(nc, c, x, gain, out_dram):
    with ExitStack() as ctx:
        g = c.sb("final_gain", [P, D], ctx=ctx)
        sq = c.sb("squares", [P, TT, D], ctx=ctx)
        ss = c.sb("ss", [P, 2 * TT], ctx=ctx)
        g_in, summed, root, own, ready, stored = (c.sem(n) for n in ("final_gain_in", "summed", "root", "dve_own",
                                                                     "out_ready", "out_stored"))
        with nc.Block() as block:

            @block.sync
            def _(sp):
                sp.dma_start(g[:, :], gain.rearrange("(o d) -> o d", o=1).to_broadcast([P, D])).then_inc(g_in, 16)
                for t in range(TT):
                    sp.wait_ge(ready, t + 1)
                    sp.dma_start(out_dram[t * P:(t + 1) * P, :], sq[:, t, :]).then_inc(stored, 16)
                sp.wait_ge(stored, 16 * TT)

            @block.scalar
            def _(act):
                for t in range(TT):
                    nc.scalar.activation(sq[:, t, :], x[:, t, :], ACT.Square,
                                         accum_out=ss[:, t:t + 1]).then_inc(summed, 1)
                act.wait_ge(summed, TT)
                nc.scalar.activation(ss[:, TT:2 * TT], ss[:, 0:TT], ACT.Sqrt, scale=1.0 / D,
                                     bias=c.eps[:, 0:1]).then_inc(root, 1)

            @block.vector
            def _(dve):
                link = chain(dve, own)
                dve.wait_ge(g_in, 16)
                dve.wait_ge(root, 1)
                link(nc.vector.reciprocal(ss[:, TT:2 * TT], ss[:, TT:2 * TT]))
                for t in range(TT):
                    nc.vector.scalar_tensor_tensor(out=sq[:, t, :], in0=x[:, t, :], scalar=ss[:, TT + t:TT + t + 1],
                                                   in1=g[:, :], op0=ALU.mult, op1=ALU.mult).then_inc(ready, 1)


def build(nc, a, out):
    with ExitStack() as ctx:
        c = Core(nc, ctx)
        x = c.sb("x", [P, TT, D])
        ps = [ctx.enter_context(nc.psum_tensor(f"ps{i}", [P, BANK], F32)) for i in range(8)]
        xrows = nc.dram_tensor("sorted_rows", [N_ROWS, D], F32).ap()
        yrows = nc.dram_tensor("expert_rows", [N_ROWS, D], F32).ap()
        load_x(nc, c, x, a["x"][0])
        constants(nc, c)
        prm = {n: a["a_" + n][0] for n in ("mu_lora", "mu_rkv", "w0", "w1", "w2", "a0", "a1", "a2", "g1", "g2",
                                           "k_k", "k_a", "ln_g", "ln_b")}
        prm["r_k"] = a["a_r_k"][0].rearrange("h d -> (h d)")
        prm.update({n: a["b_" + n][0] for n in ("kv_norm", "w_kv_up", "idx_k_norm")})
        for layer in range(a["moe_norm"].shape[0]):
            if layer % 2 == 0:
                even_mixer(nc, c, ps, x, a["ev_norm"][layer // 2], a["ev_w_in"][layer // 2],
                           a["ev_w_out"][layer // 2], prm)
            else:
                odd_mixer(nc, c, ps, x, a["od_norm"][layer // 2], a["od_w_qkv"][layer // 2],
                          a["od_w_out"][layer // 2])
            moe(nc, c, ps, x, xrows, yrows, a["moe_norm"][layer], a["moe_router_group"][layer],
                a["moe_router_expert"][layer], a["moe_w1"][layer], a["moe_w3"][layer], a["moe_w2"][layer])
        final_norm(nc, c, x, a["final_norm"], out[0])


_INS = ["x", "ev_norm", "ev_w_in", "ev_w_out", "a_mu_rkv", "a_mu_lora", "a_w0", "a_w1", "a_w2", "a_a0", "a_a1",
        "a_a2", "a_g1", "a_g2", "a_k_k", "a_k_a", "a_r_k", "a_ln_g", "a_ln_b", "b_kv_norm", "b_w_kv_up",
        "b_idx_k_norm", "od_norm", "od_w_qkv", "od_w_out", "moe_norm", "moe_router_group", "moe_router_expert",
        "moe_w1", "moe_w3", "moe_w2", "final_norm"]


def kernel(**inputs):
    import numpy as np
    import concourse.bacc as bacc
    from concourse.bass_utils import run_bass_kernel_spmd

    nc = bacc.Bacc("TRN2", target_bir_lowering=False, num_devices=1)
    arrays, args = {}, {}
    for name in _INS:
        arrays[f"in_{name}"] = np.ascontiguousarray(inputs[name])
        args[name] = nc.dram_tensor(f"in_{name}", arrays[f"in_{name}"].shape, F32, kind="ExternalInput").ap()
    shape = inputs["x"].shape
    out = nc.dram_tensor("out_x", shape, F32, kind="ExternalOutput").ap()
    build(nc, args, out)
    r = run_bass_kernel_spmd(nc, [arrays], core_ids=[0])
    return r.results[0]["out_x"]
```

```python
import math
from contextlib import ExitStack

import concourse.bass as bass
from concourse import mybir

F32 = mybir.dt.float32
I32 = mybir.dt.int32
F32R = mybir.dt.float32r
U32 = mybir.dt.uint32
ALU = mybir.AluOpType
ACT = mybir.ActivationFunctionType
AX = mybir.AxisListType

P = 128
BANK = 512
D = 1024
T = 512
TT = T // P
KD = D // P
HD = 64
RMS_EPS = 1e-6
NEG = -1e30
TAKEN = -3e38

N_EXP = 32
N_GRP = 4
EPG = N_EXP // N_GRP
FF = 512
KF = FF // P
MB = 64
N_ASG = 2 * T
N_ROWS = N_ASG + MB


class Core:

    def __init__(self, nc, ctx):
        self.nc, self.ctx, self.made, self.of_stage = nc, ctx, 0, []

    def sb(self, name, shape, dt=F32, ctx=None, side="left"):
        self.made += 1
        return (ctx or self.ctx).enter_context(self.nc.sbuf_tensor(f"{name}_{self.made}", shape, dt, side=side))

    def lasting_sem(self, name):
        self.made += 1
        return self.nc.alloc_semaphore(name=f"{name}_{self.made}")

    def sem(self, name):
        self.made += 1
        s = self.nc.alloc_semaphore(name=f"{name}_{self.made}")
        self.of_stage.append(s)
        return s

    def end_stage(self):
        if self.of_stage:
            self.nc.clear_and_free_semaphores(self.of_stage)
            self.nc.all_engine_barrier()
        self.of_stage = []


def stage(f):
    def run(nc, c, *args):
        f(nc, c, *args)
        c.end_stage()
    return run


def chain(eng, sem):
    done = [0]

    def link(ins):
        done[0] += 1
        ins.then_inc(sem, 1)
        eng.wait_ge(sem, done[0])

    return link


@stage
def constants(nc, c):
    c.ident = c.sb("ident", [P, P])
    c.ones = c.sb("ones", [P, P])
    c.tri = c.sb("tri", [P, P])
    c.half = c.sb("half", [P, P], mybir.dt.bfloat16)
    c.headones = c.sb("headones", [P, P])
    c.count32 = c.sb("count32", [P, N_EXP])
    c.eps = c.sb("eps", [P, 4])
    made = c.sem("const_made")
    with nc.Block() as block:

        @block.gpsimd
        def _(pool):
            link = chain(pool, made)
            link(nc.gpsimd.memset(c.ones[:, :], 1.0))
            link(nc.gpsimd.memset(c.ident[:, :], 0.0))
            link(nc.gpsimd.affine_select(out=c.ident[:, :], in_=c.ident[:, :], compare_op=ALU.not_equal,
                                         fill=1.0, base=0, pattern=[[-1, P]], channel_multiplier=1))
            link(nc.gpsimd.affine_select(out=c.tri[:, :], in_=c.ones[:, :], compare_op=ALU.is_gt,
                                         fill=0.0, base=0, pattern=[[1, P]], channel_multiplier=-1))
            link(nc.gpsimd.memset(c.half[:, :], 0.0))
            link(nc.gpsimd.memset(c.headones[:, :], 0.0))
            link(nc.gpsimd.memset(c.headones[0:HD, 0:HD], 1.0))
            link(nc.gpsimd.memset(c.headones[HD:P, HD:P], 1.0))
            link(nc.gpsimd.memset(c.eps[:, :], 0.0))
            link(nc.gpsimd.memset(c.eps[:, 0:1], RMS_EPS))
            link(nc.gpsimd.memset(c.eps[:, 1:2], 64e-5))
            link(nc.gpsimd.iota(c.count32[:, :], [[1, N_EXP]], base=0, channel_multiplier=0,
                                allow_small_or_imprecise_dtypes=True))


def rms_scale(nc, c, x, xn, ss, rstd, sem_ss, sem_std, block):

    @block.scalar
    def _(act):
        for t in range(TT):
            nc.scalar.activation(xn[:, t, :], x[:, t, :], ACT.Square,
                                 accum_out=ss[:, t:t + 1]).then_inc(sem_ss, 1)
        act.wait_ge(sem_ss, TT)
        nc.scalar.activation(ss[:, TT:2 * TT], ss[:, 0:TT], ACT.Sqrt, scale=1.0 / D,
                             bias=c.eps[:, 0:1]).then_inc(sem_std, 1)


def norm_transpose(nc, c, ctx, ps, block, x, xn, gain_dram, evacuate):
    g = c.sb("gain", [P, KD], ctx=ctx)
    ss = c.sb("ss", [P, 2 * TT], ctx=ctx)
    rstd = c.sb("rstd", [P, TT], ctx=ctx)
    gain_in, ss_done, std_done, dve_own = c.sem("gain_in"), c.sem("ss_done"), c.sem("std_done"), c.sem("dve_own")
    xn_done, turned = c.sem("xn_done"), c.sem("turned")

    @block.sync
    def _(sp):
        sp.dma_start(g[:, :], gain_dram.rearrange("(p k) -> p k", k=KD)).then_inc(gain_in, 16)

    rms_scale(nc, c, x, xn, ss, rstd, ss_done, std_done, block)

    @block.vector
    def _(dve):
        link = chain(dve, dve_own)
        dve.wait_ge(std_done, 1)
        link(nc.vector.reciprocal(rstd[:, :], ss[:, TT:2 * TT]))
        for t in range(TT):
            nc.vector.tensor_scalar(xn[:, t, :], x[:, t, :], rstd[:, t:t + 1], None,
                                    ALU.mult).then_inc(xn_done, 1)

    @block.tensor
    def _(pe):
        pe.wait_ge(xn_done, TT)
        for k in range(KD):
            for t in range(TT):
                last = nc.tensor.transpose(ps[k][:, t * P:(t + 1) * P], xn[:, t, k::KD], c.ident[:, :])
            last.then_inc(turned, 1)

    evacuate(block, g, gain_in, turned)


@stage
def moe_norm(nc, c, ctx, ps, x, xn, hT, gain_dram, ahead):

    def evacuate(block, g, gain_in, turned):

        @block.vector
        def _(dve):
            dve.wait_ge(gain_in, 16)
            for k in range(0, KD, 2):
                dve.wait_ge(turned, k + 1)
                nc.vector.tensor_scalar(hT[:, k, :], ps[k][:, :], g[:, k:k + 1], None, ALU.mult)

        @block.scalar
        def _(act):
            act.wait_ge(gain_in, 16)
            for k in range(1, KD, 2):
                act.wait_ge(turned, k + 1)
                nc.scalar.activation(hT[:, k, :], ps[k][:, :], ACT.Copy, scale=g[:, k:k + 1])

    with nc.Block() as block:
        norm_transpose(nc, c, ctx, ps, block, x, xn, gain_dram, evacuate)

        @block.sync
        def _(sp):
            ahead(sp)


@stage
def router(nc, c, ctx, ps, hT, xn, w_group, w_expert, xrows, r, ahead):
    wr = c.sb("w_router", [P, KD, N_GRP + N_EXP], ctx=ctx)
    NL = N_GRP + N_EXP
    lgT = c.sb("logitsT", [NL, T], ctx=ctx)
    lg = c.sb("logits", [P, TT, NL], ctx=ctx)
    g8 = c.sb("group8", [P, TT, 8], ctx=ctx)
    e8 = c.sb("expert8", [P, TT, EPG], ctx=ctx)
    best = c.sb("best", [P, 2, TT, 8], ctx=ctx)
    besti = c.sb("best_index", [P, 2, TT, 8], U32, ctx=ctx)
    bestf = c.sb("best_index_f", [P, 2, TT, 8], ctx=ctx)
    prod = c.sb("prod", [P, TT, N_EXP], ctx=ctx)
    small = c.sb("small", [P, 12, TT], ctx=ctx)
    gex = c.sb("group_exp", [P, TT, N_GRP], ctx=ctx)
    hot = c.sb("hot", [P, 3, TT, N_EXP], ctx=ctx)
    pos = c.sb("pos", [P, TT, N_EXP], ctx=ctx)
    tab = c.sb("tab", [P, 8, N_EXP], ctx=ctx)
    w_in, scattered = c.sem("router_w_in"), c.sem("rows_scattered")
    logitsT_done, logitsT_out, logits_done = c.sem("logitsT_done"), c.sem("logitsT_out"), c.sem("logits_done")
    own, sub_done, exp_done = c.sem("dve_own"), c.sem("sub_done"), c.sem("exp_done")
    hot_done, pos_done, dest_done = c.sem("hot_done"), c.sem("pos_done"), c.sem("dest_done")

    def col(t):
        return t[:, :, :]

    def wide(ap, n):
        return ap.rearrange("p (t o) -> p t o", o=1).to_broadcast([P, TT, n])

    with nc.Block() as block:

        @block.sync
        def _(sp):
            sp.dma_start(wr[:, :, 0:N_GRP], w_group.rearrange("(p k) n -> p k n", k=KD)).then_inc(w_in, 16)
            for g in range(N_GRP):
                lo = N_GRP + g * EPG
                sp.dma_start(wr[:, :, lo:lo + EPG],
                             w_expert[g].rearrange("(p k) n -> p k n", k=KD)).then_inc(w_in, 16)
            ahead(sp)

        @block.tensor
        def _(pe):
            pe.wait_ge(w_in, 16 * (1 + N_GRP))
            for k in range(KD):
                last = nc.tensor.matmul(ps[0][0:NL, :], wr[:, k, :], hT[:, k, :],
                                        start=k == 0, stop=k == KD - 1)
            last.then_inc(logitsT_done, 1)
            pe.wait_ge(logitsT_out, 1)
            for t in range(TT):
                last = nc.tensor.transpose(ps[1][:, t * NL:(t + 1) * NL], lgT[:, t * P:(t + 1) * P],
                                           c.ident[0:NL, 0:NL])
            last.then_inc(logits_done, 1)
            pe.wait_ge(hot_done, 1)
            nc.tensor.matmul(ps[2][:, 0:P], c.tri[:, :], hot[:, 2, :, :].rearrange("p t e -> p (t e)"),
                             start=True, stop=True)
            nc.tensor.matmul(ps[3][:, 0:P], c.ones[:, :], hot[:, 2, :, :].rearrange("p t e -> p (t e)"),
                             start=True, stop=True).then_inc(pos_done, 1)

        @block.scalar
        def _(act):
            act.wait_ge(sub_done, 1)
            nc.scalar.activation(gex[:, :, :], gex[:, :, :], ACT.Exp).then_inc(exp_done, 1)
            act.wait_ge(sub_done, 2)
            nc.scalar.activation(small[:, 3, :], small[:, 2, :], ACT.Exp).then_inc(exp_done, 1)

        @block.vector
        def _(dve):
            link = chain(dve, own)
            V = nc.vector
            link(V.memset(g8[:, :, :], NEG))
            dve.wait_ge(logitsT_done, 1)
            V.tensor_copy(lgT[:, :], ps[0][0:NL, :]).then_inc(logitsT_out, 1)
            dve.wait_ge(logits_done, 1)
            link(V.tensor_copy(lg[:, :, :], ps[1][:, 0:TT * NL].rearrange("p (t n) -> p t n", n=NL)))
            link(V.tensor_copy(g8[:, :, 0:N_GRP], lg[:, :, 0:N_GRP]))
            for t in range(TT):
                link(V.max(best[:, 0, t, :], g8[:, t, :]))
                link(V.max_index(besti[:, 0, t, :], best[:, 0, t, :], g8[:, t, :]))
            link(V.tensor_copy(bestf[:, 0, :, :], besti[:, 0, :, :]))
            V.tensor_tensor(gex[:, :, :], lg[:, :, 0:N_GRP], best[:, 0, :, 0:1].to_broadcast([P, TT, N_GRP]),
                            ALU.subtract).then_inc(sub_done, 1)
            link(V.tensor_tensor(pos[:, :, 0:N_GRP], c.count32[:, 0:N_GRP].rearrange("p (o g) -> p o g", o=1)
                                 .to_broadcast([P, TT, N_GRP]),
                                 bestf[:, 0, :, 0:1].to_broadcast([P, TT, N_GRP]), ALU.is_equal))
            for t in range(TT):
                link(V.tensor_tensor(prod[:, t, :].rearrange("p (g e) -> p g e", e=EPG),
                                     lg[:, t, N_GRP:NL].rearrange("p (g e) -> p g e", e=EPG),
                                     pos[:, t, 0:N_GRP].rearrange("p (g o) -> p g o", o=1)
                                     .to_broadcast([P, N_GRP, EPG]), ALU.mult))
                link(V.tensor_reduce(e8[:, t, :], prod[:, t, :].rearrange("p (g e) -> p e g", e=EPG), AX.X, ALU.add))
                link(V.max(best[:, 1, t, :], e8[:, t, :]))
                link(V.max_index(besti[:, 1, t, :], best[:, 1, t, :], e8[:, t, :]))
            link(V.tensor_copy(bestf[:, 1, :, :], besti[:, 1, :, :]))
            V.tensor_tensor(small[:, 2, :], best[:, 1, :, 1], best[:, 1, :, 0], ALU.subtract).then_inc(sub_done, 1)
            for j in range(2):
                link(V.scalar_tensor_tensor(out=small[:, 4 + j, :], in0=bestf[:, 0, :, 0], scalar=float(EPG),
                                            in1=bestf[:, 1, :, j], op0=ALU.mult, op1=ALU.add))
                link(V.tensor_tensor(hot[:, j, :, :], c.count32[:, :].rearrange("p (o e) -> p o e", o=1)
                                     .to_broadcast([P, TT, N_EXP]), wide(small[:, 4 + j, :], N_EXP), ALU.is_equal))
            V.tensor_tensor(hot[:, 2, :, :], hot[:, 0, :, :], hot[:, 1, :, :], ALU.add).then_inc(hot_done, 1)
            dve.wait_ge(exp_done, 2)
            link(V.tensor_reduce(small[:, 6, :], gex[:, :, :], AX.X, ALU.add))
            link(V.tensor_scalar(small[:, 7, :], small[:, 3, :], 1.0, None, ALU.add))
            link(V.tensor_tensor(small[:, 8, :], small[:, 6, :], small[:, 7, :], ALU.mult))
            link(V.reciprocal(r.gate[:, 0, :], small[:, 8, :]))
            link(V.tensor_tensor(r.gate[:, 1, :], r.gate[:, 0, :], small[:, 3, :], ALU.mult))
            dve.wait_ge(pos_done, 1)
            total = ps[3][:, 0:P].rearrange("p (t e) -> p t e", e=N_EXP)
            link(V.memset(tab[:, 0, :], 0.0))
            for t in range(TT):
                link(V.tensor_tensor(tab[:, t + 1, :], total[:, t, :], tab[:, t, :], ALU.add))
            link(V.tensor_tensor_scan(tab[:, 5, :], c.ones[:, 0:N_EXP], tab[:, TT, :], 0.0, ALU.mult, ALU.add))
            link(V.tensor_tensor(tab[:, 6, :], tab[:, 5, :], tab[:, TT, :], ALU.subtract))
            link(V.tensor_tensor(pos[:, :, :], ps[2][:, 0:P].rearrange("p (t e) -> p t e", e=N_EXP),
                                 tab[:, 0:TT, :], ALU.add))
            link(V.tensor_tensor(pos[:, :, :], pos[:, :, :], tab[:, 6:7, :].to_broadcast([P, TT, N_EXP]), ALU.add))
            for j in range(2):
                link(V.tensor_tensor(prod[:, :, :], pos[:, :, :], hot[:, j, :, :], ALU.mult))
                link(V.tensor_reduce(small[:, 9, :], prod[:, :, :], AX.X, ALU.add))
                last = V.tensor_copy(r.dest[:, j, :], small[:, 9, :])
                link(last) if j == 0 else last.then_inc(dest_done, 1)
            link(V.memset(tab[:, 7, :], 0.0))
            for b in range(1, T // MB):
                link(V.tensor_scalar(tab[:, 3, :], tab[:, TT, :], float(b * MB), None, ALU.is_gt))
                link(V.tensor_tensor(tab[:, 7, :], tab[:, 7, :], tab[:, 3, :], ALU.add))
            link(V.tensor_tensor_scan(tab[:, 0, :], c.ones[:, 0:N_EXP], tab[:, 7, :], 0.0, ALU.mult, ALU.add))
            link(V.tensor_tensor(tab[:, 1, :], tab[:, 0, :], tab[:, 7, :], ALU.subtract))
            link(V.tensor_copy(r.start[:, :], tab[0:1, 6, :]))
            link(V.tensor_copy(r.end[:, :], tab[0:1, 5, :]))
            link(V.tensor_copy(r.extra_before[:, :], tab[0:1, 1, :]))
            link(V.tensor_copy(r.extra_total[:, :], tab[0:1, 0, N_EXP - 1:N_EXP]))
            link(V.tensor_scalar(r.blocks[:, :], tab[0:1, 7, :], 1.0, None, ALU.add))

        @block.gpsimd
        def _(pool):
            pool.wait_ge(dest_done, 1)
            for j in range(2):
                for t in range(TT):
                    nc.gpsimd.indirect_dma_start(
                        out=xrows[0:N_ASG, :], out_offset=bass.IndirectOffsetOnAxis(ap=r.dest[:, j, t:t + 1], axis=0),
                        in_=xn[:, t, :], in_offset=None).then_inc(scattered, 16)
            pool.wait_ge(scattered, 16 * 2 * TT)


SLOTS = 3


class ExpertWeights:

    def __init__(self, c):
        self.c = c
        self.up_in = [c.lasting_sem(f"up_in{j}") for j in range(SLOTS)]
        self.down_in = [c.lasting_sem(f"down_in{j}") for j in range(SLOTS)]

    def start_layer(self, w1, w3, w2):
        self.w1_dram, self.w3_dram, self.w2_dram = w1, w3, w2
        self.w1, self.w3, self.w2 = [], [], []

    def add_slot(self, ctx):
        j = len(self.w1)
        self.w1.append(self.c.sb(f"w1_{j}", [P, KD, FF], ctx=ctx, side="right"))
        self.w3.append(self.c.sb(f"w3_{j}", [P, KD, FF], ctx=ctx, side="right"))
        self.w2.append(self.c.sb(f"w2_{j}", [P, KF, D], ctx=ctx, side="right"))

    def load_up(self, eng, j, e):
        eng.dma_start(self.w1[j][:, :, :], expert(self.w1_dram, e, KD)).then_inc(self.up_in[j], 16)
        eng.dma_start(self.w3[j][:, :, :], expert(self.w3_dram, e, KD)).then_inc(self.up_in[j], 16)

    def load_down(self, eng, j, e):
        eng.dma_start(self.w2[j][:, :, :], expert(self.w2_dram, e, KF)).then_inc(self.down_in[j], 16)

    def prefetch(self, slots):
        def issue(sp):
            for j in slots:
                self.load_up(sp, j, j)
                self.load_down(sp, j, j)
        return issue

    def end_layer(self, c):
        c.of_stage += self.up_in + self.down_in
        self.__init__(c)


def expert(w, e, k):
    return w[bass.ds(e, 1)].rearrange("o (p k) n -> p (o k) n", k=k)


@stage
def experts(nc, c, ctx, ps, xrows, yrows, r, gain_dram, wts):
    x_rows = [c.sb(f"x_rows{j}", [MB, D], ctx=ctx) for j in range(SLOTS)]
    y_sb = [c.sb(f"y_{j}", [P, FF], ctx=ctx) for j in range(SLOTS)]
    w1_sb, w3_sb, w2_sb, up_in, down_in = wts.w1, wts.w3, wts.w2, wts.up_in, wts.down_in
    xT = c.sb("xT", [P, KD, MB], ctx=ctx)
    gate_act = c.sb("gate_act", [MB, FF], ctx=ctx)
    hid = c.sb("hid", [MB, FF], ctx=ctx)
    hidT = c.sb("hidT", [P, KF, MB], ctx=ctx)
    g = c.sb("gain", [P, KD], ctx=ctx)
    ps_x, ps_1, ps_3, ps_h, ps_y0, ps_y1 = ps[0], ps[1], ps[2], ps[3], ps[4], ps[5]

    gain_in = c.sem("gain_in")
    rows_in = [c.sem(f"rows_in{j}") for j in range(SLOTS)]
    stored = [c.sem(f"stored{j}") for j in range(SLOTS)]
    xT_done, xT_out = c.sem("xT_done"), c.sem("xT_out")
    up_done, silu_done, hid_done = c.sem("up_done"), c.sem("silu_done"), c.sem("hid_done")
    hidT_done, hidT_out = c.sem("hidT_done"), c.sem("hidT_out")
    down_done, y0_out, y1_out = c.sem("down_done"), c.sem("y0_out"), c.sem("y1_out")

    def load(sp, j, n, e, row, wait=True):
        if wait:
            sp.wait_ge(xT_done, n - SLOTS + 1)
        sp.dma_start(x_rows[j][:, :], xrows[bass.ds(row, MB), :]).then_inc(rows_in[j], 16)
        if wait:
            sp.wait_ge(up_done, n - SLOTS + 1)
        wts.load_up(sp, j, e)
        if wait:
            sp.wait_ge(down_done, n - SLOTS + 1)
        wts.load_down(sp, j, e)

    def pe_step(pe, j, n, u):
        pe.wait_ge(rows_in[j], 16 * u + 16)
        nc.tensor.ldweights(c.half[:, :], tile_position=(0, 0))
        for k in range(KD):
            last = nc.tensor.transpose(ps_x[:, k * MB:(k + 1) * MB], x_rows[j][:, k::KD], c.ident[0:MB, 0:MB])
        last.then_inc(xT_done, 1)
        pe.wait_ge(xT_out, n + 1)
        pe.wait_ge(up_in[j], 32 * u + 32)
        for k in range(KD):
            nc.tensor.matmul(ps_1[0:MB, :], xT[:, k, :], w1_sb[j][:, k, :], start=k == 0, stop=k == KD - 1)
            last = nc.tensor.matmul(ps_3[MB:P, :], xT[:, k, :], w3_sb[j][:, k, :], start=k == 0, stop=k == KD - 1)
        last.then_inc(up_done, 1)
        pe.wait_ge(hid_done, n + 1)
        nc.tensor.ldweights(c.half[:, :], tile_position=(0, 0))
        for k in range(KF):
            last = nc.tensor.transpose(ps_h[:, k * MB:(k + 1) * MB], hid[:, k::KF], c.ident[0:MB, 0:MB])
        last.then_inc(hidT_done, 1)
        pe.wait_ge(hidT_out, n + 1)
        pe.wait_ge(down_in[j], 16 * u + 16)
        pe.wait_ge(y0_out, n + 1)
        pe.wait_ge(y1_out, n + 1)
        for k in range(KF):
            nc.tensor.matmul(ps_y0[0:MB, :], hidT[:, k, :], w2_sb[j][:, k, 0:FF], start=k == 0, stop=k == KF - 1)
            last = nc.tensor.matmul(ps_y1[MB:P, :], hidT[:, k, :], w2_sb[j][:, k, FF:D], start=k == 0, stop=k == KF - 1)
        last.then_inc(down_done, 1)

    def dve_step(dve, j, n, u):
        dve.wait_ge(xT_done, n + 1)
        nc.vector.tensor_tensor(xT[:, :, :], ps_x[:, :].rearrange("p (k m) -> p k m", m=MB),
                                g[:, :].rearrange("p (k o) -> p k o", o=1).to_broadcast([P, KD, MB]),
                                ALU.mult).then_inc(xT_out, 1)
        dve.wait_ge(silu_done, n + 1)
        nc.vector.tensor_tensor(hid[:, :], gate_act[:, :], ps_3[MB:P, :], ALU.mult).then_inc(hid_done, 1)
        dve.wait_ge(down_done, n + 1)
        dve.wait_ge(stored[j], 32 * u + 32)
        nc.vector.tensor_copy(y_sb[j][MB:P, :], ps_y1[MB:P, :]).then_inc(y1_out, 1)

    def act_step(act, j, n, u, row, before):
        act.wait_ge(up_done, n + 1)
        nc.scalar.activation(gate_act[:, :], ps_1[0:MB, :], ACT.Silu).then_inc(silu_done, 1)
        act.wait_ge(hidT_done, n + 1)
        nc.scalar.activation(hidT[:, :, :], ps_h[:, 0:KF * MB].rearrange("p (k m) -> p k m", m=MB),
                             ACT.Copy).then_inc(hidT_out, 1)
        act.wait_ge(down_done, n + 1)
        act.wait_ge(stored[j], 32 * u + 32)
        nc.scalar.activation(y_sb[j][0:MB, :], ps_y0[0:MB, :], ACT.Copy).then_inc(y0_out, 1)
        act.wait_ge(y0_out, n + 2)
        act.wait_ge(y1_out, n + 2)
        before(act)
        for h in range(2):
            act.dma_start(yrows[bass.ds(row, MB), h * FF:(h + 1) * FF],
                          y_sb[j][h * MB:(h + 1) * MB, :]).then_inc(stored[j], 16)

    ROUNDS = N_EXP // SLOTS
    LEFT = N_EXP - ROUNDS * SLOTS
    XSLOT = LEFT
    XUSES = ROUNDS

    def steps(eng, step, first=0):
        with eng.Fori(first, ROUNDS) as i:
            for j in range(SLOTS):
                step(j, SLOTS * i + j, i)
        for j in range(LEFT):
            step(j, SLOTS * ROUNDS + j, ROUNDS)

    def further(eng, step):
        more = eng.value_load(r.extra_total[0:1, 0:1], min_val=0, max_val=N_ASG // MB)
        with eng.If(more > 0):
            with eng.Fori(0, N_EXP) as e:
                blocks = eng.value_load(r.blocks[0:1, bass.ds(e, 1)], min_val=1, max_val=T // MB)
                done = eng.value_load(r.extra_before[0:1, bass.ds(e, 1)], min_val=0, max_val=N_ASG // MB)
                with eng.If(blocks > 1):
                    end = eng.value_load(r.end[0:1, bass.ds(e, 1)], min_val=MB, max_val=N_ASG)
                    with eng.Fori(1, blocks) as b:
                        step(e, eng.snap(done + b - 1), nc.s_assert_within(eng.snap(end - b * MB), 0, N_ASG - MB, skip_runtime_bounds_check_because="further blocks lie inside the expert's rows"))
                eng.nop()
            eng.nop()
        eng.nop()

    def row_of(eng, e):
        return eng.value_load(r.start[0:1, bass.ds(e, 1)], min_val=0, max_val=N_ASG)

    with nc.Block() as block:

        @block.sync
        def _(sp):
            sp.dma_start(g[:, :], gain_dram.rearrange("(p k) -> p k", k=KD)).then_inc(gain_in, 16)
            for j in range(SLOTS):
                sp.dma_start(x_rows[j][:, :], xrows[bass.ds(row_of(sp, j), MB), :]).then_inc(rows_in[j], 16)
            steps(sp, lambda j, n, i: load(sp, j, n, n, row_of(sp, n)), first=1)

            def more(e, m, row):
                sp.wait_ge(down_done, m + N_EXP)
                load(sp, XSLOT, None, e, row, wait=False)

            further(sp, more)

        @block.tensor
        def _(pe):
            pe.wait_ge(gain_in, 16)
            steps(pe, lambda j, n, i: pe_step(pe, j, n, i))
            further(pe, lambda e, m, row: pe_step(pe, XSLOT, m + N_EXP, m + XUSES))

        @block.vector
        def _(dve):
            dve.wait_ge(gain_in, 16)
            dve.sem_inc(y1_out, 1)
            steps(dve, lambda j, n, i: dve_step(dve, j, n, i))
            further(dve, lambda e, m, row: dve_step(dve, XSLOT, m + N_EXP, m + XUSES))

        @block.scalar
        def _(act):
            act.sem_inc(y0_out, 1)
            for s in stored:
                act.sem_inc(s, 32)

            def step(j, n, i):
                uses = i + 1 if j else i
                act_step(act, j, n, i, row_of(act, n),
                         lambda a: a.wait_ge(stored[(j - 1) % SLOTS], 32 * uses + 32))

            steps(act, step)

            def more(e, m, row):
                act_step(act, XSLOT, m + N_EXP, m + XUSES, row,
                         lambda a: a.wait_ge(stored[(XSLOT - 1) % SLOTS], 32 * XUSES + 64))
                act.wait_ge(stored[XSLOT], 32 * m + 32 * XUSES + 64)

            further(act, more)
            for j in range(SLOTS):
                act.wait_ge(stored[j], 32 * (ROUNDS + (j < LEFT)) + 32)


@stage
def combine(nc, c, ctx, x, yrows, r):
    got = c.sb("got", [P, 2, TT, D], ctx=ctx)
    gathered = [[c.sem(f"gathered{j}{t}") for t in range(TT)] for j in range(2)]
    own = c.sem("dve_own")
    with nc.Block() as block:

        @block.gpsimd
        def _(pool):
            for t in range(TT):
                for j in range(2):
                    nc.gpsimd.indirect_dma_start(
                        out=got[:, j, t, :], out_offset=None, in_=yrows[0:N_ASG, :],
                        in_offset=bass.IndirectOffsetOnAxis(ap=r.dest[:, j, t:t + 1], axis=0)
                    ).then_inc(gathered[j][t], 16)

        @block.vector
        def _(dve):
            link = chain(dve, own)
            for t in range(TT):
                for j in range(2):
                    dve.wait_ge(gathered[j][t], 16)
                    link(nc.vector.scalar_tensor_tensor(out=x[:, t, :], in0=got[:, j, t, :],
                                                        scalar=r.gate[:, j, t:t + 1], in1=x[:, t, :],
                                                        op0=ALU.mult, op1=ALU.add))


class Routes:

    def __init__(self, c, ctx):
        self.gate = c.sb("gate", [P, 2, TT], ctx=ctx)
        self.dest = c.sb("dest", [P, 2, TT], U32, ctx=ctx)
        self.start = c.sb("start", [1, N_EXP], I32, ctx=ctx)
        self.end = c.sb("end", [1, N_EXP], I32, ctx=ctx)
        self.blocks = c.sb("blocks", [1, N_EXP], I32, ctx=ctx)
        self.extra_before = c.sb("extra_before", [1, N_EXP], I32, ctx=ctx)
        self.extra_total = c.sb("extra_total", [1, 1], I32, ctx=ctx)


def moe(nc, c, ps, x, xrows, yrows, gain, w_group, w_expert, wts, slots):
    with ExitStack() as outer:
        r = Routes(c, outer)
        with ExitStack() as ctx:
            xn = c.sb("xn", [P, TT, D], ctx=ctx)
            hT = c.sb("hT", [P, KD, T], ctx=ctx)
            wts.add_slot(slots)
            moe_norm(nc, c, ctx, ps, x, xn, hT, gain, wts.prefetch([SLOTS - 1]))
            router(nc, c, ctx, ps, hT, xn, w_group, w_expert, xrows, r, lambda sp: None)
        with ExitStack() as ctx:
            experts(nc, c, ctx, ps, xrows, yrows, r, gain, wts)
            wts.end_layer(c)
        slots.close()
        with ExitStack() as ctx:
            combine(nc, c, ctx, x, yrows, r)


class Bank:

    def __init__(self, ps, filled, emptied):
        self.ps, self.filled, self.emptied, self.n = ps, filled, emptied, 0

    def open(self, pe):
        if self.n:
            pe.wait_ge(self.emptied, self.n)
        return self.ps

    def close(self, last):
        last.then_inc(self.filled, 1)
        self.n += 1

    def copied(self, pe):
        pe.wait_ge(self.emptied, self.n)

    def read(self, eng):
        self.n += 1
        eng.wait_ge(self.filled, self.n)
        return self.ps

    def empty(self, ins):
        ins.then_inc(self.emptied, 1)


def bank_sems(c, what):
    return [(c.sem(f"{what}_filled{b}"), c.sem(f"{what}_emptied{b}")) for b in range(8)]


def bank_set(ps, sems):
    return [Bank(ps[b], *sems[b]) for b in range(8)]


@stage
def out_project(nc, c, ctx, ps, x, yT, w_dram, ahead):
    w = c.sb("w_out", [P, KD, D], ctx=ctx)
    w_in = [c.sem(f"w_out_in{f}") for f in range(2)]
    done = c.sem("out_done")
    with nc.Block() as block:

        @block.sync
        def _(sp):
            for h in range(2):
                sp.dma_start(w[:, :, h * BANK:(h + 1) * BANK],
                             w_dram.rearrange("(f p) n -> p f n", p=P)[:, :, h * BANK:(h + 1) * BANK]
                             ).then_inc(w_in[h], 16)
            ahead(sp)

        @block.tensor
        def _(pe):
            for h in range(2):
                pe.wait_ge(w_in[h], 16)
                for t in range(TT):
                    for f in range(KD):
                        last = nc.tensor.matmul(ps[h * TT + t][:, :], yT[:, f, t * P:(t + 1) * P],
                                                w[:, f, h * BANK:(h + 1) * BANK], start=f == 0, stop=f == KD - 1)
                    last.then_inc(done, 1)

        @block.vector
        def _(dve):
            for h in range(2):
                for t in range(TT):
                    dve.wait_ge(done, h * TT + t + 1)
                    xs = x[:, t, h * BANK:(h + 1) * BANK]
                    nc.vector.tensor_tensor(xs, ps[h * TT + t][:, :], xs, ALU.add)


HIGH_BITS = -4096
GC = 256


class SplitNorm:

    def __init__(self, c, ctx, scratch):
        self.c = c
        self.high, self.low = (c.sb(n, [P, KD, T + 1], F32R, ctx=ctx) for n in ("hT_high", "hT_low"))
        self.full = [c.sb(f"hT_full{i}", [P, T], ctx=scratch) for i in range(2)]
        self.cut = [c.sb(f"hT_cut{i}", [P, T], ctx=scratch) for i in range(2)]
        self.evacuated, self.masked = c.sem("hT_evacuated"), c.sem("hT_masked")
        self.high_done, self.low_done, self.edge = c.sem("hT_high_done"), c.sem("hT_low_done"), c.sem("hT_edge")

    def ready(self, pe, k):
        pe.wait_ge(self.edge, 2)
        pe.wait_ge(self.high_done, k + 1)
        pe.wait_ge(self.low_done, k + 1)

    def evacuate(self, nc, ps):
        def add(block, g, gain_in, turned):

            @block.scalar
            def _(act):
                act.wait_ge(gain_in, 16)
                for k in range(KD + 1):
                    if k < KD:
                        act.wait_ge(turned, k + 1)
                        if k >= 2:
                            act.wait_ge(self.low_done, k - 1)
                        nc.scalar.activation(self.full[k % 2][:, :], ps[k][:, :], ACT.Copy,
                                             scale=g[:, k:k + 1]).then_inc(self.evacuated, 1)
                    if k >= 1:
                        act.wait_ge(self.masked, k)
                        nc.scalar.activation(self.high[:, k - 1, 1:T + 1], self.cut[(k - 1) % 2][:, :],
                                             ACT.Copy).then_inc(self.high_done, 1)

            @block.vector
            def _(dve):
                for half in (self.high, self.low):
                    nc.vector.tensor_scalar(half[:, :, 0:1].rearrange("p k o -> p (k o)"), c_zero(self.c), 0.0, None,
                                            ALU.mult).then_inc(self.edge, 1)
                for k in range(KD):
                    dve.wait_ge(self.evacuated, k + 1)
                    if k >= 2:
                        dve.wait_ge(self.high_done, k - 1)
                        dve.wait_ge(self.low_done, k - 1)
                    nc.vector.tensor_scalar(self.cut[k % 2][:, :].bitcast(I32), self.full[k % 2][:, :].bitcast(I32),
                                            HIGH_BITS, None, ALU.bitwise_and).then_inc(self.masked, 1)
                    dve.wait_ge(self.masked, k + 1)
                    nc.vector.tensor_tensor(self.low[:, k, 1:T + 1], self.full[k % 2][:, :], self.cut[k % 2][:, :],
                                            ALU.subtract).then_inc(self.low_done, 1)

        return add


def c_zero(c):
    return c.ident[:, 0:KD]


class SplitWeights:
    RAW = 3

    def __init__(self, nc, c, ctx, width=GC):
        self.nc = nc
        self.raw = [c.sb(f"w_raw{i}", [P, KD, width], ctx=ctx) for i in range(self.RAW)]
        self.cut = c.sb("w_cut", [P, KD, width], ctx=ctx)
        self.high = [c.sb(f"w_high{i}", [P, KD, width], F32R, ctx=ctx) for i in range(2)]
        self.low = [c.sb(f"w_low{i}", [P, KD, width], F32R, ctx=ctx) for i in range(2)]
        self.raw_in = [c.sem(f"w_raw_in{i}") for i in range(self.RAW)]
        self.masked, self.high_done, self.low_done, self.used = (
            c.sem(n) for n in ("w_masked", "w_high_done", "w_low_done", "w_used"))

    def load(self, sp, g, pieces):
        if g >= self.RAW:
            sp.wait_ge(self.low_done, g - self.RAW + 1)
        for lo, view in pieces:
            n = view.shape[-1]
            sp.dma_start(self.raw[g % self.RAW][:, :, lo:lo + n], view).then_inc(self.raw_in[g % self.RAW], 16)

    def split_low(self, dve, g, n, arrived):
        raw = self.raw[g % self.RAW]
        dve.wait_ge(self.raw_in[g % self.RAW], 16 * arrived)
        if g >= 1:
            dve.wait_ge(self.high_done, g)
            dve.wait_ge(self.low_done, g)
        self.nc.vector.tensor_scalar(self.cut[:, :, 0:n].bitcast(I32), raw[:, :, 0:n].bitcast(I32), HIGH_BITS, None,
                                     ALU.bitwise_and).then_inc(self.masked, 1)
        dve.wait_ge(self.masked, g + 1)
        if g >= 2:
            dve.wait_ge(self.used, g - 1)
        self.nc.vector.tensor_tensor(self.low[g % 2][:, :, 0:n], raw[:, :, 0:n], self.cut[:, :, 0:n],
                                     ALU.subtract).then_inc(self.low_done, 1)

    def split_high(self, act, g, n):
        act.wait_ge(self.masked, g + 1)
        if g >= 2:
            act.wait_ge(self.used, g - 1)
        self.nc.scalar.activation(self.high[g % 2][:, :, 0:n], self.cut[:, :, 0:n],
                                  ACT.Copy).then_inc(self.high_done, 1)

    def ready(self, pe, g):
        pe.wait_ge(self.high_done, g + 1)
        pe.wait_ge(self.low_done, g + 1)

    def release(self, pe, last_bank):
        pe.wait_ge(last_bank.filled, last_bank.n)
        pe.sem_inc(self.used, 1)


def three_passes(nc, out, lhsT, rhs, start, stop):
    nc.tensor.matmul(out, lhsT[0], rhs[0], start=start, stop=False)
    nc.tensor.matmul(out, lhsT[0], rhs[1], start=False, stop=False)
    return nc.tensor.matmul(out, lhsT[1], rhs[0], start=False, stop=stop)


C_HEADS = 16
LAG_T, LAG_PV = 3, 4


@stage
def odd_project(nc, c, ctx, ps, x, xn, gain_dram, w_dram, qT, kT, v):
    NG = 3 * D // GC
    FG = GC // P
    hT = SplitNorm(c, ctx, ctx)
    w = SplitWeights(nc, c, ctx)
    sems = bank_sems(c, "qkv")
    is_v = lambda g: g >= 2 * D // GC
    outs = [(g, s) for g in range(NG) for s in range(TT if is_v(g) else FG)]

    def dest(g, s):
        if is_v(g):
            lo = g * GC - 2 * D
            return v[:, s, lo:lo + GC]
        f = FG * g + s
        return qT[:, f, :] if f < KD else kT[:, f - KD, :]

    def width(g):
        return GC if is_v(g) else T

    def empty_and_split(eng, parity, copy, split):
        banks = bank_set(ps, sems)
        split(0)
        split(1)
        for n, (g, s) in enumerate(outs):
            if n % 2 == parity:
                b = banks[n % 8]
                b.empty(copy(dest(g, s), b.read(eng)[:, 0:width(g)], HD ** -0.5 if g < D // GC else 1.0))
            if n + 1 < len(outs) and outs[n + 1][0] != g and g + 2 < NG:
                split(g + 2)

    with nc.Block() as block:
        norm_transpose(nc, c, ctx, ps, block, x, xn, gain_dram, hT.evacuate(nc, ps))

        @block.sync
        def _(sp):
            for g in range(NG):
                w.load(sp, g, [(0, w_dram.rearrange("(p k) n -> p k n", k=KD)[:, :, g * GC:(g + 1) * GC])])

        @block.tensor
        def _(pe):
            banks = bank_set(ps, sems)
            for n, (g, s) in enumerate(outs):
                if s == 0:
                    w.ready(pe, g)
                b = banks[n % 8]
                out = b.open(pe)
                for k in range(KD):
                    if n == 0:
                        hT.ready(pe, k)
                    wk = [h[g % 2][:, k, :] for h in (w.high, w.low)]
                    if is_v(g):
                        xk = [h[:, k, 1 + s * P:1 + (s + 1) * P] for h in (hT.high, hT.low)]
                        last = three_passes(nc, out[:, 0:GC], xk, wk, k == 0, k == KD - 1)
                    else:
                        xk = [h[:, k, 1:T + 1] for h in (hT.high, hT.low)]
                        last = three_passes(nc, out[:, :], [h[:, s * P:(s + 1) * P] for h in wk], xk,
                                            k == 0, k == KD - 1)
                b.close(last)
                if n + 1 == len(outs) or outs[n + 1][0] != g:
                    w.release(pe, b)

        @block.vector
        def _(dve):
            empty_and_split(dve, 0, lambda out, in_, scale: nc.vector.tensor_scalar(out, in_, scale, None, ALU.mult),
                            lambda g: w.split_low(dve, g, GC, g // w.RAW + 1))

        @block.scalar
        def _(act):
            empty_and_split(act, 1, lambda out, in_, scale: nc.scalar.activation(out, in_, ACT.Copy, scale=scale),
                            lambda g: w.split_high(act, g, GC))


@stage
def stick_breaking(nc, c, ctx, ps, qT, kT, v, yT):
    units = [(h, t) for h in range(C_HEADS) for t in range(TT)]
    N = len(units)
    keep = [c.sb(f"keep{i}", [P, T], ctx=ctx) for i in range(4)]
    beta = [c.sb(f"beta{i}", [P, T], ctx=ctx) for i in range(4)]
    tail = [c.sb(f"tail{t}", [P, T + 1], ctx=ctx) for t in range(TT)]
    wT = [c.sb(f"wT{i}", [P, T], ctx=ctx) for i in range(2)]
    zero = c.sb("zero", [P, T], ctx=ctx)
    z_done, beta_done, masked = c.sem("z_done"), c.sem("beta_done"), c.sem("masked")
    scanned, weighted = c.sem("scanned"), c.sem("weighted")
    turned, wT_out, pv_done, y_out, ready = (c.sem("turned"), c.sem("wT_out"), c.sem("pv_done"),
                                             c.sem("y_out"), c.sem("stick_ready"))
    ps_z, ps_t, ps_y = ps[0:3], ps[3:5], ps[5:7]

    with nc.Block() as block:

        @block.tensor
        def _(pe):
            def scores(u):
                h, t = units[u]
                q = HD * (h % 2)
                if u >= 3:
                    pe.wait_ge(beta_done, 2 * (u - 3) + 2)
                nc.tensor.matmul(ps_z[u % 3][:, 0:(t + 1) * P], qT[q:q + HD, h // 2, t * P:(t + 1) * P],
                                 kT[q:q + HD, h // 2, 0:(t + 1) * P], start=True, stop=True).then_inc(z_done, 1)

            def turn(u):
                h, t = units[u]
                pe.wait_ge(weighted, u + 1)
                if u >= 2:
                    pe.wait_ge(wT_out, u - 1)
                for b in range(t + 1):
                    last = nc.tensor.transpose(ps_t[u % 2][:, b * P:(b + 1) * P], beta[u % 4][:, b * P:(b + 1) * P],
                                               c.ident[:, :])
                last.then_inc(turned, 1)

            def weigh(u):
                h, t = units[u]
                q = HD * (h % 2)
                pair = h // 2
                pe.wait_ge(wT_out, u + 1)
                if h % 2 == 0 and t == 0 and pair >= 2:
                    pe.wait_ge(y_out, pair - 1)
                for b in range(t + 1):
                    last = nc.tensor.matmul(ps_y[pair % 2][q:q + HD, t * P:(t + 1) * P],
                                            v[:, b, h * HD:(h + 1) * HD], wT[u % 2][:, b * P:(b + 1) * P],
                                            start=b == 0, stop=b == t)
                last.then_inc(pv_done, 1)

            for i in range(N + LAG_PV):
                if i < N:
                    scores(i)
                if 0 <= i - LAG_T < N:
                    turn(i - LAG_T)
                if 0 <= i - LAG_PV < N:
                    weigh(i - LAG_PV)

        @block.scalar
        def _(act):
            for i in range(N + LAG_T):
                if i < N:
                    h, t = units[i]
                    L = (t + 1) * P
                    act.wait_ge(z_done, i + 1)
                    if i >= 4:
                        act.wait_ge(scanned, i - 3)
                        act.wait_ge(turned, i - 3)
                    nc.scalar.activation(keep[i % 4][:, 0:L], ps_z[i % 3][:, 0:L], ACT.Sigmoid,
                                         scale=-1.0).then_inc(beta_done, 1)
                    nc.scalar.activation(beta[i % 4][:, 0:L], ps_z[i % 3][:, 0:L],
                                         ACT.Sigmoid).then_inc(beta_done, 1)
                u = i - LAG_T
                if u >= 0:
                    L = (units[u][1] + 1) * P
                    act.wait_ge(turned, u + 1)
                    if u >= 2:
                        act.wait_ge(pv_done, u - 1)
                    nc.scalar.activation(wT[u % 2][:, 0:L], ps_t[u % 2][:, 0:L], ACT.Copy).then_inc(wT_out, 1)

        @block.gpsimd
        def _(pool):
            for i, (h, t) in enumerate(units):
                pool.wait_ge(beta_done, 2 * i + 2)
                lo, hi = t * P, (t + 1) * P
                for buf, fill in ((keep, 1.0), (beta, 0.0)):
                    last = nc.gpsimd.affine_select(out=buf[i % 4][:, lo:hi], in_=buf[i % 4][:, lo:hi],
                                                   compare_op=ALU.is_gt, fill=fill, base=0, pattern=[[-1, P]],
                                                   channel_multiplier=1)
                last.then_inc(masked, 1)

        @block.vector
        def _(dve):
            nc.vector.memset(zero[:, :], 0.0).then_inc(ready, 1)
            for t in range(TT):
                L = (t + 1) * P
                nc.vector.memset(tail[t][:, L:L + 1], 1.0).then_inc(ready, 1)
            dve.wait_ge(ready, 1 + TT)
            for i, (h, t) in enumerate(units):
                L = (t + 1) * P
                dve.wait_ge(masked, i + 1)
                if i >= 4:
                    dve.wait_ge(weighted, i - 3)
                nc.vector.tensor_tensor_scan(tail[t][:, 0:L][:, ::-1],
                                             keep[i % 4][:, 0:L][:, ::-1], zero[:, 0:L], 1.0,
                                             ALU.mult, ALU.add).then_inc(scanned, 1)
                dve.wait_ge(scanned, i + 1)
                nc.vector.tensor_tensor(beta[i % 4][:, 0:L], beta[i % 4][:, 0:L], tail[t][:, 1:L + 1],
                                        ALU.mult).then_inc(weighted, 1)
                if h % 2 == 1 and t == 1 and h >= 3:
                    pair = h // 2 - 1
                    dve.wait_ge(pv_done, 8 * (pair + 1))
                    nc.vector.tensor_copy(yT[:, pair, :], ps_y[pair % 2][:, :]).then_inc(y_out, 1)
            pair = C_HEADS // 2 - 1
            dve.wait_ge(pv_done, N)
            nc.vector.tensor_copy(yT[:, pair, :], ps_y[pair % 2][:, :]).then_inc(y_out, 1)


def odd_mixer(nc, c, ps, x, gain, w_qkv, w_out, wts, slots):
    with ExitStack() as ctx:
        yT = c.sb("yT", [P, KD, T], ctx=ctx)
        with ExitStack() as inner:
            qT = c.sb("qT", [P, KD, T], ctx=inner)
            kT = c.sb("kT", [P, KD, T], ctx=inner)
            v = c.sb("v", [P, TT, D], ctx=inner)
            with ExitStack() as proj:
                xn = c.sb("xn", [P, TT, D], ctx=proj)
                odd_project(nc, c, proj, ps, x, xn, gain, w_qkv, qT, kT, v)
            stick_breaking(nc, c, inner, ps, qT, kT, v, yT)
        for _ in range(SLOTS - 1):
            wts.add_slot(slots)
        out_project(nc, c, ctx, ps, x, yT, w_out, wts.prefetch(range(SLOTS - 1)))


A_HEADS, A_WIDTH = 8, 512
B_HEADS, B_WIDTH = 8, 512
KV_RANK = 128
IDX_HEADS = 8
TOPK = min(256, T // 4)
FT = A_WIDTH // P
CH = 64
NCH = T // CH
DECAY = math.exp(-0.5)
COLS = dict(r=0, k=512, v=1024, qb=1536, ckv=2048, qi=2176, ki=2688, wi=2752)


@stage
def even_project(nc, c, ctx, ps, x, xn, gain_dram, w_dram, m, prm):
    hT = SplitNorm(c, ctx, ctx)
    w = SplitWeights(nc, c, ctx)
    mu = c.sb("mu_lora", [P, 3, KD], ctx=ctx)
    less = c.sb("one_less_mu", [P, 3, FT], ctx=ctx)
    raw = [xn[:, i, 0:T + 1] for i in range(2)]
    own, prm_in = c.sem("dve_own"), c.sem("prm_in")
    raw_out, raw_read, raw_zero = c.sem("raw_out"), c.sem("raw_read"), c.sem("raw_zero")
    sems = bank_sems(c, "proj")

    def columns(name, width):
        return [(name, i * GC, GC, [P] * (GC // P)) for i in range(width // GC)]

    groups = (columns("r", A_WIDTH) + columns("k", A_WIDTH) + columns("v", A_WIDTH) + columns("qb", B_WIDTH)
              + columns("qi", IDX_HEADS * HD) + [("misc", 0, GC, [P, P]), ("wi", 0, IDX_HEADS, [IDX_HEADS]),
                                                 ("da", 0, GC, [P]), ("gate", 0, GC, [P])])
    NG = len(groups)
    wv = w_dram.rearrange("(p k) n -> p k n", k=KD)
    wide = lambda ap: ap.rearrange("(p k) n -> p k n", k=KD)

    def pieces(g):
        name, lo, n, _ = groups[g]
        if name == "misc":
            ki = wv[:, :, COLS["ki"]:COLS["ki"] + HD]
            return [(0, wv[:, :, COLS["ckv"]:COLS["ckv"] + KV_RANK]), (P, ki), (P + HD, ki)]
        if name == "da":
            return [(0, wide(prm["w1"])), (HD, wide(prm["a1"]))]
        if name == "gate":
            return [(0, wide(prm["g1"]))]
        return [(0, wv[:, :, COLS[name] + lo:COLS[name] + lo + n])]

    def arrived(g):
        return sum(len(pieces(i)) for i in range(g % w.RAW, g + 1, w.RAW))

    with nc.Block() as block:
        norm_transpose(nc, c, ctx, ps, block, x, xn, gain_dram, hT.evacuate(nc, ps))

        @block.sync
        def _(sp):
            for g in range(NG):
                w.load(sp, g, pieces(g))
                if g == 2:
                    sp.dma_start(mu[:, :, :], prm["mu_lora"].rearrange("m (p k) -> p m k", k=KD)).then_inc(prm_in, 16)
                    for i in range(3):
                        sp.dma_start(m.mu[:, i, :], prm["mu_rkv"][i].rearrange("(f p) -> p f", p=P),
                                     allow_slow_non_contiguous=True).then_inc(prm_in, 16)

        @block.tensor
        def _(pe):
            banks = bank_set(ps, sems)
            n = 0
            for g, (name, _, _, tiles) in enumerate(groups):
                w.ready(pe, g)
                for f, rows in enumerate(tiles):
                    b = banks[n % 8]
                    out = b.open(pe)
                    shifts = 2 if name in ("da", "gate") else 1
                    for s in range(shifts):
                        lo = (f + s) * P
                        for k in range(KD):
                            if n == 0:
                                hT.ready(pe, k)
                            last = three_passes(nc, out[0:rows, :],
                                                [h[g % 2][:, k, lo:lo + rows] for h in (w.high, w.low)],
                                                [h[:, k, 1 - s:T + 1 - s] for h in (hT.high, hT.low)],
                                                s == 0 and k == 0, s == shifts - 1 and k == KD - 1)
                    b.close(last)
                    n += 1
                w.release(pe, b)

        @block.scalar
        def _(act):
            banks = bank_set(ps, sems)
            jobs = [0]

            def take():
                b = banks[jobs[0] % 8]
                jobs[0] += 1
                return b, b.read(act)

            def plain(dest, scale=1.0):
                b, out = take()
                b.empty(nc.scalar.activation(dest, out[0:dest.shape[0], :], ACT.Copy, scale=scale))

            w.split_high(act, 0, groups[0][2])
            w.split_high(act, 1, groups[1][2])
            act.wait_ge(raw_zero, 1)
            for g, (name, lo, _, tiles) in enumerate(groups):
                for f in range(len(tiles)):
                    if name in ("r", "k", "v"):
                        n = jobs[0]
                        b, out = take()
                        if n >= 2:
                            act.wait_ge(raw_read, n - 1)
                        b.empty(nc.scalar.activation(raw[n % 2][:, 1:T + 1], out[:, :], ACT.Copy))
                        act.wait_ge(b.emptied, b.n)
                        act.sem_inc(raw_out, 1)
                    elif name in ("qb", "qi"):
                        dest = m.qb if name == "qb" else m.qi
                        plain(dest[:, lo // P + f, :], HD ** -0.5)
                    elif name == "misc":
                        plain((m.ck, m.ki)[f][:, :])
                    elif name == "wi":
                        plain(m.wiT[:, :], IDX_HEADS ** -0.5)
                    elif name == "da":
                        b, out = take()
                        nc.scalar.activation(m.lo_da[0:HD, :], out[0:HD, :], ACT.Tanh)
                        b.empty(nc.scalar.activation(m.lo_da[HD:P, :], out[HD:P, :], ACT.Copy))
                    else:
                        b, out = take()
                        b.empty(nc.scalar.activation(m.lo_g[:, :], out[:, :], ACT.Sigmoid))
                if g + 2 < NG:
                    w.split_high(act, g + 2, groups[g + 2][2])

        @block.vector
        def _(dve):
            link = chain(dve, own)

            def mix_weights(g):
                slot = w.raw[g % w.RAW]
                dve.wait_ge(w.raw_in[g % w.RAW], 16 * arrived(g))
                for lo, n, i in ((0, HD, 0), (HD, HD, 1)) if groups[g][0] == "da" else ((0, P, 2),):
                    mub = mu[:, i, :].rearrange("p (k o) -> p k o", o=1).to_broadcast([P, KD, n])
                    link(nc.vector.tensor_tensor(slot[:, :, P + lo:P + lo + n], slot[:, :, lo:lo + n], mub, ALU.mult))
                    link(nc.vector.tensor_tensor(slot[:, :, lo:lo + n], slot[:, :, lo:lo + n],
                                                 slot[:, :, P + lo:P + lo + n], ALU.subtract))

            def split(g):
                if groups[g][0] in ("da", "gate"):
                    mix_weights(g)
                w.split_low(dve, g, groups[g][2], arrived(g))

            link(nc.vector.memset(raw[0][:, 0:1], 0.0))
            nc.vector.memset(raw[1][:, 0:1], 0.0).then_inc(raw_zero, 1)
            split(0)
            split(1)
            dve.wait_ge(prm_in, 16 * 4)
            link(nc.vector.tensor_scalar(less[:, :, :], m.mu[:, :, :], -1.0, 1.0, ALU.mult, ALU.add))
            n = 0
            for g, (name, _, _, tiles) in enumerate(groups):
                for f in range(len(tiles) if name in ("r", "k", "v") else 0):
                    i, fz = n // FT, n % FT
                    z = m.rkv[i][:, fz, :]
                    dve.wait_ge(raw_out, n + 1)
                    link(nc.vector.tensor_scalar(z, raw[n % 2][:, 1:T + 1], less[:, i, fz:fz + 1], None, ALU.mult))
                    nc.vector.scalar_tensor_tensor(out=z, in0=raw[n % 2][:, 0:T], scalar=m.mu[:, i, fz:fz + 1], in1=z,
                                                   op0=ALU.mult, op1=ALU.add).then_inc(raw_read, 1)
                    n += 1
                if g + 2 < NG:
                    split(g + 2)


@stage
def rwkv_prepare(nc, c, ctx, ps, m, prm):
    R, K, V = m.rkv
    w2a2 = c.sb("w2a2", [P, A_WIDTH], ctx=ctx)
    g2 = c.sb("g2", [P, A_WIDTH], ctx=ctx)
    vec = c.sb("vec", [P, 5, FT], ctx=ctx)
    dec, rn, sq, rw = (c.sb(n, [P, FT, T], ctx=ctx) for n in ("decay", "rnorm", "square", "rW"))
    zero = c.sb("zero", [P, CH], ctx=ctx)
    lora_in, vec_in, own = c.sem("lora_in"), c.sem("vec_in"), c.sem("dve_own")
    kk0, sq_done, clamped, root, dec_done, own_act = (c.sem("kk0"), c.sem("sq_done"), c.sem("clamped"), c.sem("root"),
                                                      c.sem("dec_done"), c.sem("act_own"))
    km_done, bonus_in, pool_own, W_done = c.sem("km_done"), c.sem("bonus_in"), c.sem("pool_own"), c.sem("W_done")
    sems = bank_sems(c, "prep")
    V_ = nc.vector

    with nc.Block() as block:

        @block.sync
        def _(sp):
            for i, name in enumerate(("w0", "a0", "k_k", "k_a", "r_k")):
                sp.dma_start(vec[:, i, :], prm[name].rearrange("(f p) -> p f", p=P),
                             allow_slow_non_contiguous=True).then_inc(vec_in, 16)
            sp.dma_start(w2a2[0:HD, :], prm["w2"]).then_inc(lora_in, 16)
            sp.dma_start(w2a2[HD:P, :], prm["a2"]).then_inc(lora_in, 16)
            sp.dma_start(g2[:, :], prm["g2"]).then_inc(lora_in, 16)

        @block.tensor
        def _(pe):
            banks = bank_set(ps, sems)
            pe.wait_ge(lora_in, 48)
            n = 0
            for lhsT, rhs in ((w2a2[0:HD], m.lo_da[0:HD, :]), (w2a2[HD:P], m.lo_da[HD:P, :]), (g2[:], m.lo_g[:, :])):
                for f in range(FT):
                    b = banks[n % 4]
                    n += 1
                    b.open(pe)
                    b.close(nc.tensor.matmul(b.ps[:, :], lhsT[:, f * P:(f + 1) * P], rhs, start=True, stop=True))
            for f in range(FT):
                pe.wait_ge(sq_done, f + 1)
                b = banks[4 + f]
                b.open(pe)
                b.close(nc.tensor.matmul(b.ps[:, :], c.headones[:, :], sq[:, f, :], start=True, stop=True))
            for f in range(FT):
                pe.wait_ge(bonus_in, f + 1)
                b = banks[4 + f]
                b.open(pe)
                b.close(nc.tensor.matmul(b.ps[:, :], c.headones[:, :], m.bonus[:, f, :], start=True, stop=True))

        @block.scalar
        def _(act):
            banks = bank_set(ps, sems)
            act.wait_ge(vec_in, 16 * 5)
            n = 0
            for dest, i in ((dec, 0), (m.rate, 1), (m.gate, None)):
                for f in range(FT):
                    b = banks[n % 4]
                    n += 1
                    out = b.read(act)
                    if i is None:
                        b.empty(nc.scalar.activation(dest[:, f, :], out[:, :], ACT.Copy))
                    else:
                        b.empty(nc.scalar.activation(dest[:, f, :], out[:, :], ACT.Sigmoid, bias=vec[:, i, f:f + 1]))
            act.wait_ge(banks[3].emptied, banks[3].n)
            act.wait_ge(banks[2].emptied, banks[2].n)
            act.wait_ge(banks[1].emptied, banks[1].n)
            act.wait_ge(banks[0].emptied, banks[0].n)
            nc.scalar.activation(dec[:, :, :], dec[:, :, :], ACT.Exp, scale=-DECAY).then_inc(dec_done, 1)
            act.wait_ge(clamped, 1)
            nc.scalar.activation(rn[:, :, :], rn[:, :, :], ACT.Sqrt).then_inc(root, 1)

        @block.gpsimd
        def _(pool):
            link = chain(pool, pool_own)
            for f in range(FT):
                pool.wait_ge(kk0, f + 1)
                nc.gpsimd.tensor_tensor(sq[:, f, :], m.kk[:, f, :], m.kk[:, f, :], ALU.mult).then_inc(sq_done, 1)
            for f in range(FT):
                pool.wait_ge(km_done, f + 1)
                link(nc.gpsimd.tensor_tensor(m.bonus[:, f, :], R[:, f, :], m.kmod[:, f, :], ALU.mult))
                nc.gpsimd.tensor_scalar(m.bonus[:, f, :], m.bonus[:, f, :], vec[:, 4, f:f + 1], None,
                                        ALU.mult).then_inc(bonus_in, 1)
            pool.wait_ge(bonus_in, FT)
            pool.wait_ge(W_done, FT)
            for f in range(FT):
                nc.gpsimd.tensor_tensor(R[:, f, :], R[:, f, :], m.W[:, f, :], ALU.mult)

        @block.vector
        def _(dve):
            banks = bank_set(ps, sems)
            link = chain(dve, own)
            link(V_.memset(zero[:, :], 0.0))
            dve.wait_ge(vec_in, 16 * 5)
            for f in range(FT):
                V_.tensor_scalar(m.kk[:, f, :], K[:, f, :], vec[:, 2, f:f + 1], None, ALU.mult).then_inc(kk0, 1)
            dve.wait_ge(dec_done, 1)
            for f in range(FT):
                link(V_.tensor_scalar(m.kmod[:, f, :], m.rate[:, f, :], 1.0, vec[:, 3, f:f + 1], ALU.subtract, ALU.mult))
                V_.scalar_tensor_tensor(out=m.kmod[:, f, :], in0=m.kmod[:, f, :], scalar=1.0, in1=K[:, f, :],
                                        op0=ALU.add, op1=ALU.mult).then_inc(km_done, 1)
            for f in range(FT):
                out = banks[4 + f].read(dve)
                ins = V_.tensor_scalar(rn[:, f, :], out[:, :], 1e-12, None, ALU.max)
                banks[4 + f].empty(ins)
            for f in range(FT):
                dve.wait_ge(banks[4 + f].emptied, 1)
            dve.sem_inc(clamped, 1)
            for f in range(FT):
                for i in range(NCH):
                    part = slice(i * CH, (i + 1) * CH)
                    ins = V_.tensor_tensor_scan(m.W[:, f, part], dec[:, f, part], zero[:, :], 1.0, ALU.mult, ALU.add)
                link(ins)
                dve.sem_inc(W_done, 1)
            link(V_.reciprocal(rw[:, :, :], m.W[:, :, :]))
            dve.wait_ge(root, 1)
            link(V_.reciprocal(rn[:, :, :], rn[:, :, :]))
            link(V_.tensor_tensor(m.kk[:, :, :], m.kk[:, :, :], rn[:, :, :], ALU.mult))
            link(V_.tensor_tensor(m.rate[:, :, :], m.rate[:, :, :], m.kk[:, :, :], ALU.mult))
            link(V_.tensor_tensor(m.rate[:, :, :], m.rate[:, :, :], rw[:, :, :], ALU.mult))
            kkc = m.kk[:, :, :].rearrange("p f (c i) -> p (f c) i", i=CH)
            Wc = m.W[:, :, :].rearrange("p f (c i) -> p (f c) i", i=CH)
            link(V_.tensor_tensor(kkc[:, :, 1:CH], kkc[:, :, 1:CH], Wc[:, :, 0:CH - 1], ALU.mult))
            for f in range(FT):
                out = banks[4 + f].read(dve)
                link(V_.tensor_tensor(m.bonus[:, f, :], out[:, :], V[:, f, :], ALU.mult))
                banks[4 + f].empty(V_.tensor_tensor(m.kmod[:, f, :], m.kmod[:, f, :], rw[:, f, :], ALU.mult))


@stage
def rwkv_chunks(nc, c, ctx, ps, m, yA):
    al, be, ka, rho, V, W = m.kk, m.rate, m.kmod, m.rkv[0], m.rkv[2], m.W
    LEVELS = CH.bit_length() - 2
    mask = c.sb("mask", [P, 4, P], ctx=ctx)
    grams = ["AT", "QbT", "NT", "QkT", "A"]
    G = {g: c.sb(g, [P, 2, FT, P], ctx=ctx) for g in ("QbT", "NT", "QkT")}
    A = [c.sb(f"A{i}", [P, 2, FT, P], ctx=ctx) for i in range(2)]
    AT = [c.sb(f"AT{i}", [P, 2, FT, P], ctx=ctx) for i in range(2)]
    XT = c.sb("XT", [P, 2, FT, P], ctx=ctx)
    Cm = c.sb("Cm", [P, 2, FT, P], ctx=ctx)
    vt, kt, bt = (c.sb(n, [P, FT, P], ctx=ctx) for n in ("v_tok", "kappa_tok", "beta_tok"))
    U0, Wt, nU = (c.sb(n, [P, FT, P], ctx=ctx) for n in ("U0", "Walpha", "minusU"))
    WT = c.sb("WalphaT", [P, FT, P], ctx=ctx)
    S = c.sb("state", [P, FT, P], ctx=ctx)
    made, own, x_ready, mask_ready = c.sem("masks_made"), c.sem("dve_own"), c.sem("XT_ready"), c.sem("mask_ready")
    gram_out, s_ready, vt_out = c.sem("gram_out"), c.sem("state_ready"), c.sem("vt_out")
    sems = bank_sems(c, "chunk")

    def heads():
        return [(par, f) for par in range(2) for f in range(FT)]

    with nc.Block() as block:

        @block.gpsimd
        def _(pool):
            link = chain(pool, made)
            G_ = nc.gpsimd
            for i, (cmp, sign, chan) in enumerate(((ALU.is_gt, -1.0, -1), (ALU.is_gt, -1.0, 1),
                                                   (ALU.is_gt, 1.0, -1), (ALU.is_ge, 1.0, -1))):
                link(G_.memset(mask[:, i, :], sign))
                link(G_.affine_select(out=mask[:, i, :], in_=mask[:, i, :], compare_op=cmp, fill=0.0, base=0,
                                      pattern=[[-chan, P]], channel_multiplier=chan))
                link(G_.memset(mask[0:CH, i, CH:P], 0.0))
                link(G_.memset(mask[CH:P, i, 0:CH], 0.0))
            link(G_.memset(S[:, :, :], 0.0))
            pool.sem_inc(mask_ready, 1)
            for t in range(TT):
                for par in range(2):
                    pool.wait_ge(gram_out, 2 * t + par + 1)
                    G_.tensor_tensor(XT[:, par, :, :], AT[0][:, par, :, :],
                                     c.ident[:, :].rearrange("p (o n) -> p o n", o=1).to_broadcast([P, FT, P]),
                                     ALU.add).then_inc(x_ready, 1)

        @block.tensor
        def _(pe):
            B = bank_set(ps, sems)
            M = nc.tensor.matmul

            def four(b, one):
                out = b.open(pe)
                for f in range(FT):
                    last = one(out[:, f * P:(f + 1) * P], f)
                b.close(last)

            def mm(lhsT, rhs):
                return lambda out, f: M(out, lhsT(f), rhs(f), start=True, stop=True)

            pe.wait_ge(mask_ready, 1)
            for t in range(TT):
                tok = slice(t * P, (t + 1) * P)
                for b, src in ((B[0], V), (B[4], ka), (B[1], be), (B[5], al)):
                    four(b, lambda out, f: nc.tensor.transpose(out, src[:, f, tok], c.ident[:, :]))
                n = 0
                for par in range(2):
                    q = slice(par * HD, (par + 1) * HD)
                    for g in grams:
                        l, r = dict(AT=(be, al), QbT=(be, rho), NT=(ka, al), QkT=(ka, rho), A=(al, be))[g]
                        four(B[(2 + n) % 4], mm(lambda f: l[q, f, tok], lambda f: r[q, f, tok]))
                        n += 1
                for b in B[0:4]:
                    b.copied(pe)
                for lv in range(1, LEVELS + 1):
                    old, new = (lv - 1) % 2, lv % 2
                    for par in range(2):
                        four(B[4 + par], mm(lambda f: AT[old][:, par, f, :], lambda f: A[old][:, par, f, :]))
                        if lv < LEVELS:
                            four(B[6 + par], mm(lambda f: A[old][:, par, f, :], lambda f: AT[old][:, par, f, :]))
                    for par in range(2):
                        B[4 + par].copied(pe)
                        if lv == 1:
                            pe.wait_ge(x_ready, 2 * t + par + 1)
                        else:
                            B[par].copied(pe)
                        four(B[par], mm(lambda f: A[new][:, par, f, :], lambda f: XT[:, par, f, :]))
                        if lv < LEVELS:
                            B[6 + par].copied(pe)
                for par in range(2):
                    four(B[2 + par], mm(lambda f: G["NT"][:, par, f, :], lambda f: vt[:, f, :]))
                for par in range(2):
                    B[2 + par].copied(pe)
                    B[par].copied(pe)
                    B[5].copied(pe)
                    four(B[par], mm(lambda f: XT[:, par, f, :], lambda f: Cm[:, par, f, :]))
                B[0].copied(pe)
                B[1].copied(pe)
                four(B[4], lambda out, f: nc.tensor.transpose(out, Wt[:, f, :], c.ident[:, :]))
                B[4].copied(pe)
                y = B[5].open(pe)
                for s in range(2):
                    p = slice(s * CH, (s + 1) * CH)
                    cur = slice(t * P + s * CH, t * P + (s + 1) * CH)
                    if t or s:
                        B[3].copied(pe)
                    out = B[2].open(pe)
                    for f in range(FT):
                        last = M(out[p, f * P:(f + 1) * P], WT[:, f, p], S[:, f, :], start=True, stop=True)
                    B[2].close(last)
                    for f in range(FT):
                        M(y[:, f * P + s * CH:f * P + (s + 1) * CH], S[:, f, :], rho[:, f, cur],
                          start=s == 0 and f == 0, stop=False, skip_group_check=True)
                    if s == 0:
                        for par, f in heads():
                            q = slice(par * HD, (par + 1) * HD)
                            M(y[q, f * P:(f + 1) * P], vt[:, f, q], G["QkT"][:, par, f, :],
                              start=False, stop=False, skip_group_check=True)
                    out = B[3].open(pe)
                    B[2].copied(pe)
                    for f in range(FT):
                        M(out[:, f * P:(f + 1) * P], kt[p, f, :], vt[p, f, :], start=True, stop=False)
                        last = M(out[:, f * P:(f + 1) * P], bt[p, f, :], nU[p, f, :], start=False, stop=True)
                    B[3].close(last)
                for par, f in heads():
                    q = slice(par * HD, (par + 1) * HD)
                    last = M(y[q, f * P:(f + 1) * P], nU[:, f, q], G["QbT"][:, par, f, :],
                             start=False, stop=(par, f) == (1, FT - 1), skip_group_check=True)
                B[5].close(last)

        def view(out):
            return out[:, :].rearrange("p (f n) -> p f n", f=FT)

        @block.scalar
        def _(act):
            B = bank_set(ps, sems)
            cp = lambda out, in_: nc.scalar.activation(out, in_, ACT.Copy)
            for t in range(TT):
                o = view(B[4].read(act))
                B[4].empty(cp(kt[:, :, :], o))
                o = view(B[5].read(act))
                cp(Cm[:, 0, :, HD:P], o[:, :, 0:HD])
                B[5].empty(cp(Cm[:, 1, :, HD:P], o[:, :, HD:P]))
                for lv in range(1, LEVELS + 1):
                    for par in range(2):
                        B[4 + par].empty(cp(A[lv % 2][:, par, :, :], view(B[4 + par].read(act))))
                        if lv < LEVELS:
                            B[6 + par].empty(cp(AT[lv % 2][:, par, :, :], view(B[6 + par].read(act))))
                B[4].empty(cp(WT[:, :, :], view(B[4].read(act))))
                B[5].empty(cp(yA[:, :, t * P:(t + 1) * P], view(B[5].read(act))))

        @block.vector
        def _(dve):
            B = bank_set(ps, sems)
            link = chain(dve, own)
            V_ = nc.vector
            dve.wait_ge(mask_ready, 1)
            dest = dict(AT=(AT[0], 0), QbT=(G["QbT"], 3), NT=(G["NT"], 2), QkT=(G["QkT"], 3), A=(A[0], 1))
            for t in range(TT):
                B[0].empty(V_.tensor_copy(vt[:, :, :], view(B[0].read(dve))))
                B[1].empty(V_.tensor_copy(bt[:, :, :], view(B[1].read(dve))))
                n = 0
                for par in range(2):
                    for g in grams:
                        b = B[(2 + n) % 4]
                        n += 1
                        out, i = dest[g]
                        ins = V_.tensor_tensor(out[:, par, :, :], view(b.read(dve)),
                                               mask[:, i:i + 1, :].to_broadcast([P, FT, P]), ALU.mult)
                        b.empty(ins)
                        if g == "AT":
                            dve.wait_ge(b.emptied, b.n)
                            dve.sem_inc(gram_out, 1)
                for lv in range(1, LEVELS + 1):
                    for par in range(2):
                        B[par].empty(V_.tensor_tensor(XT[:, par, :, :], view(B[par].read(dve)), XT[:, par, :, :],
                                                      ALU.add))
                for par in range(2):
                    B[2 + par].empty(V_.tensor_copy(Cm[:, par, :, 0:HD],
                                                    view(B[2 + par].read(dve))[:, :, par * HD:(par + 1) * HD]))
                for par in range(2):
                    q = slice(par * HD, (par + 1) * HD)
                    o = view(B[par].read(dve))
                    V_.tensor_copy(U0[:, :, q], o[:, :, 0:HD])
                    B[par].empty(V_.tensor_copy(Wt[:, :, q], o[:, :, HD:P]))
                for par in range(2):
                    dve.wait_ge(B[par].emptied, B[par].n)
                for s in range(2):
                    p = slice(s * CH, (s + 1) * CH)
                    end = t * P + (s + 1) * CH - 1
                    o = view(B[2].read(dve))
                    B[2].empty(V_.scalar_tensor_tensor(out=nU[p, :, :], in0=o[p, :, :], scalar=-1.0, in1=U0[p, :, :],
                                                       op0=ALU.mult, op1=ALU.subtract))
                    o = view(B[3].read(dve))
                    for par in range(2):
                        q = slice(par * HD, (par + 1) * HD)
                        link(V_.tensor_tensor(S[q, :, q], o[q, :, q], S[q, :, q], ALU.add))
                        ins = V_.tensor_tensor(S[q, :, q], S[q, :, q],
                                               W[q, :, end:end + 1].to_broadcast([HD, FT, HD]), ALU.mult)
                        if par == 0:
                            link(ins)
                    B[3].empty(ins)
                    dve.wait_ge(B[3].emptied, B[3].n)


@stage
def rwkv_finish(nc, c, ctx, ps, m, yA, yT, prm):
    vec = c.sb("ln", [P, 2, FT], ctx=ctx)
    sq = c.sb("sq", [P, FT, T], ctx=ctx)
    vec_in, centred, sq_done, root, own = (c.sem("ln_in"), c.sem("centred"), c.sem("sq_done"), c.sem("root"),
                                           c.sem("dve_own"))
    sum_done, var_done = c.sem("sum_done"), c.sem("var_done")
    with nc.Block() as block:

        @block.sync
        def _(sp):
            for i, name in enumerate(("ln_g", "ln_b")):
                sp.dma_start(vec[:, i, :], prm[name].rearrange("(f p) -> p f", p=P),
                             allow_slow_non_contiguous=True).then_inc(vec_in, 16)

        @block.tensor
        def _(pe):
            for f in range(FT):
                nc.tensor.matmul(ps[f][:, :], c.headones[:, :], yA[:, f, :], start=True, stop=True).then_inc(sum_done, 1)
            for f in range(FT):
                pe.wait_ge(sq_done, f + 1)
                nc.tensor.matmul(ps[4 + f][:, :], c.headones[:, :], sq[:, f, :], start=True, stop=True
                                 ).then_inc(var_done, 1)

        @block.gpsimd
        def _(pool):
            for f in range(FT):
                pool.wait_ge(centred, f + 1)
                nc.gpsimd.tensor_tensor(sq[:, f, :], yA[:, f, :], yA[:, f, :], ALU.mult).then_inc(sq_done, 1)

        @block.scalar
        def _(act):
            for f in range(FT):
                act.wait_ge(var_done, f + 1)
                nc.scalar.activation(sq[:, f, :], ps[4 + f][:, :], ACT.Sqrt, scale=1.0 / HD,
                                     bias=c.eps[:, 1:2]).then_inc(root, 1)

        @block.vector
        def _(dve):
            link = chain(dve, own)
            V_ = nc.vector
            for f in range(FT):
                dve.wait_ge(sum_done, f + 1)
                V_.scalar_tensor_tensor(out=yA[:, f, :], in0=ps[f][:, :], scalar=-1.0 / HD, in1=yA[:, f, :],
                                        op0=ALU.mult, op1=ALU.add).then_inc(centred, 1)
            dve.wait_ge(vec_in, 32)
            dve.wait_ge(centred, FT)
            for f in range(FT):
                y = yA[:, f, :]
                dve.wait_ge(root, f + 1)
                link(V_.reciprocal(sq[:, f, :], sq[:, f, :]))
                link(V_.tensor_tensor(y, y, sq[:, f, :], ALU.mult))
                link(V_.tensor_scalar(y, y, vec[:, 0, f:f + 1], vec[:, 1, f:f + 1], ALU.mult, ALU.add))
                link(V_.tensor_tensor(y, y, m.bonus[:, f, :], ALU.add))
                link(V_.tensor_tensor(yT[:, f, :], y, m.gate[:, f, :], ALU.mult))


@stage
def sparse_prepare(nc, c, ctx, ps, m, prm):
    wkv = c.sb("w_kv_up", [P, 2 * B_WIDTH], ctx=ctx)
    gkv = c.sb("kv_gain", [P, 1], ctx=ctx)
    gki = c.sb("ki_gain", [P, 1], ctx=ctx)
    sq = c.sb("sq", [P, 2, T], ctx=ctx)
    w_in, sq_done, sum_done, root, own = (c.sem("wkv_in"), c.sem("sq_done"), c.sem("sum_done"), c.sem("root"),
                                          c.sem("dve_own"))
    normed, up_done, wi_done, up_out = c.sem("normed"), c.sem("up_done"), c.sem("wi_done"), c.sem("up_out")
    with nc.Block() as block:

        @block.sync
        def _(sp):
            sp.dma_start(wkv[:, :], prm["w_kv_up"]).then_inc(w_in, 16)
            sp.dma_start(gkv[:, :], prm["kv_norm"].rearrange("(p o) -> p o", o=1)).then_inc(w_in, 16)
            for i in range(2):
                sp.dma_start(gki[i * HD:(i + 1) * HD, :],
                             prm["idx_k_norm"].rearrange("(p o) -> p o", o=1)).then_inc(w_in, 16)

        @block.tensor
        def _(pe):
            for t in range(TT):
                last = nc.tensor.transpose(ps[2][:, t * IDX_HEADS:(t + 1) * IDX_HEADS],
                                           m.wiT[:, t * P:(t + 1) * P], c.ident[0:IDX_HEADS, 0:IDX_HEADS])
            last.then_inc(wi_done, 1)
            for i, mat in enumerate((c.ones, c.headones)):
                pe.wait_ge(sq_done, i + 1)
                nc.tensor.matmul(ps[i][:, :], mat[:, :], sq[:, i, :], start=True, stop=True).then_inc(sum_done, 1)
            pe.wait_ge(w_in, 64)
            pe.wait_ge(normed, 1)
            for f in range(FT):
                if f >= 1:
                    pass
                nc.tensor.matmul(ps[3 + f][:, :], wkv[:, f * P:(f + 1) * P], m.ck[:, :], start=True, stop=True
                                 ).then_inc(up_done, 1)
            for t in range(TT):
                pe.wait_ge(up_out, t + 1)
                nc.tensor.matmul(ps[3 + t][:, :], m.ck[:, t * P:(t + 1) * P], wkv[:, B_WIDTH:2 * B_WIDTH],
                                 start=True, stop=True).then_inc(up_done, 1)

        @block.scalar
        def _(act):
            for i, src in enumerate((m.ck, m.ki)):
                nc.scalar.activation(sq[:, i, :], src[:, :], ACT.Square).then_inc(sq_done, 1)
            for i, n in enumerate((KV_RANK, HD)):
                act.wait_ge(sum_done, i + 1)
                nc.scalar.activation(sq[:, i, :], ps[i][:, :], ACT.Sqrt, scale=1.0 / n,
                                     bias=c.eps[:, 0:1]).then_inc(root, 1)
            for n in range(2 * FT):
                act.wait_ge(up_done, n + 1)
                dest = m.kb[:, n, :] if n < FT else m.vb[:, n - FT, :]
                nc.scalar.activation(dest, ps[3 + n % FT][:, :], ACT.Copy).then_inc(up_out, 1)

        @block.vector
        def _(dve):
            link = chain(dve, own)
            V_ = nc.vector
            dve.wait_ge(w_in, 64)
            for i, (x, g) in enumerate(((m.ck, gkv), (m.ki, gki))):
                dve.wait_ge(root, i + 1)
                link(V_.reciprocal(sq[:, i, :], sq[:, i, :]))
                V_.scalar_tensor_tensor(out=x[:, :], in0=x[:, :], scalar=g[:, 0:1], in1=sq[:, i, :],
                                        op0=ALU.mult, op1=ALU.mult).then_inc(normed, 1)
            dve.wait_ge(wi_done, 1)
            V_.tensor_copy(m.wi[:, :, :], ps[2][:, 0:TT * IDX_HEADS].rearrange("p (t h) -> p t h", t=TT))


@stage
def index_select(nc, c, ctx, ps, m):
    score = [c.sb(f"score{t}", [P, T], ctx=ctx) for t in range(TT)]
    best = [c.sb(f"best{t}", [P, 8], ctx=ctx) for t in range(TT)]
    rl = [c.sb(f"relu{i}", [P, T], ctx=ctx) for i in range(4)]
    dots, relu, added, own = c.sem("dots"), c.sem("relu"), c.sem("added"), c.sem("dve_own")
    scored, masked, zeroed = c.sem("scored"), c.sem("masked"), c.sem("zeroed")
    tiles = [3, 2, 1]
    units = [(t, h) for t in tiles for h in range(IDX_HEADS)]
    with nc.Block() as block:

        @block.tensor
        def _(pe):
            for u, (t, h) in enumerate(units):
                q = slice((h % 2) * HD, (h % 2 + 1) * HD)
                if u >= 4:
                    pe.wait_ge(relu, u - 3)
                nc.tensor.matmul(ps[u % 4][:, 0:(t + 1) * P], m.qi[q, h // 2, t * P:(t + 1) * P],
                                 m.ki[q, 0:(t + 1) * P], start=True, stop=True).then_inc(dots, 1)

        @block.scalar
        def _(act):
            for u, (t, h) in enumerate(units):
                act.wait_ge(dots, u + 1)
                if u >= 4:
                    act.wait_ge(added, u - 3)
                nc.scalar.activation(rl[u % 4][:, 0:(t + 1) * P], ps[u % 4][:, 0:(t + 1) * P],
                                     ACT.Relu).then_inc(relu, 1)

        @block.gpsimd
        def _(pool):
            G_ = nc.gpsimd
            G_.memset(m.bias[:, 0, 0:P], 0.0).then_inc(zeroed, 1)
            pool.wait_ge(zeroed, 1)
            G_.affine_select(out=m.bias[:, 0, 0:P], in_=m.bias[:, 0, 0:P], compare_op=ALU.is_ge, fill=NEG, base=0,
                             pattern=[[-1, P]], channel_multiplier=1)
            for i, t in enumerate(tiles):
                pool.wait_ge(scored, i + 1)
                part = score[t][:, t * P:(t + 1) * P]
                G_.affine_select(out=part, in_=part, compare_op=ALU.is_ge, fill=NEG, base=0,
                                 pattern=[[-1, P]], channel_multiplier=1).then_inc(masked, 1)

        @block.vector
        def _(dve):
            link = chain(dve, own)
            V_ = nc.vector

            def scores(t):
                for u, (tu, h) in enumerate(units):
                    if tu != t:
                        continue
                    s, r = score[t][:, 0:(t + 1) * P], rl[u % 4][:, 0:(t + 1) * P]
                    dve.wait_ge(relu, u + 1)
                    if h == 0:
                        V_.tensor_scalar(s, r, m.wi[:, t, h:h + 1], None, ALU.mult).then_inc(added, 1)
                    else:
                        dve.wait_ge(added, u)
                        V_.scalar_tensor_tensor(out=s, in0=r, scalar=m.wi[:, t, h:h + 1], in1=s,
                                                op0=ALU.mult, op1=ALU.add).then_inc(added, 1)
                dve.wait_ge(added, u + 1 if t == tiles[-1] else (tiles.index(t) + 1) * IDX_HEADS)
                dve.sem_inc(scored, 1)

            def search(t):
                s = score[t][:, 0:(t + 1) * P]
                dve.wait_ge(masked, tiles.index(t) + 1)
                for _ in range(TOPK // 8):
                    link(V_.max(best[t][:, :], s))
                    link(V_.match_replace(s, best[t][:, :], s, TAKEN))
                V_.tensor_scalar(m.bias[:, t, 0:(t + 1) * P], s, TAKEN / 2, NEG, ALU.is_gt, ALU.mult)

            scores(3)
            scores(2)
            search(3)
            scores(1)
            search(2)
            search(1)


@stage
def sparse_attend(nc, c, ctx, ps, m, yT):
    units = [(h, t) for h in range(B_HEADS) for t in range(TT)]
    N = len(units)
    RING, LT, LP = 4, 3, 4
    lg = [c.sb(f"prob{i}", [P, T], ctx=ctx) for i in range(RING)]
    pT = [c.sb(f"probT{i}", [P, T], ctx=ctx) for i in range(2)]
    nmax = c.sb("minus_max", [P, N], ctx=ctx)
    tot = c.sb("total", [P, N], ctx=ctx)
    inv = c.sb("inverse", [P, N], ctx=ctx)
    qk, biased, maxed, exped, inverted, scaled, turned, pT_out, pv, y_out = (
        c.sem(n) for n in ("qk", "biased", "maxed", "exped", "inverted", "scaled", "turned", "pT_out", "pv", "y_out"))
    ps_z, ps_t, ps_y = ps[0:3], ps[3:5], ps[5:7]
    with nc.Block() as block:

        @block.tensor
        def _(pe):
            for i in range(N + LP):
                if i < N:
                    h, t = units[i]
                    q = slice((h % 2) * HD, (h % 2 + 1) * HD)
                    if i >= 3:
                        pe.wait_ge(biased, i - 2)
                    nc.tensor.matmul(ps_z[i % 3][:, 0:(t + 1) * P], m.qb[q, h // 2, t * P:(t + 1) * P],
                                     m.kb[q, h // 2, 0:(t + 1) * P], start=True, stop=True).then_inc(qk, 1)
                u = i - LT
                if 0 <= u < N:
                    pe.wait_ge(scaled, u + 1)
                    if u >= 2:
                        pe.wait_ge(pT_out, u - 1)
                    for b in range(units[u][1] + 1):
                        last = nc.tensor.transpose(ps_t[u % 2][:, b * P:(b + 1) * P],
                                                   lg[u % RING][:, b * P:(b + 1) * P], c.ident[:, :])
                    last.then_inc(turned, 1)
                u = i - LP
                if 0 <= u < N:
                    h, t = units[u]
                    q = slice((h % 2) * HD, (h % 2 + 1) * HD)
                    pair = h // 2
                    pe.wait_ge(pT_out, u + 1)
                    if h % 2 == 0 and t == 0 and pair >= 2:
                        pe.wait_ge(y_out, pair - 1)
                    for b in range(t + 1):
                        last = nc.tensor.matmul(ps_y[pair % 2][q, t * P:(t + 1) * P], m.vb[:, b, h * HD:(h + 1) * HD],
                                                pT[u % 2][:, b * P:(b + 1) * P], start=b == 0, stop=b == t)
                    last.then_inc(pv, 1)

        @block.vector
        def _(dve):
            V_ = nc.vector
            for i in range(N + 1):
                if i < N:
                    h, t = units[i]
                    L = (t + 1) * P
                    dve.wait_ge(qk, i + 1)
                    if i >= RING:
                        dve.wait_ge(turned, i - RING + 1)
                    V_.tensor_tensor(lg[i % RING][:, 0:L], ps_z[i % 3][:, 0:L], m.bias[:, t, 0:L],
                                     ALU.add).then_inc(biased, 1)
                    dve.wait_ge(biased, i + 1)
                    V_.tensor_reduce(nmax[:, i:i + 1], lg[i % RING][:, 0:L], AX.X, ALU.max,
                                     negate=True).then_inc(maxed, 1)
                if i >= 1:
                    dve.wait_ge(exped, i)
                    V_.reciprocal(inv[:, i - 1:i], tot[:, i - 1:i]).then_inc(inverted, 1)

        @block.scalar
        def _(act):
            for i in range(N + LT):
                if i < N:
                    L = (units[i][1] + 1) * P
                    act.wait_ge(maxed, i + 1)
                    nc.scalar.activation(lg[i % RING][:, 0:L], lg[i % RING][:, 0:L], ACT.Exp,
                                         bias=nmax[:, i:i + 1], accum_out=tot[:, i:i + 1]).then_inc(exped, 1)
                u = i - LT
                if u >= 0:
                    L = (units[u][1] + 1) * P
                    act.wait_ge(turned, u + 1)
                    if u >= 2:
                        act.wait_ge(pv, u - 1)
                    nc.scalar.activation(pT[u % 2][:, 0:L], ps_t[u % 2][:, 0:L], ACT.Copy).then_inc(pT_out, 1)
                    if u % 8 == 2 and u > 8:
                        pair = u // 8 - 1
                        act.wait_ge(pv, 8 * (pair + 1))
                        nc.scalar.activation(yT[:, FT + pair, :], ps_y[pair % 2][:, :], ACT.Copy).then_inc(y_out, 1)
            pair = B_HEADS // 2 - 1
            act.wait_ge(pv, N)
            nc.scalar.activation(yT[:, FT + pair, :], ps_y[pair % 2][:, :], ACT.Copy).then_inc(y_out, 1)

        @block.gpsimd
        def _(pool):
            for i, (h, t) in enumerate(units):
                L = (t + 1) * P
                pool.wait_ge(inverted, i + 1)
                nc.gpsimd.tensor_scalar(lg[i % RING][:, 0:L], lg[i % RING][:, 0:L], inv[:, i:i + 1], None,
                                        ALU.mult).then_inc(scaled, 1)


class Mixed:
    pass


def even_mixer(nc, c, ps, x, gain, w_in, w_out, prm, wts, slots):
    with ExitStack() as ctx:
        yT = c.sb("yT", [P, KD, T], ctx=ctx)
        with ExitStack() as mid:
            m = Mixed()
            m.qb, m.qi = (c.sb(n, [P, FT, T], ctx=mid) for n in ("q_b", "q_idx"))
            m.ck, m.ki = (c.sb(n, [P, T], ctx=mid) for n in ("c_kv", "k_idx"))
            m.wiT = c.sb("w_idxT", [IDX_HEADS, T], ctx=mid)
            with ExitStack() as rw:
                m.rkv = [c.sb(n, [P, FT, T], ctx=rw) for n in "rkv"]
                m.mu = c.sb("mu_rkv", [P, 3, FT], ctx=rw)
                m.lo_da, m.lo_g = c.sb("lora_da", [P, T], ctx=rw), c.sb("lora_g", [P, T], ctx=rw)
                with ExitStack() as proj:
                    xn = c.sb("xn", [P, TT, D], ctx=proj)
                    even_project(nc, c, proj, ps, x, xn, gain, w_in, m, prm)
                m.rate, m.gate, m.kk, m.kmod, m.bonus, m.W = (
                    c.sb(n, [P, FT, T], ctx=rw) for n in ("rate", "gate", "kk", "k_mod", "bonus", "W"))
                with ExitStack() as prep:
                    rwkv_prepare(nc, c, prep, ps, m, prm)
                yA = c.sb("yA", [P, FT, T], ctx=rw)
                with ExitStack() as chunks:
                    rwkv_chunks(nc, c, chunks, ps, m, yA)
                with ExitStack() as fin:
                    rwkv_finish(nc, c, fin, ps, m, yA, yT, prm)
            with ExitStack() as sp:
                m.kb, m.vb, m.bias = (c.sb(n, [P, FT, T], ctx=sp) for n in ("k_b", "v_b", "bias"))
                m.wi = c.sb("w_idx", [P, TT, IDX_HEADS], ctx=sp)
                with ExitStack() as inner:
                    sparse_prepare(nc, c, inner, ps, m, prm)
                with ExitStack() as inner:
                    index_select(nc, c, inner, ps, m)
                with ExitStack() as inner:
                    sparse_attend(nc, c, inner, ps, m, yT)
        for _ in range(SLOTS - 1):
            wts.add_slot(slots)
        out_project(nc, c, ctx, ps, x, yT, w_out, wts.prefetch(range(SLOTS - 1)))


@stage
def load_x(nc, c, x, x_dram, xrows):
    x_in, cleared, zeroed = c.sem("x_in"), c.sem("rows_cleared"), c.sem("zeroed")
    with ExitStack() as ctx:
        zero = c.sb("zero_rows", [MB, D], ctx=ctx)
        with nc.Block() as block:

            @block.vector
            def _(dve):
                nc.vector.memset(zero[:, :], 0.0).then_inc(zeroed, 1)

            @block.sync
            def _(sp):
                sp.dma_start(x[:, :, :], x_dram.rearrange("(t p) d -> p t d", p=P)).then_inc(x_in, 16)
                sp.wait_ge(zeroed, 1)
                sp.dma_start(xrows[N_ASG:N_ROWS, :], zero[:, :]).then_inc(cleared, 16)
                sp.wait_ge(cleared, 16)
                sp.wait_ge(x_in, 16)


@stage
def final_norm(nc, c, x, gain, out_dram):
    with ExitStack() as ctx:
        g = c.sb("final_gain", [P, D], ctx=ctx)
        sq = c.sb("squares", [P, TT, D], ctx=ctx)
        ss = c.sb("ss", [P, 2 * TT], ctx=ctx)
        g_in, summed, root, own, ready, stored = (c.sem(n) for n in ("final_gain_in", "summed", "root", "dve_own",
                                                                     "out_ready", "out_stored"))
        with nc.Block() as block:

            @block.sync
            def _(sp):
                sp.dma_start(g[:, :], gain.rearrange("(o d) -> o d", o=1).to_broadcast([P, D])).then_inc(g_in, 16)
                for t in range(TT):
                    sp.wait_ge(ready, t + 1)
                    sp.dma_start(out_dram[t * P:(t + 1) * P, :], sq[:, t, :]).then_inc(stored, 16)
                sp.wait_ge(stored, 16 * TT)

            @block.scalar
            def _(act):
                for t in range(TT):
                    nc.scalar.activation(sq[:, t, :], x[:, t, :], ACT.Square,
                                         accum_out=ss[:, t:t + 1]).then_inc(summed, 1)
                act.wait_ge(summed, TT)
                nc.scalar.activation(ss[:, TT:2 * TT], ss[:, 0:TT], ACT.Sqrt, scale=1.0 / D,
                                     bias=c.eps[:, 0:1]).then_inc(root, 1)

            @block.vector
            def _(dve):
                link = chain(dve, own)
                dve.wait_ge(g_in, 16)
                dve.wait_ge(root, 1)
                link(nc.vector.reciprocal(ss[:, TT:2 * TT], ss[:, TT:2 * TT]))
                for t in range(TT):
                    nc.vector.scalar_tensor_tensor(out=sq[:, t, :], in0=x[:, t, :], scalar=ss[:, TT + t:TT + t + 1],
                                                   in1=g[:, :], op0=ALU.mult, op1=ALU.mult).then_inc(ready, 1)


def build(nc, a, out):
    with ExitStack() as ctx:
        c = Core(nc, ctx)
        x = c.sb("x", [P, TT, D])
        ps = [ctx.enter_context(nc.psum_tensor(f"ps{i}", [P, BANK], F32)) for i in range(8)]
        xrows = nc.dram_tensor("sorted_rows", [N_ROWS, D], F32).ap()
        yrows = nc.dram_tensor("expert_rows", [N_ROWS, D], F32).ap()
        load_x(nc, c, x, a["x"][0], xrows)
        constants(nc, c)
        prm = {n: a["a_" + n][0] for n in ("mu_lora", "mu_rkv", "w0", "w1", "w2", "a0", "a1", "a2", "g1", "g2",
                                           "k_k", "k_a", "ln_g", "ln_b")}
        prm["r_k"] = a["a_r_k"][0].rearrange("h d -> (h d)")
        prm.update({n: a["b_" + n][0] for n in ("kv_norm", "w_kv_up", "idx_k_norm")})
        wts = ExpertWeights(c)
        for layer in range(a["moe_norm"].shape[0]):
            wts.start_layer(a["moe_w1"][layer], a["moe_w3"][layer], a["moe_w2"][layer])
            slots = ctx.enter_context(ExitStack())
            if layer % 2 == 0:
                even_mixer(nc, c, ps, x, a["ev_norm"][layer // 2], a["ev_w_in"][layer // 2],
                           a["ev_w_out"][layer // 2], prm, wts, slots)
            else:
                odd_mixer(nc, c, ps, x, a["od_norm"][layer // 2], a["od_w_qkv"][layer // 2],
                          a["od_w_out"][layer // 2], wts, slots)
            moe(nc, c, ps, x, xrows, yrows, a["moe_norm"][layer], a["moe_router_group"][layer],
                a["moe_router_expert"][layer], wts, slots)
        final_norm(nc, c, x, a["final_norm"], out[0])


_INS = ["x", "ev_norm", "ev_w_in", "ev_w_out", "a_mu_rkv", "a_mu_lora", "a_w0", "a_w1", "a_w2", "a_a0", "a_a1",
        "a_a2", "a_g1", "a_g2", "a_k_k", "a_k_a", "a_r_k", "a_ln_g", "a_ln_b", "b_kv_norm", "b_w_kv_up",
        "b_idx_k_norm", "od_norm", "od_w_qkv", "od_w_out", "moe_norm", "moe_router_group", "moe_router_expert",
        "moe_w1", "moe_w3", "moe_w2", "final_norm"]


def kernel(**inputs):
    import numpy as np
    import concourse.bacc as bacc
    from concourse.bass_utils import run_bass_kernel_spmd

    nc = bacc.Bacc("TRN2", target_bir_lowering=False, num_devices=1)
    arrays, args = {}, {}
    for name in _INS:
        arrays[f"in_{name}"] = np.ascontiguousarray(inputs[name])
        args[name] = nc.dram_tensor(f"in_{name}", arrays[f"in_{name}"].shape, F32, kind="ExternalInput").ap()
    shape = inputs["x"].shape
    out = nc.dram_tensor("out_x", shape, F32, kind="ExternalOutput").ap()
    build(nc, args, out)
    r = run_bass_kernel_spmd(nc, [arrays], core_ids=[0])
    return r.results[0]["out_x"]
```

```python
import math
from contextlib import ExitStack

import concourse.bass as bass
from concourse import mybir

F32 = mybir.dt.float32
I32 = mybir.dt.int32
F32R = mybir.dt.float32r
U32 = mybir.dt.uint32
ALU = mybir.AluOpType
ACT = mybir.ActivationFunctionType
AX = mybir.AxisListType

P = 128
BANK = 512
D = 1024
T = 512
TT = T // P
KD = D // P
HD = 64
RMS_EPS = 1e-6
NEG = -1e30
TAKEN = -3e38

N_EXP = 32
N_GRP = 4
EPG = N_EXP // N_GRP
FF = 512
KF = FF // P
MB = 48
MB_MAX = -(-T // MB)
UP = 64
N_ASG = 2 * T
N_ROWS = N_ASG + MB


class Core:

    def __init__(self, nc, ctx):
        self.nc, self.ctx, self.made, self.of_stage = nc, ctx, 0, []

    def sb(self, name, shape, dt=F32, ctx=None, side="left"):
        self.made += 1
        return (ctx or self.ctx).enter_context(self.nc.sbuf_tensor(f"{name}_{self.made}", shape, dt, side=side))

    def lasting_sem(self, name):
        self.made += 1
        return self.nc.alloc_semaphore(name=f"{name}_{self.made}")

    def sem(self, name):
        self.made += 1
        s = self.nc.alloc_semaphore(name=f"{name}_{self.made}")
        self.of_stage.append(s)
        return s

    def end_stage(self):
        if self.of_stage:
            self.nc.clear_and_free_semaphores(self.of_stage)
            self.nc.all_engine_barrier()
        self.of_stage = []


def stage(f):
    def run(nc, c, *args):
        f(nc, c, *args)
        c.end_stage()
    return run


def chain(eng, sem):
    done = [0]

    def link(*instructions):
        for ins in instructions:
            done[0] += 1
            ins.then_inc(sem, 1)
        eng.wait_ge(sem, done[0])

    return link


def keep_warm(nc, c, ps, n):
    for _ in range(n):
        nc.tensor.matmul(ps[:, 0:P], c.half[:, :], c.half[:, :], start=True, stop=True)


@stage
def constants(nc, c, loads):
    c.ident = c.sb("ident", [P, P])
    c.ones = c.sb("ones", [P, P])
    c.tri = c.sb("tri", [P, P])
    c.half = c.sb("half", [P, P], mybir.dt.bfloat16)
    c.headones = c.sb("headones", [P, P])
    c.count32 = c.sb("count32", [P, N_EXP])
    c.eps = c.sb("eps", [P, 4])
    made = c.sem("const_made")
    with nc.Block() as block:

        @block.sync
        def _(sp):
            loads(sp)

        @block.gpsimd
        def _(pool):
            link = chain(pool, made)
            link(nc.gpsimd.memset(c.ones[:, :], 1.0))
            link(nc.gpsimd.memset(c.ident[:, :], 0.0))
            link(nc.gpsimd.affine_select(out=c.ident[:, :], in_=c.ident[:, :], compare_op=ALU.not_equal,
                                         fill=1.0, base=0, pattern=[[-1, P]], channel_multiplier=1))
            link(nc.gpsimd.affine_select(out=c.tri[:, :], in_=c.ones[:, :], compare_op=ALU.is_gt,
                                         fill=0.0, base=0, pattern=[[1, P]], channel_multiplier=-1))
            link(nc.gpsimd.memset(c.half[:, :], 0.0))
            link(nc.gpsimd.memset(c.headones[:, :], 0.0))
            link(nc.gpsimd.memset(c.headones[0:HD, 0:HD], 1.0))
            link(nc.gpsimd.memset(c.headones[HD:P, HD:P], 1.0))
            link(nc.gpsimd.memset(c.eps[:, :], 0.0))
            link(nc.gpsimd.memset(c.eps[:, 0:1], RMS_EPS))
            link(nc.gpsimd.memset(c.eps[:, 1:2], 64e-5))
            link(nc.gpsimd.iota(c.count32[:, :], [[1, N_EXP]], base=0, channel_multiplier=0,
                                allow_small_or_imprecise_dtypes=True))


class InPlace:

    def wait_tile(self, eng, t):
        pass

    def add_tile(self, dve, link, t):
        pass

    def start(self, block):
        pass

    def free_banks(self, pe):
        pass


class Arriving(InPlace):

    def __init__(self, c, x, x_dram):
        self.c, self.x, self.x_dram = c, x, x_dram
        self.x_in = [c.lasting_sem(f"x_in{t}") for t in range(TT)]

    def load(self, sp):
        for t in range(TT):
            sp.dma_start(self.x[:, t, :], self.x_dram[t * P:(t + 1) * P, :]).then_inc(self.x_in[t], 16)

    def wait_tile(self, eng, t):
        eng.wait_ge(self.x_in[t], 16)

    def add_tile(self, dve, link, t):
        dve.wait_ge(self.x_in[t], 16)

    def start(self, block):
        self.c.of_stage += self.x_in


class OutProject(InPlace):

    def __init__(self, nc, c, ps, x, yT, wts):
        self.nc, self.ps, self.x, self.yT, self.wts = nc, ps, x, yT, wts
        c.of_stage += wts.guest_in
        self.done, self.added = c.sem("out_done"), c.sem("out_added")

    def start(self, block):
        w = self.wts.guest()

        @block.sync
        def _(sp):
            self.wts.prefetch(range(SLOTS - 1))(sp)
            sp.wait_ge(self.done, 2 * TT)
            self.wts.prefetch([SLOTS - 1])(sp)

        @block.tensor
        def _(pe):
            for t in range(TT):
                for h in range(2):
                    if t == 0:
                        pe.wait_ge(self.wts.guest_in[h], 16)
                    for f in range(KD):
                        last = self.nc.tensor.matmul(self.ps[2 * t + h][:, :], self.yT[:, f, t * P:(t + 1) * P],
                                                     w[h][:, f, :], start=f == 0, stop=f == KD - 1)
                    last.then_inc(self.done, 1)

    def add_tile(self, dve, link, t):
        for h in range(2):
            dve.wait_ge(self.done, 2 * t + h + 1)
            xs = self.x[:, t, h * BANK:(h + 1) * BANK]
            link(self.nc.vector.tensor_tensor(xs, self.ps[2 * t + h][:, :], xs, ALU.add))
        dve.sem_inc(self.added, 1)

    def wait_tile(self, eng, t):
        eng.wait_ge(self.added, t + 1)

    def free_banks(self, pe):
        pe.wait_ge(self.added, TT)


def norm_transpose(nc, c, ctx, ps, block, x, xn, gain_dram, evacuate, update=InPlace()):
    g = c.sb("gain", [P, KD], ctx=ctx)
    ss = c.sb("ss", [P, 2 * TT], ctx=ctx)
    rstd = c.sb("rstd", [P, TT], ctx=ctx)
    gain_in, ss_done, std_done, dve_own = c.sem("gain_in"), c.sem("ss_done"), c.sem("std_done"), c.sem("dve_own")
    xn_done, turned = c.sem("xn_done"), c.sem("turned")

    @block.sync
    def _(sp):
        sp.dma_start(g[:, :], gain_dram.rearrange("(p k) -> p k", k=KD)).then_inc(gain_in, 16)

    update.start(block)

    @block.scalar
    def _(act):
        for t in range(TT):
            update.wait_tile(act, t)
            nc.scalar.activation(xn[:, t, :], x[:, t, :], ACT.Square, accum_out=ss[:, t:t + 1]).then_inc(ss_done, 1)
            act.wait_ge(ss_done, t + 1)
            nc.scalar.activation(ss[:, TT + t:TT + t + 1], ss[:, t:t + 1], ACT.Sqrt, scale=1.0 / D,
                                 bias=c.eps[:, 0:1]).then_inc(std_done, 1)

    @block.vector
    def _(dve):
        link = chain(dve, dve_own)
        for t in range(TT + 1):
            if t < TT:
                update.add_tile(dve, link, t)
            if t >= 1:
                u = t - 1
                dve.wait_ge(std_done, u + 1)
                link(nc.vector.reciprocal(rstd[:, u:u + 1], ss[:, TT + u:TT + u + 1]))
                nc.vector.tensor_scalar(xn[:, u, :], x[:, u, :], rstd[:, u:u + 1], None, ALU.mult).then_inc(xn_done, 1)

    @block.tensor
    def _(pe):
        update.free_banks(pe)
        for t in range(TT):
            pe.wait_ge(xn_done, t + 1)
            for k in range(KD):
                last = nc.tensor.transpose(ps[k][:, t * P:(t + 1) * P], xn[:, t, k::KD], c.ident[:, :])
                if t == TT - 1:
                    last.then_inc(turned, 1)

    evacuate(block, g, gain_in, turned)


@stage
def router(nc, c, ctx, ps, x, xn, hT, gain_dram, w_group, w_expert, xrows, r, update):
    zero = c.sb("zero_rows", [MB, D], ctx=ctx)
    cleared, zeroed = c.sem("rows_cleared"), c.sem("zeroed")
    wr = c.sb("w_router", [P, KD, N_GRP + N_EXP], ctx=ctx)
    NL = N_GRP + N_EXP
    lgT = c.sb("logitsT", [NL, T], ctx=ctx)
    lg = c.sb("logits", [P, TT, NL], ctx=ctx)
    g8 = c.sb("group8", [P, TT, 8], ctx=ctx)
    e8 = c.sb("expert8", [P, TT, EPG], ctx=ctx)
    best = c.sb("best", [P, 2, TT, 8], ctx=ctx)
    besti = c.sb("best_index", [P, 2, TT, 8], U32, ctx=ctx)
    bestf = c.sb("best_index_f", [P, 2, TT, 8], ctx=ctx)
    prod = c.sb("prod", [P, TT, N_EXP], ctx=ctx)
    small = c.sb("small", [P, 12, TT], ctx=ctx)
    gex = c.sb("group_exp", [P, TT, N_GRP], ctx=ctx)
    hot = c.sb("hot", [P, 3, TT, N_EXP], ctx=ctx)
    pos = c.sb("pos", [P, TT, N_EXP], ctx=ctx)
    tab = c.sb("tab", [P, 8, N_EXP], ctx=ctx)
    hT_even, hT_odd = c.sem("hT_even_steps"), c.sem("hT_odd_steps")
    w_in, scattered = c.sem("router_w_in"), c.sem("rows_scattered")
    logitsT_done, logitsT_out, logits_done = c.sem("logitsT_done"), c.sem("logitsT_out"), c.sem("logits_done")
    own, sub_done, exp_done = c.sem("dve_own"), c.sem("sub_done"), c.sem("exp_done")
    hot_done, pos_done, dest_done = c.sem("hot_done"), c.sem("pos_done"), c.sem("dest_done")

    def col(t):
        return t[:, :, :]

    def wide(ap, n):
        return ap.rearrange("p (t o) -> p t o", o=1).to_broadcast([P, TT, n])

    def evacuate(block, g, gain_in, turned):

        @block.vector
        def _(dve):
            dve.wait_ge(gain_in, 16)
            for k in range(0, KD, 2):
                dve.wait_ge(turned, k + 1)
                nc.vector.tensor_scalar(hT[:, k, :], ps[k][:, :], g[:, k:k + 1], None, ALU.mult).then_inc(hT_even, 1)

        @block.scalar
        def _(act):
            act.wait_ge(gain_in, 16)
            for k in range(1, KD, 2):
                act.wait_ge(turned, k + 1)
                nc.scalar.activation(hT[:, k, :], ps[k][:, :], ACT.Copy, scale=g[:, k:k + 1]).then_inc(hT_odd, 1)

    with nc.Block() as block:
        @block.sync
        def _(sp):
            sp.dma_start(wr[:, :, 0:N_GRP], w_group.rearrange("(p k) n -> p k n", k=KD)).then_inc(w_in, 16)
            for g in range(N_GRP):
                lo = N_GRP + g * EPG
                sp.dma_start(wr[:, :, lo:lo + EPG],
                             w_expert[g].rearrange("(p k) n -> p k n", k=KD)).then_inc(w_in, 16)

        norm_transpose(nc, c, ctx, ps, block, x, xn, gain_dram, evacuate, update)

        @block.gpsimd
        def _(pool):
            nc.gpsimd.memset(zero[:, :], 0.0).then_inc(zeroed, 1)
            pool.wait_ge(zeroed, 1)
            pool.dma_start(xrows[N_ASG:N_ROWS, :], zero[:, :]).then_inc(cleared, 16)
            pool.wait_ge(cleared, 16)

        @block.tensor
        def _(pe):
            pe.wait_ge(w_in, 16 * (1 + N_GRP))
            for k in range(KD):
                pe.wait_ge(hT_odd if k % 2 else hT_even, k // 2 + 1)
                last = nc.tensor.matmul(ps[0][0:NL, :], wr[:, k, :], hT[:, k, :],
                                        start=k == 0, stop=k == KD - 1)
            last.then_inc(logitsT_done, 1)
            pe.wait_ge(logitsT_out, 1)
            for t in range(TT):
                last = nc.tensor.transpose(ps[1][:, t * NL:(t + 1) * NL], lgT[:, t * P:(t + 1) * P],
                                           c.ident[0:NL, 0:NL])
            last.then_inc(logits_done, 1)
            pe.wait_ge(hot_done, 1)
            nc.tensor.matmul(ps[2][:, 0:P], c.tri[:, :], hot[:, 2, :, :].rearrange("p t e -> p (t e)"),
                             start=True, stop=True)
            nc.tensor.matmul(ps[3][:, 0:P], c.ones[:, :], hot[:, 2, :, :].rearrange("p t e -> p (t e)"),
                             start=True, stop=True).then_inc(pos_done, 1)

        @block.scalar
        def _(act):
            act.wait_ge(sub_done, 1)
            nc.scalar.activation(gex[:, :, :], gex[:, :, :], ACT.Exp).then_inc(exp_done, 1)
            act.wait_ge(sub_done, 2)
            nc.scalar.activation(small[:, 3, :], small[:, 2, :], ACT.Exp).then_inc(exp_done, 1)

        @block.vector
        def _(dve):
            link = chain(dve, own)
            V = nc.vector
            link(V.memset(g8[:, :, :], NEG))
            dve.wait_ge(logitsT_done, 1)
            V.tensor_copy(lgT[:, :], ps[0][0:NL, :]).then_inc(logitsT_out, 1)
            dve.wait_ge(logits_done, 1)
            link(V.tensor_copy(lg[:, :, :], ps[1][:, 0:TT * NL].rearrange("p (t n) -> p t n", n=NL)))
            link(V.tensor_copy(g8[:, :, 0:N_GRP], lg[:, :, 0:N_GRP]))
            link(*(V.max(best[:, 0, t, :], g8[:, t, :]) for t in range(TT)))
            link(*(V.max_index(besti[:, 0, t, :], best[:, 0, t, :], g8[:, t, :]) for t in range(TT)))
            link(V.tensor_copy(bestf[:, 0, :, :], besti[:, 0, :, :]))
            V.tensor_tensor(gex[:, :, :], lg[:, :, 0:N_GRP], best[:, 0, :, 0:1].to_broadcast([P, TT, N_GRP]),
                            ALU.subtract).then_inc(sub_done, 1)
            link(V.tensor_tensor(pos[:, :, 0:N_GRP], c.count32[:, 0:N_GRP].rearrange("p (o g) -> p o g", o=1)
                                 .to_broadcast([P, TT, N_GRP]),
                                 bestf[:, 0, :, 0:1].to_broadcast([P, TT, N_GRP]), ALU.is_equal))
            by_group = prod[:, :, :].rearrange("p t (g e) -> p t g e", e=EPG)
            link(V.tensor_tensor(by_group, lg[:, :, N_GRP:NL].rearrange("p t (g e) -> p t g e", e=EPG),
                                 pos[:, :, 0:N_GRP].rearrange("p t (g o) -> p t g o", o=1)
                                 .to_broadcast([P, TT, N_GRP, EPG]), ALU.mult))
            link(V.tensor_reduce(e8[:, :, :], prod[:, :, :].rearrange("p t (g e) -> p t e g", e=EPG), AX.X, ALU.add))
            link(*(V.max(best[:, 1, t, :], e8[:, t, :]) for t in range(TT)))
            link(*(V.max_index(besti[:, 1, t, :], best[:, 1, t, :], e8[:, t, :]) for t in range(TT)))
            link(V.tensor_copy(bestf[:, 1, :, :], besti[:, 1, :, :]))
            V.tensor_tensor(small[:, 2, :], best[:, 1, :, 1], best[:, 1, :, 0], ALU.subtract).then_inc(sub_done, 1)
            link(*(V.scalar_tensor_tensor(out=small[:, 4 + j, :], in0=bestf[:, 0, :, 0], scalar=float(EPG),
                                          in1=bestf[:, 1, :, j], op0=ALU.mult, op1=ALU.add) for j in range(2)))
            link(*(V.tensor_tensor(hot[:, j, :, :], c.count32[:, :].rearrange("p (o e) -> p o e", o=1)
                                   .to_broadcast([P, TT, N_EXP]), wide(small[:, 4 + j, :], N_EXP), ALU.is_equal)
                   for j in range(2)))
            V.tensor_tensor(hot[:, 2, :, :], hot[:, 0, :, :], hot[:, 1, :, :], ALU.add).then_inc(hot_done, 1)
            dve.wait_ge(pos_done, 1)
            total = ps[3][:, 0:P].rearrange("p (t e) -> p t e", e=N_EXP)
            link(V.memset(tab[:, 0, :], 0.0))
            for t in range(TT):
                link(V.tensor_tensor(tab[:, t + 1, :], total[:, t, :], tab[:, t, :], ALU.add))
            link(V.tensor_tensor_scan(tab[:, 5, :], c.ones[:, 0:N_EXP], tab[:, TT, :], 0.0, ALU.mult, ALU.add))
            link(V.tensor_tensor(tab[:, 6, :], tab[:, 5, :], tab[:, TT, :], ALU.subtract))
            link(V.tensor_tensor(pos[:, :, :], ps[2][:, 0:P].rearrange("p (t e) -> p t e", e=N_EXP),
                                 tab[:, 0:TT, :], ALU.add))
            link(V.tensor_tensor(pos[:, :, :], pos[:, :, :], tab[:, 6:7, :].to_broadcast([P, TT, N_EXP]), ALU.add))
            for j in range(2):
                link(V.tensor_tensor(prod[:, :, :], pos[:, :, :], hot[:, j, :, :], ALU.mult))
                link(V.tensor_reduce(small[:, 9 + j, :], prod[:, :, :], AX.X, ALU.add))
                V.tensor_copy(r.dest[:, j, :], small[:, 9 + j, :]).then_inc(dest_done, 1)
            dve.wait_ge(exp_done, 2)
            link(V.tensor_reduce(small[:, 6, :], gex[:, :, :], AX.X, ALU.add))
            link(V.tensor_scalar(small[:, 7, :], small[:, 3, :], 1.0, None, ALU.add))
            link(V.tensor_tensor(small[:, 8, :], small[:, 6, :], small[:, 7, :], ALU.mult))
            link(V.reciprocal(r.gate[:, 0, :], small[:, 8, :]))
            link(V.tensor_tensor(r.gate[:, 1, :], r.gate[:, 0, :], small[:, 3, :], ALU.mult))
            link(V.memset(tab[:, 7, :], 0.0))
            for b in range(1, MB_MAX):
                link(V.scalar_tensor_tensor(out=tab[:, 7, :], in0=tab[:, TT, :], scalar=float(b * MB),
                                            in1=tab[:, 7, :], op0=ALU.is_gt, op1=ALU.add))
            link(V.tensor_tensor_scan(tab[:, 0, :], c.ones[:, 0:N_EXP], tab[:, 7, :], 0.0, ALU.mult, ALU.add))
            link(V.tensor_tensor(tab[:, 1, :], tab[:, 0, :], tab[:, 7, :], ALU.subtract))
            link(V.tensor_copy(r.start[:, :], tab[0:1, 6, :]))
            link(V.tensor_copy(r.end[:, :], tab[0:1, 5, :]))
            link(V.tensor_copy(r.extra_before[:, :], tab[0:1, 1, :]))
            link(V.tensor_copy(r.extra_total[:, :], tab[0:1, 0, N_EXP - 1:N_EXP]))
            link(V.tensor_scalar(r.blocks[:, :], tab[0:1, 7, :], 1.0, None, ALU.add))

        @block.gpsimd
        def _(pool):
            for j in range(2):
                pool.wait_ge(dest_done, j + 1)
                for t in range(TT):
                    nc.gpsimd.indirect_dma_start(
                        out=xrows[0:N_ASG, :], out_offset=bass.IndirectOffsetOnAxis(ap=r.dest[:, j, t:t + 1], axis=0),
                        in_=xn[:, t, :], in_offset=None).then_inc(scattered, 16)
            pool.wait_ge(scattered, 16 * 2 * TT)


SLOTS = 3


class ExpertWeights:

    def __init__(self, c):
        self.c = c
        self.up_in = [c.lasting_sem(f"up_in{j}") for j in range(SLOTS)]
        self.down_in = [c.lasting_sem(f"down_in{j}") for j in range(SLOTS)]

    def start_layer(self, w1, w3, w2):
        self.w1_dram, self.w3_dram, self.w2_dram = w1, w3, w2
        self.w1, self.w3, self.w2 = {}, {}, {}

    def add_slot(self, ctx, j):
        self.w1[j] = self.c.sb(f"w1_{j}", [P, KD, FF], ctx=ctx, side="right")
        self.w3[j] = self.c.sb(f"w3_{j}", [P, KD, FF], ctx=ctx, side="right")
        self.w2[j] = self.c.sb(f"w2_{j}", [P, KF, D], ctx=ctx, side="right")

    def load_up(self, eng, j, e):
        eng.dma_start(self.w1[j][:, :, :], expert(self.w1_dram, e, KD)).then_inc(self.up_in[j], 16)
        eng.dma_start(self.w3[j][:, :, :], expert(self.w3_dram, e, KD)).then_inc(self.up_in[j], 16)

    def load_down(self, eng, j, e):
        eng.dma_start(self.w2[j][:, :, :], expert(self.w2_dram, e, KF)).then_inc(self.down_in[j], 16)

    def load_guest(self, eng, w_dram):
        self.guest_in = [self.c.lasting_sem(f"w_out_in{h}") for h in range(2)]
        for h, tile in enumerate(self.guest()):
            eng.dma_start(tile[:, :, :], w_dram.rearrange("(f p) n -> p f n", p=P)[:, :, h * BANK:(h + 1) * BANK]
                          ).then_inc(self.guest_in[h], 16)

    def guest(self):
        return self.w1[SLOTS - 1], self.w3[SLOTS - 1]

    def prefetch(self, slots):
        def issue(sp):
            for j in slots:
                self.load_up(sp, j, j)
                self.load_down(sp, j, j)
        return issue

    def end_layer(self, c):
        c.of_stage += self.up_in + self.down_in
        self.__init__(c)


def expert(w, e, k):
    return w[bass.ds(e, 1)].rearrange("o (p k) n -> p (o k) n", k=k)


@stage
def experts(nc, c, ctx, ps, xrows, yrows, r, gain_dram, wts):
    x_rows = [c.sb(f"x_rows{j}", [MB, D], ctx=ctx) for j in range(SLOTS)]
    y_sb = [c.sb(f"y_{j}", [P, FF], ctx=ctx) for j in range(SLOTS)]
    w1_sb, w3_sb, w2_sb, up_in, down_in = wts.w1, wts.w3, wts.w2, wts.up_in, wts.down_in
    xT = [c.sb(f"xT{b}", [P, KD, MB], ctx=ctx) for b in range(2)]
    gate_act = c.sb("gate_act", [MB, FF], ctx=ctx)
    hid = c.sb("hid", [MB, FF], ctx=ctx)
    hidT = c.sb("hidT", [P, KF, MB], ctx=ctx)
    g = c.sb("gain", [P, KD], ctx=ctx)
    ps_x, ps_h, ps_y0, ps_y1 = ps[0], ps[1], ps[2], ps[3]
    ps_1, ps_3 = ps[4:6], ps[6:8]

    gain_in = c.sem("gain_in")
    rows_in = [c.sem(f"rows_in{j}") for j in range(SLOTS)]
    stored = [c.sem(f"stored{j}") for j in range(SLOTS)]
    xT_done, xT_out = c.sem("xT_done"), c.sem("xT_out")
    up_done, silu_done, hid_done = c.sem("up_done"), c.sem("silu_done"), c.sem("hid_done")
    hidT_done, hidT_out = c.sem("hidT_done"), c.sem("hidT_out")
    down_done, y0_out, y1_out = c.sem("down_done"), c.sem("y0_out"), c.sem("y1_out")


    def turn_rows(pe, j, n, u):
        pe.wait_ge(rows_in[j], 16 * u + 16)
        nc.tensor.ldweights(c.half[:, :], tile_position=(0, 0))
        for k in range(KD):
            last = nc.tensor.transpose(ps_x[:, k * MB:(k + 1) * MB], x_rows[j][:, k::KD], c.ident[0:MB, 0:MB])
        last.then_inc(xT_done, 1)

    def up(pe, j, n, u, b):
        pe.wait_ge(xT_out, n + 1)
        pe.wait_ge(up_in[j], 32 * u + 32)
        for k in range(KD):
            nc.tensor.matmul(ps_1[b][0:MB, :], xT[b][:, k, :], w1_sb[j][:, k, :], start=k == 0, stop=k == KD - 1)
            last = nc.tensor.matmul(ps_3[b][UP:UP + MB, :], xT[b][:, k, :], w3_sb[j][:, k, :],
                                    start=k == 0, stop=k == KD - 1)
        last.then_inc(up_done, 1)

    def turn_hidden(pe, n):
        pe.wait_ge(hid_done, n + 1)
        nc.tensor.ldweights(c.half[:, :], tile_position=(0, 0))
        for k in range(KF):
            last = nc.tensor.transpose(ps_h[:, k * MB:(k + 1) * MB], hid[:, k::KF], c.ident[0:MB, 0:MB])
        last.then_inc(hidT_done, 1)

    def down(pe, j, n, u):
        pe.wait_ge(hidT_out, n + 1)
        pe.wait_ge(down_in[j], 16 * u + 16)
        pe.wait_ge(y0_out, n + 1)
        pe.wait_ge(y1_out, n + 1)
        for k in range(KF):
            nc.tensor.matmul(ps_y0[0:MB, :], hidT[:, k, :], w2_sb[j][:, k, 0:FF], start=k == 0, stop=k == KF - 1)
            last = nc.tensor.matmul(ps_y1[UP:UP + MB, :], hidT[:, k, :], w2_sb[j][:, k, FF:D], start=k == 0, stop=k == KF - 1)
        last.then_inc(down_done, 1)

    def gain_rows(dve, n, b):
        dve.wait_ge(xT_done, n + 1)
        nc.vector.tensor_tensor(xT[b][:, :, :], ps_x[:, 0:KD * MB].rearrange("p (k m) -> p k m", m=MB),
                                g[:, :].rearrange("p (k o) -> p k o", o=1).to_broadcast([P, KD, MB]),
                                ALU.mult).then_inc(xT_out, 1)

    def hidden(dve, n, b, turned):
        if turned is not None:
            dve.wait_ge(hidT_done, turned)
        dve.wait_ge(silu_done, n + 1)
        nc.vector.tensor_tensor(hid[:, :], gate_act[:, :], ps_3[b][UP:UP + MB, :], ALU.mult).then_inc(hid_done, 1)

    def right_half(dve, j, n, u):
        dve.wait_ge(down_done, n + 1)
        dve.wait_ge(stored[j], 32 * u + 32)
        nc.vector.tensor_copy(y_sb[j][UP:UP + MB, :], ps_y1[UP:UP + MB, :]).then_inc(y1_out, 1)

    def copy_hidden(act, n):
        act.wait_ge(hidT_done, n + 1)
        nc.scalar.activation(hidT[:, :, :], ps_h[:, 0:KF * MB].rearrange("p (k m) -> p k m", m=MB),
                             ACT.Copy).then_inc(hidT_out, 1)

    def silu(act, n, b):
        act.wait_ge(up_done, n + 1)
        nc.scalar.activation(gate_act[:, :], ps_1[b][0:MB, :], ACT.Silu).then_inc(silu_done, 1)

    def left_half_and_store(act, j, n, u, row, before):
        act.wait_ge(down_done, n + 1)
        act.wait_ge(stored[j], 32 * u + 32)
        nc.scalar.activation(y_sb[j][0:MB, :], ps_y0[0:MB, :], ACT.Copy).then_inc(y0_out, 1)
        act.wait_ge(y0_out, n + 2)
        act.wait_ge(y1_out, n + 2)
        before(act)
        for h in range(2):
            act.dma_start(yrows[bass.ds(row, MB), h * FF:(h + 1) * FF],
                          y_sb[j][h * UP:h * UP + MB, :]).then_inc(stored[j], 16)

    UNROLL = 2 * SLOTS
    XSLOT = N_EXP % SLOTS
    XUSES = N_EXP // SLOTS

    def steps(eng, step, first):
        rounds = (N_EXP - 1 - first) // UNROLL

        with eng.Fori(0, rounds) as i:
            for s in range(first, first + UNROLL):
                step(UNROLL * i + s, s % SLOTS, 2 * i + s // SLOTS, s % 2)
        for n in range(first + rounds * UNROLL, N_EXP):
            step(n, n % SLOTS, n // SLOTS, n % 2)

    def further(eng, step):
        more = eng.value_load(r.extra_total[0:1, 0:1], min_val=0, max_val=N_ASG // MB)
        with eng.If(more > 0):
            with eng.Fori(0, N_EXP) as e:
                blocks = eng.value_load(r.blocks[0:1, bass.ds(e, 1)], min_val=1, max_val=MB_MAX)
                done = eng.value_load(r.extra_before[0:1, bass.ds(e, 1)], min_val=0, max_val=N_ASG // MB)
                with eng.If(blocks > 1):
                    end = eng.value_load(r.end[0:1, bass.ds(e, 1)], min_val=MB, max_val=N_ASG)
                    with eng.Fori(1, blocks) as b:
                        step(e, eng.snap(done + b - 1), nc.s_assert_within(eng.snap(end - b * MB), 0, N_ASG - MB, skip_runtime_bounds_check_because="further blocks lie inside the expert's rows"))
                eng.nop()
            eng.nop()
        eng.nop()

    def row_of(eng, e):
        return eng.value_load(r.start[0:1, bass.ds(e, 1)], min_val=0, max_val=N_ASG)

    def load_rows(sp, j, row):
        sp.dma_start(x_rows[j][:, :], xrows[bass.ds(row, MB), :]).then_inc(rows_in[j], 16)

    with nc.Block() as block:

        @block.sync
        def _(sp):
            for j in range(SLOTS):
                load_rows(sp, j, row_of(sp, j))
                if j == 0:
                    sp.dma_start(g[:, :], gain_dram.rearrange("(p k) -> p k", k=KD)).then_inc(gain_in, 16)

            def load(n, j, u, b):
                sp.wait_ge(xT_done, n - SLOTS + 1)
                load_rows(sp, j, row_of(sp, n))
                sp.wait_ge(up_done, n - SLOTS + 1)
                wts.load_up(sp, j, n)
                sp.wait_ge(down_done, n - SLOTS + 1)
                wts.load_down(sp, j, n)

            steps(sp, load, SLOTS)

            def more(e, m, row):
                sp.wait_ge(down_done, m + N_EXP)
                load_rows(sp, XSLOT, row)
                wts.load_up(sp, XSLOT, e)
                wts.load_down(sp, XSLOT, e)

            further(sp, more)

        @block.tensor
        def _(pe):
            keep_warm(nc, c, ps_y0, 40)
            pe.wait_ge(gain_in, 16)
            turn_rows(pe, 0, 0, 0)
            up(pe, 0, 0, 0, 0)
            turn_rows(pe, 1, 1, 0)

            def step(n, j, u, b):
                last = isinstance(n, int) and n == N_EXP - 1
                before, uses = (j - 1) % SLOTS, u if j else u - 1
                following, next_uses = (j + 1) % SLOTS, u if j < SLOTS - 1 else u + 1
                up(pe, j, n, u, b)
                turn_hidden(pe, n - 1)
                if not last:
                    turn_rows(pe, following, n + 1, next_uses)
                down(pe, before, n - 1, uses)
                if last:
                    turn_hidden(pe, n)
                    down(pe, j, n, u)

            steps(pe, step, 1)

            def more(e, m, row):
                n, u = m + N_EXP, m + XUSES
                turn_rows(pe, XSLOT, n, u)
                up(pe, XSLOT, n, u, 0)
                turn_hidden(pe, n)
                down(pe, XSLOT, n, u)

            further(pe, more)

        @block.vector
        def _(dve):
            dve.wait_ge(gain_in, 16)
            dve.sem_inc(y1_out, 1)
            gain_rows(dve, 0, 0)
            gain_rows(dve, 1, 1)
            hidden(dve, 0, 0, None)

            def step(n, j, u, b):
                last = isinstance(n, int) and n == N_EXP - 1
                if not last:
                    gain_rows(dve, n + 1, 1 - b)
                hidden(dve, n, b, n)
                right_half(dve, (j - 1) % SLOTS, n - 1, u if j else u - 1)
                if last:
                    right_half(dve, j, n, u)

            steps(dve, step, 1)

            def more(e, m, row):
                n, u = m + N_EXP, m + XUSES
                gain_rows(dve, n, 0)
                hidden(dve, n, 0, None)
                right_half(dve, XSLOT, n, u)

            further(dve, more)

        @block.scalar
        def _(act):
            act.sem_inc(y0_out, 1)
            for s in stored:
                act.sem_inc(s, 32)

            def stored_before(j, u):
                return lambda a: a.wait_ge(stored[(j - 1) % SLOTS], 32 * (u + 1 if j else u) + 32)

            silu(act, 0, 0)

            def step(n, j, u, b):
                before, uses = (j - 1) % SLOTS, u if j else u - 1
                copy_hidden(act, n - 1)
                silu(act, n, b)
                left_half_and_store(act, before, n - 1, uses, row_of(act, n - 1), stored_before(before, uses))
                if isinstance(n, int) and n == N_EXP - 1:
                    copy_hidden(act, n)
                    left_half_and_store(act, j, n, u, row_of(act, n), stored_before(j, u))

            steps(act, step, 1)

            def more(e, m, row):
                n, u = m + N_EXP, m + XUSES
                silu(act, n, 0)
                copy_hidden(act, n)
                left_half_and_store(act, XSLOT, n, u, row, stored_before(XSLOT, XUSES))
                act.wait_ge(stored[XSLOT], 32 * m + 32 * XUSES + 64)

            further(act, more)
            for j in range(SLOTS):
                act.wait_ge(stored[j], 32 * (XUSES + (j < XSLOT)) + 32)


class Combine(InPlace):

    def __init__(self, nc, c, x, yrows, r, got):
        self.nc, self.x, self.yrows, self.r, self.got = nc, x, yrows, r, got
        self.gathered = [[c.sem(f"gathered{j}{t}") for t in range(TT)] for j in range(2)]
        self.added = c.sem("tile_added")

    def start(self, block):
        @block.gpsimd
        def _(pool):
            for t in range(TT):
                for j in range(2):
                    self.nc.gpsimd.indirect_dma_start(
                        out=self.got[j][:, t, :], out_offset=None, in_=self.yrows[0:N_ASG, :],
                        in_offset=bass.IndirectOffsetOnAxis(ap=self.r.dest[:, j, t:t + 1], axis=0)
                    ).then_inc(self.gathered[j][t], 16)

    def add_tile(self, dve, link, t):
        for j in range(2):
            dve.wait_ge(self.gathered[j][t], 16)
            link(self.nc.vector.scalar_tensor_tensor(out=self.x[:, t, :], in0=self.got[j][:, t, :],
                                                     scalar=self.r.gate[:, j, t:t + 1], in1=self.x[:, t, :],
                                                     op0=ALU.mult, op1=ALU.add))
        dve.sem_inc(self.added, 1)

    def wait_tile(self, eng, t):
        eng.wait_ge(self.added, t + 1)


class Routes:

    def __init__(self, c, ctx):
        self.gate = c.sb("gate", [P, 2, TT], ctx=ctx)
        self.dest = c.sb("dest", [P, 2, TT], U32, ctx=ctx)
        self.start = c.sb("start", [1, N_EXP], I32, ctx=ctx)
        self.end = c.sb("end", [1, N_EXP], I32, ctx=ctx)
        self.blocks = c.sb("blocks", [1, N_EXP], I32, ctx=ctx)
        self.extra_before = c.sb("extra_before", [1, N_EXP], I32, ctx=ctx)
        self.extra_total = c.sb("extra_total", [1, 1], I32, ctx=ctx)


def moe(nc, c, ps, x, yT, xrows, yrows, gain, w_group, w_expert, wts, slots, r):
    yT, y_ctx = yT
    with y_ctx, ExitStack() as ctx:
        xn = c.sb("xn", [P, TT, D], ctx=ctx)
        router(nc, c, ctx, ps, x, xn, yT, gain, w_group, w_expert, xrows, r, OutProject(nc, c, ps, x, yT, wts))
    with ExitStack() as ctx:
        experts(nc, c, ctx, ps, xrows, yrows, r, gain, wts)
        wts.end_layer(c)
    slots.close()


class Bank:

    def __init__(self, ps, filled, emptied):
        self.ps, self.filled, self.emptied, self.n = ps, filled, emptied, 0

    def open(self, pe):
        if self.n:
            pe.wait_ge(self.emptied, self.n)
        return self.ps

    def close(self, last):
        last.then_inc(self.filled, 1)
        self.n += 1

    def copied(self, pe):
        pe.wait_ge(self.emptied, self.n)

    def read(self, eng):
        self.n += 1
        eng.wait_ge(self.filled, self.n)
        return self.ps

    def empty(self, ins):
        ins.then_inc(self.emptied, 1)


def bank_sems(c, what):
    return [(c.sem(f"{what}_filled{b}"), c.sem(f"{what}_emptied{b}")) for b in range(8)]


def bank_set(ps, sems):
    return [Bank(ps[b], *sems[b]) for b in range(8)]


HIGH_BITS = -4096
GC = 256


class SplitNorm:

    def __init__(self, c, ctx, scratch):
        self.c = c
        self.high, self.low = (c.sb(n, [P, KD, T + 1], F32R, ctx=ctx) for n in ("hT_high", "hT_low"))
        self.full = [c.sb(f"hT_full{i}", [P, T], ctx=scratch) for i in range(2)]
        self.cut = [c.sb(f"hT_cut{i}", [P, T], ctx=scratch) for i in range(2)]
        self.evacuated, self.masked = c.sem("hT_evacuated"), c.sem("hT_masked")
        self.high_done, self.low_done, self.edge = c.sem("hT_high_done"), c.sem("hT_low_done"), c.sem("hT_edge")

    def ready(self, pe, k):
        pe.wait_ge(self.edge, 2)
        pe.wait_ge(self.high_done, k + 1)
        pe.wait_ge(self.low_done, k + 1)

    def evacuate(self, nc, ps):
        def add(block, g, gain_in, turned):

            @block.scalar
            def _(act):
                act.wait_ge(gain_in, 16)
                for k in range(KD + 1):
                    if k < KD:
                        act.wait_ge(turned, k + 1)
                        if k >= 2:
                            act.wait_ge(self.low_done, k - 1)
                        nc.scalar.activation(self.full[k % 2][:, :], ps[k][:, :], ACT.Copy,
                                             scale=g[:, k:k + 1]).then_inc(self.evacuated, 1)
                    if k >= 1:
                        act.wait_ge(self.masked, k)
                        nc.scalar.activation(self.high[:, k - 1, 1:T + 1], self.cut[(k - 1) % 2][:, :],
                                             ACT.Copy).then_inc(self.high_done, 1)

            @block.vector
            def _(dve):
                for half in (self.high, self.low):
                    nc.vector.tensor_scalar(half[:, :, 0:1].rearrange("p k o -> p (k o)"), c_zero(self.c), 0.0, None,
                                            ALU.mult).then_inc(self.edge, 1)
                for k in range(KD):
                    dve.wait_ge(self.evacuated, k + 1)
                    if k >= 2:
                        dve.wait_ge(self.high_done, k - 1)
                        dve.wait_ge(self.low_done, k - 1)
                    nc.vector.tensor_scalar(self.cut[k % 2][:, :].bitcast(I32), self.full[k % 2][:, :].bitcast(I32),
                                            HIGH_BITS, None, ALU.bitwise_and).then_inc(self.masked, 1)
                    dve.wait_ge(self.masked, k + 1)
                    nc.vector.tensor_tensor(self.low[:, k, 1:T + 1], self.full[k % 2][:, :], self.cut[k % 2][:, :],
                                            ALU.subtract).then_inc(self.low_done, 1)

        return add


def c_zero(c):
    return c.ident[:, 0:KD]


class SplitWeights:
    RAW = 3

    def __init__(self, nc, c, ctx, width=GC):
        self.nc = nc
        self.raw = [c.sb(f"w_raw{i}", [P, KD, width], ctx=ctx) for i in range(self.RAW)]
        self.cut = c.sb("w_cut", [P, KD, width], ctx=ctx)
        self.high = [c.sb(f"w_high{i}", [P, KD, width], F32R, ctx=ctx) for i in range(2)]
        self.low = [c.sb(f"w_low{i}", [P, KD, width], F32R, ctx=ctx) for i in range(2)]
        self.raw_in = [c.sem(f"w_raw_in{i}") for i in range(self.RAW)]
        self.masked, self.high_done, self.low_done, self.used = (
            c.sem(n) for n in ("w_masked", "w_high_done", "w_low_done", "w_used"))

    def load(self, sp, g, pieces):
        if g >= self.RAW:
            sp.wait_ge(self.low_done, g - self.RAW + 1)
        for lo, view in pieces:
            n = view.shape[-1]
            sp.dma_start(self.raw[g % self.RAW][:, :, lo:lo + n], view).then_inc(self.raw_in[g % self.RAW], 16)

    def split_low(self, dve, g, n, arrived):
        raw = self.raw[g % self.RAW]
        dve.wait_ge(self.raw_in[g % self.RAW], 16 * arrived)
        if g >= 1:
            dve.wait_ge(self.high_done, g)
            dve.wait_ge(self.low_done, g)
        self.nc.vector.tensor_scalar(self.cut[:, :, 0:n].bitcast(I32), raw[:, :, 0:n].bitcast(I32), HIGH_BITS, None,
                                     ALU.bitwise_and).then_inc(self.masked, 1)
        dve.wait_ge(self.masked, g + 1)
        if g >= 2:
            dve.wait_ge(self.used, g - 1)
        self.nc.vector.tensor_tensor(self.low[g % 2][:, :, 0:n], raw[:, :, 0:n], self.cut[:, :, 0:n],
                                     ALU.subtract).then_inc(self.low_done, 1)

    def split_high(self, act, g, n):
        act.wait_ge(self.masked, g + 1)
        if g >= 2:
            act.wait_ge(self.used, g - 1)
        self.nc.scalar.activation(self.high[g % 2][:, :, 0:n], self.cut[:, :, 0:n],
                                  ACT.Copy).then_inc(self.high_done, 1)

    def ready(self, pe, g):
        pe.wait_ge(self.high_done, g + 1)
        pe.wait_ge(self.low_done, g + 1)

    def release(self, pe, last_bank):
        pe.wait_ge(last_bank.filled, last_bank.n)
        pe.sem_inc(self.used, 1)


def three_passes(nc, out, lhsT, rhs, start, stop):
    nc.tensor.matmul(out, lhsT[0], rhs[0], start=start, stop=False)
    nc.tensor.matmul(out, lhsT[0], rhs[1], start=False, stop=False)
    return nc.tensor.matmul(out, lhsT[1], rhs[0], start=False, stop=stop)


C_HEADS = 16
RING = 6
LAG_T, LAG_PV = 4, 6


@stage
def odd_project(nc, c, ctx, ps, x, xn, gain_dram, w_dram, qT, kT, v, combine):
    NG = 3 * D // GC
    FG = GC // P
    hT = SplitNorm(c, ctx, ctx)
    w = SplitWeights(nc, c, ctx)
    sems = bank_sems(c, "qkv")
    is_v = lambda g: g >= 2 * D // GC
    outs = [(g, s) for g in range(NG) for s in range(TT if is_v(g) else FG)]

    def dest(g, s):
        if is_v(g):
            lo = g * GC - 2 * D
            return v[:, s, lo:lo + GC]
        f = FG * g + s
        return qT[:, f, :] if f < KD else kT[:, f - KD, :]

    def width(g):
        return GC if is_v(g) else T

    def empty_and_split(eng, parity, copy, split):
        banks = bank_set(ps, sems)
        split(0)
        split(1)
        for n, (g, s) in enumerate(outs):
            if n % 2 == parity:
                b = banks[n % 8]
                b.empty(copy(dest(g, s), b.read(eng)[:, 0:width(g)], HD ** -0.5 if g < D // GC else 1.0))
            if n + 1 < len(outs) and outs[n + 1][0] != g and g + 2 < NG:
                split(g + 2)

    with nc.Block() as block:
        got = [t[:, :, :].rearrange("p (t a) n -> p t (a n)", t=TT) for t in (qT, kT)]
        norm_transpose(nc, c, ctx, ps, block, x, xn, gain_dram, hT.evacuate(nc, ps), combine(got))

        @block.sync
        def _(sp):
            for g in range(NG):
                w.load(sp, g, [(0, w_dram.rearrange("(p k) n -> p k n", k=KD)[:, :, g * GC:(g + 1) * GC])])

        @block.tensor
        def _(pe):
            banks = bank_set(ps, sems)
            for n, (g, s) in enumerate(outs):
                if s == 0:
                    w.ready(pe, g)
                b = banks[n % 8]
                out = b.open(pe)
                for k in range(KD):
                    if n == 0:
                        hT.ready(pe, k)
                    wk = [h[g % 2][:, k, :] for h in (w.high, w.low)]
                    if is_v(g):
                        xk = [h[:, k, 1 + s * P:1 + (s + 1) * P] for h in (hT.high, hT.low)]
                        last = three_passes(nc, out[:, 0:GC], xk, wk, k == 0, k == KD - 1)
                    else:
                        xk = [h[:, k, 1:T + 1] for h in (hT.high, hT.low)]
                        last = three_passes(nc, out[:, :], [h[:, s * P:(s + 1) * P] for h in wk], xk,
                                            k == 0, k == KD - 1)
                b.close(last)
                if n + 1 == len(outs) or outs[n + 1][0] != g:
                    w.release(pe, b)

        @block.vector
        def _(dve):
            empty_and_split(dve, 0, lambda out, in_, scale: nc.vector.tensor_scalar(out, in_, scale, None, ALU.mult),
                            lambda g: w.split_low(dve, g, GC, g // w.RAW + 1))

        @block.scalar
        def _(act):
            empty_and_split(act, 1, lambda out, in_, scale: nc.scalar.activation(out, in_, ACT.Copy, scale=scale),
                            lambda g: w.split_high(act, g, GC))


@stage
def stick_breaking(nc, c, ctx, ps, qT, kT, v, yT, w_out, wts):
    units = [(h, t) for h in range(C_HEADS) for t in range(TT)]
    N = len(units)
    keep = [c.sb(f"keep{i}", [P, T], ctx=ctx) for i in range(RING)]
    beta = [c.sb(f"beta{i}", [P, T], ctx=ctx) for i in range(RING)]
    tail = [c.sb(f"tail{t}", [P, T + 1], ctx=ctx) for t in range(TT)]
    wT = [c.sb(f"wT{i}", [P, T], ctx=ctx) for i in range(2)]
    zero = c.sb("zero", [P, T], ctx=ctx)
    z_done, beta_done, masked = c.sem("z_done"), c.sem("beta_done"), c.sem("masked")
    scanned, weighted = c.sem("scanned"), c.sem("weighted")
    turned, wT_out, pv_done, y_out, ready = (c.sem("turned"), c.sem("wT_out"), c.sem("pv_done"),
                                             c.sem("y_out"), c.sem("stick_ready"))
    ps_z, ps_t, ps_y = ps[0:3], ps[3:5], ps[5:7]

    with nc.Block() as block:

        @block.sync
        def _(sp):
            wts.load_guest(sp, w_out)

        @block.tensor
        def _(pe):
            def scores(u):
                h, t = units[u]
                q = HD * (h % 2)
                if u >= 3:
                    pe.wait_ge(beta_done, 2 * (u - 3) + 2)
                nc.tensor.matmul(ps_z[u % 3][:, 0:(t + 1) * P], qT[q:q + HD, h // 2, t * P:(t + 1) * P],
                                 kT[q:q + HD, h // 2, 0:(t + 1) * P], start=True, stop=True).then_inc(z_done, 1)

            def turn(u):
                h, t = units[u]
                pe.wait_ge(weighted, u + 1)
                if u >= 2:
                    pe.wait_ge(wT_out, u - 1)
                for b in range(t + 1):
                    last = nc.tensor.transpose(ps_t[u % 2][:, b * P:(b + 1) * P], beta[u % RING][:, b * P:(b + 1) * P],
                                               c.ident[:, :])
                last.then_inc(turned, 1)

            def weigh(u):
                h, t = units[u]
                q = HD * (h % 2)
                pair = h // 2
                pe.wait_ge(wT_out, u + 1)
                if h % 2 == 0 and t == 0 and pair >= 2:
                    pe.wait_ge(y_out, pair - 1)
                for b in range(t + 1):
                    last = nc.tensor.matmul(ps_y[pair % 2][q:q + HD, t * P:(t + 1) * P],
                                            v[:, b, h * HD:(h + 1) * HD], wT[u % 2][:, b * P:(b + 1) * P],
                                            start=b == 0, stop=b == t)
                last.then_inc(pv_done, 1)

            for i in range(N + LAG_PV):
                if i < N:
                    scores(i)
                if 0 <= i - LAG_T < N:
                    turn(i - LAG_T)
                if 0 <= i - LAG_PV < N:
                    weigh(i - LAG_PV)

        @block.scalar
        def _(act):
            for i in range(N + LAG_T):
                if i < N:
                    h, t = units[i]
                    L = (t + 1) * P
                    act.wait_ge(z_done, i + 1)
                    if i >= RING:
                        act.wait_ge(scanned, i - RING + 1)
                        act.wait_ge(turned, i - RING + 1)
                    nc.scalar.activation(keep[i % RING][:, 0:L], ps_z[i % 3][:, 0:L], ACT.Sigmoid,
                                         scale=-1.0).then_inc(beta_done, 1)
                    nc.scalar.activation(beta[i % RING][:, 0:L], ps_z[i % 3][:, 0:L],
                                         ACT.Sigmoid).then_inc(beta_done, 1)
                u = i - LAG_T
                if u >= 0:
                    L = (units[u][1] + 1) * P
                    act.wait_ge(turned, u + 1)
                    if u >= 2:
                        act.wait_ge(pv_done, u - 1)
                    nc.scalar.activation(wT[u % 2][:, 0:L], ps_t[u % 2][:, 0:L], ACT.Copy).then_inc(wT_out, 1)

        @block.gpsimd
        def _(pool):
            for i, (h, t) in enumerate(units):
                pool.wait_ge(beta_done, 2 * i + 2)
                lo, hi = t * P, (t + 1) * P
                for buf, fill in ((keep, 1.0), (beta, 0.0)):
                    last = nc.gpsimd.affine_select(out=buf[i % RING][:, lo:hi], in_=buf[i % RING][:, lo:hi],
                                                   compare_op=ALU.is_gt, fill=fill, base=0, pattern=[[-1, P]],
                                                   channel_multiplier=1)
                last.then_inc(masked, 1)

        @block.vector
        def _(dve):
            nc.vector.memset(zero[:, :], 0.0).then_inc(ready, 1)
            for t in range(TT):
                L = (t + 1) * P
                nc.vector.memset(tail[t][:, L:L + 1], 1.0).then_inc(ready, 1)
            dve.wait_ge(ready, 1 + TT)
            for i, (h, t) in enumerate(units):
                L = (t + 1) * P
                dve.wait_ge(masked, i + 1)
                if i >= TT:
                    dve.wait_ge(weighted, i - TT + 1)
                nc.vector.tensor_tensor_scan(tail[t][:, 0:L][:, ::-1],
                                             keep[i % RING][:, 0:L][:, ::-1], zero[:, 0:L], 1.0,
                                             ALU.mult, ALU.add).then_inc(scanned, 1)
                dve.wait_ge(scanned, i + 1)
                nc.vector.tensor_tensor(beta[i % RING][:, 0:L], beta[i % RING][:, 0:L], tail[t][:, 1:L + 1],
                                        ALU.mult).then_inc(weighted, 1)
                if h % 2 == 1 and t == 1 and h >= 3:
                    pair = h // 2 - 1
                    dve.wait_ge(pv_done, 8 * (pair + 1))
                    nc.vector.tensor_copy(yT[:, pair, :], ps_y[pair % 2][:, :]).then_inc(y_out, 1)
            pair = C_HEADS // 2 - 1
            dve.wait_ge(pv_done, N)
            nc.vector.tensor_copy(yT[:, pair, :], ps_y[pair % 2][:, :]).then_inc(y_out, 1)


def odd_mixer(nc, c, ps, x, gain, w_qkv, w_out, wts, slots, combine):
    ctx = c.ctx.enter_context(ExitStack())
    yT = c.sb("yT", [P, KD, T], ctx=ctx)
    with ExitStack() as inner:
        qT = c.sb("qT", [P, KD, T], ctx=inner)
        kT = c.sb("kT", [P, KD, T], ctx=inner)
        v = c.sb("v", [P, TT, D], ctx=inner)
        with ExitStack() as proj:
            xn = c.sb("xn", [P, TT, D], ctx=proj)
            odd_project(nc, c, proj, ps, x, xn, gain, w_qkv, qT, kT, v, combine)
        wts.add_slot(slots, SLOTS - 1)
        stick_breaking(nc, c, inner, ps, qT, kT, v, yT, w_out, wts)
    for j in range(SLOTS - 1):
        wts.add_slot(slots, j)
    return yT, ctx


A_HEADS, A_WIDTH = 8, 512
B_HEADS, B_WIDTH = 8, 512
KV_RANK = 128
IDX_HEADS = 8
TOPK = min(256, T // 4)
GN_EPS = 64e-5
FT = A_WIDTH // P
CH = 64
NCH = T // CH
DECAY = math.exp(-0.5)
COLS = dict(r=0, k=512, v=1024, qb=1536, ckv=2048, qi=2176, ki=2688, wi=2752)


@stage
def even_project(nc, c, ctx, ps, x, xn, gain_dram, w_dram, m, prm, update):
    hT = SplitNorm(c, ctx, ctx)
    w = SplitWeights(nc, c, ctx)
    mu = c.sb("mu_lora", [P, 3, KD], ctx=ctx)
    less = c.sb("one_less_mu", [P, 3, FT], ctx=ctx)
    raw = [xn[:, i, 0:T + 1] for i in range(2)]
    own, prm_in = c.sem("dve_own"), c.sem("prm_in")
    raw_out, raw_read, raw_zero = c.sem("raw_out"), c.sem("raw_read"), c.sem("raw_zero")
    sems = bank_sems(c, "proj")

    def columns(name, width):
        return [(name, i * GC, GC, [P] * (GC // P)) for i in range(width // GC)]

    groups = (columns("r", A_WIDTH) + columns("k", A_WIDTH) + columns("v", A_WIDTH) + columns("qb", B_WIDTH)
              + columns("qi", IDX_HEADS * HD) + [("misc", 0, GC, [P, P]), ("wi", 0, IDX_HEADS, [IDX_HEADS]),
                                                 ("da", 0, GC, [P]), ("gate", 0, GC, [P])])
    NG = len(groups)
    wv = w_dram.rearrange("(p k) n -> p k n", k=KD)
    wide = lambda ap: ap.rearrange("(p k) n -> p k n", k=KD)

    def pieces(g):
        name, lo, n, _ = groups[g]
        if name == "misc":
            ki = wv[:, :, COLS["ki"]:COLS["ki"] + HD]
            return [(0, wv[:, :, COLS["ckv"]:COLS["ckv"] + KV_RANK]), (P, ki), (P + HD, ki)]
        if name == "da":
            return [(0, wide(prm["w1"])), (HD, wide(prm["a1"]))]
        if name == "gate":
            return [(0, wide(prm["g1"]))]
        return [(0, wv[:, :, COLS[name] + lo:COLS[name] + lo + n])]

    def arrived(g):
        return sum(len(pieces(i)) for i in range(g % w.RAW, g + 1, w.RAW))

    with nc.Block() as block:
        norm_transpose(nc, c, ctx, ps, block, x, xn, gain_dram, hT.evacuate(nc, ps), update)

        @block.sync
        def _(sp):
            for g in range(NG):
                w.load(sp, g, pieces(g))
                if g == 2:
                    sp.dma_start(mu[:, :, :], prm["mu_lora"].rearrange("m (p k) -> p m k", k=KD)).then_inc(prm_in, 16)
                    for i in range(3):
                        sp.dma_start(m.mu[:, i, :], prm["mu_rkv"][i].rearrange("(f p) -> p f", p=P),
                                     allow_slow_non_contiguous=True).then_inc(prm_in, 16)

        @block.tensor
        def _(pe):
            banks = bank_set(ps, sems)
            n = 0
            for g, (name, _, _, tiles) in enumerate(groups):
                w.ready(pe, g)
                for f, rows in enumerate(tiles):
                    b = banks[n % 8]
                    out = b.open(pe)
                    shifts = 2 if name in ("da", "gate") else 1
                    for s in range(shifts):
                        lo = (f + s) * P
                        for k in range(KD):
                            if n == 0:
                                hT.ready(pe, k)
                            last = three_passes(nc, out[0:rows, :],
                                                [h[g % 2][:, k, lo:lo + rows] for h in (w.high, w.low)],
                                                [h[:, k, 1 - s:T + 1 - s] for h in (hT.high, hT.low)],
                                                s == 0 and k == 0, s == shifts - 1 and k == KD - 1)
                    b.close(last)
                    n += 1
                w.release(pe, b)

        @block.scalar
        def _(act):
            banks = bank_set(ps, sems)
            jobs = [0]

            def take():
                b = banks[jobs[0] % 8]
                jobs[0] += 1
                return b, b.read(act)

            def plain(dest, scale=1.0):
                b, out = take()
                b.empty(nc.scalar.activation(dest, out[0:dest.shape[0], :], ACT.Copy, scale=scale))

            w.split_high(act, 0, groups[0][2])
            w.split_high(act, 1, groups[1][2])
            act.wait_ge(raw_zero, 1)
            for g, (name, lo, _, tiles) in enumerate(groups):
                for f in range(len(tiles)):
                    if name in ("r", "k", "v"):
                        n = jobs[0]
                        b, out = take()
                        if n >= 2:
                            act.wait_ge(raw_read, n - 1)
                        b.empty(nc.scalar.activation(raw[n % 2][:, 1:T + 1], out[:, :], ACT.Copy))
                        act.wait_ge(b.emptied, b.n)
                        act.sem_inc(raw_out, 1)
                    elif name in ("qb", "qi"):
                        dest = m.qb if name == "qb" else m.qi
                        plain(dest[:, lo // P + f, :], HD ** -0.5)
                    elif name == "misc":
                        plain((m.ck, m.ki)[f][:, :])
                    elif name == "wi":
                        plain(m.wiT[:, :], IDX_HEADS ** -0.5)
                    elif name == "da":
                        b, out = take()
                        nc.scalar.activation(m.lo_da[0:HD, :], out[0:HD, :], ACT.Tanh)
                        b.empty(nc.scalar.activation(m.lo_da[HD:P, :], out[HD:P, :], ACT.Copy))
                    else:
                        b, out = take()
                        b.empty(nc.scalar.activation(m.lo_g[:, :], out[:, :], ACT.Sigmoid))
                if g + 2 < NG:
                    w.split_high(act, g + 2, groups[g + 2][2])

        @block.vector
        def _(dve):
            link = chain(dve, own)

            def mix_weights(g):
                slot = w.raw[g % w.RAW]
                dve.wait_ge(w.raw_in[g % w.RAW], 16 * arrived(g))
                for lo, n, i in ((0, HD, 0), (HD, HD, 1)) if groups[g][0] == "da" else ((0, P, 2),):
                    mub = mu[:, i, :].rearrange("p (k o) -> p k o", o=1).to_broadcast([P, KD, n])
                    link(nc.vector.tensor_tensor(slot[:, :, P + lo:P + lo + n], slot[:, :, lo:lo + n], mub, ALU.mult))
                    link(nc.vector.tensor_tensor(slot[:, :, lo:lo + n], slot[:, :, lo:lo + n],
                                                 slot[:, :, P + lo:P + lo + n], ALU.subtract))

            def split(g):
                if groups[g][0] in ("da", "gate"):
                    mix_weights(g)
                w.split_low(dve, g, groups[g][2], arrived(g))

            link(nc.vector.memset(raw[0][:, 0:1], 0.0))
            nc.vector.memset(raw[1][:, 0:1], 0.0).then_inc(raw_zero, 1)
            split(0)
            split(1)
            dve.wait_ge(prm_in, 16 * 4)
            link(nc.vector.tensor_scalar(less[:, :, :], m.mu[:, :, :], -1.0, 1.0, ALU.mult, ALU.add))
            n = 0
            for g, (name, _, _, tiles) in enumerate(groups):
                for f in range(len(tiles) if name in ("r", "k", "v") else 0):
                    i, fz = n // FT, n % FT
                    z = m.rkv[i][:, fz, :]
                    dve.wait_ge(raw_out, n + 1)
                    link(nc.vector.tensor_scalar(z, raw[n % 2][:, 1:T + 1], less[:, i, fz:fz + 1], None, ALU.mult))
                    nc.vector.scalar_tensor_tensor(out=z, in0=raw[n % 2][:, 0:T], scalar=m.mu[:, i, fz:fz + 1], in1=z,
                                                   op0=ALU.mult, op1=ALU.add).then_inc(raw_read, 1)
                    n += 1
                if g + 2 < NG:
                    split(g + 2)


N_SUM = 34
LAT = 32


@stage
def mixers_prepare(nc, c, ctx, ps, m, prm):
    R, K, V = m.rkv
    w2a2 = c.sb("w2a2", [P, A_WIDTH], ctx=ctx)
    g2 = c.sb("g2", [P, A_WIDTH], ctx=ctx)
    vec = c.sb("vec", [P, 5, FT], ctx=ctx)
    dec, inv = (c.sb(n, [P, FT, T], ctx=ctx) for n in ("decay", "inverse_W"))
    sq = c.sb("squares", [P, FT + 2, T], ctx=ctx)
    rl = [sq[:, i, :] for i in range(FT + 2)]
    RL = len(rl)
    sel = c.sb("select", [P, FT + 2, N_SUM], ctx=ctx)
    selT = c.sb("selectT", [N_SUM, FT + 2, P], ctx=ctx)
    norm = c.sb("norm", [N_SUM, T], ctx=ctx)
    wkv = c.sb("w_kv_up", [P, 2 * B_WIDTH], ctx=ctx)
    gkv = c.sb("kv_gain", [P, 1], ctx=ctx)
    gki = c.sb("ki_gain", [P, 1], ctx=ctx)
    restart = m.bonus

    less_ka = c.sb("less_ka", [P, FT], ctx=ctx)
    lora_in, kk_in, vec_in, kv_in = c.sem("lora_in"), c.sem("k_k_in"), c.sem("vec_in"), c.sem("kv_in")
    less_made, factor_done, rated, inv_done = (c.sem(n) for n in ("less_made", "factor_done", "rated", "inv_done"))
    own, own_pool = c.sem("dve_own"), c.sem("pool_own")
    sel_made, sq_done, clamped, root, inverted = (c.sem(n) for n in ("sel_made", "sq_done", "clamped", "root",
                                                                     "inverted"))
    decays, km_done, bonus_in, W_done, normed = (c.sem(n) for n in ("decays", "km_done", "bonus_in", "W_done",
                                                                    "normed"))
    relu, added, scored, zeroed = c.sem("relu"), c.sem("added"), c.sem("scored"), c.sem("zeroed")
    sems = bank_sems(c, "prep")
    ACT_BANKS, DVE_BANKS = (1, 2, 3, 4), (0, 5, 6, 7)
    tiles = [3, 2, 1]
    units = [(t, h) for t in tiles for h in range(IDX_HEADS)]
    V_, G_ = nc.vector, nc.gpsimd

    def rounds(banks, which):
        n = [0]

        def following():
            n[0] += 1
            return banks[which[(n[0] - 1) % len(which)]]

        return following

    with nc.Block() as block:

        @block.sync
        def _(sp):
            for i, name in ((2, "k_k"), (0, "w0"), (1, "a0"), (3, "k_a"), (4, "r_k")):
                sp.dma_start(vec[:, i, :], prm[name].rearrange("(f p) -> p f", p=P),
                             allow_slow_non_contiguous=True).then_inc(kk_in if name == "k_k" else vec_in, 16)
            sp.dma_start(w2a2[0:HD, :], prm["w2"]).then_inc(lora_in, 16)
            sp.dma_start(w2a2[HD:P, :], prm["a2"]).then_inc(lora_in, 16)
            sp.dma_start(g2[:, :], prm["g2"]).then_inc(lora_in, 16)
            sp.dma_start(gkv[:, :], prm["kv_norm"].rearrange("(p o) -> p o", o=1)).then_inc(kv_in, 16)
            for i in range(2):
                sp.dma_start(gki[i * HD:(i + 1) * HD, :],
                             prm["idx_k_norm"].rearrange("(p o) -> p o", o=1)).then_inc(kv_in, 16)
            sp.dma_start(wkv[:, :], prm["w_kv_up"]).then_inc(kv_in, 16)

        @block.tensor
        def _(pe):
            banks = bank_set(ps, sems)
            act_bank, dve_bank = rounds(banks, ACT_BANKS), rounds(banks, DVE_BANKS)

            def one(b, lhsT, rhs):
                out = b.open(pe)
                b.close(nc.tensor.matmul(out[:, 0:rhs.shape[-1]], lhsT, rhs, start=True, stop=True))

            def back(i):
                one(dve_bank(), selT[:, i, :], norm[:, :])

            b = dve_bank()
            out = b.open(pe)
            for t in range(TT):
                last = nc.tensor.transpose(out[:, t * IDX_HEADS:(t + 1) * IDX_HEADS], m.wiT[:, t * P:(t + 1) * P],
                                           c.ident[0:IDX_HEADS, 0:IDX_HEADS])
            b.close(last)
            keep_warm(nc, c, ps[7], 30)
            pe.wait_ge(sel_made, 1)
            b = dve_bank()
            out = b.open(pe)
            for n, i in enumerate((FT, FT + 1, *range(FT))):
                pe.wait_ge(sq_done, n + 1)
                last = nc.tensor.matmul(out[0:N_SUM, :], sel[:, i, :], sq[:, i, :], start=n == 0, stop=n == FT + 1)
            b.close(last)
            pe.wait_ge(lora_in, 48)
            for half, p in enumerate((slice(0, HD), slice(HD, P))):
                for f in range(FT):
                    one(act_bank(), w2a2[p, f * P:(f + 1) * P], m.lo_da[p, :])
                if half == 0:
                    keep_warm(nc, c, ps[7], 30)
                    pe.wait_ge(inverted, 1)
                    for i in (FT, FT + 1, *range(FT)):
                        back(i)
            for f in range(FT):
                one(act_bank(), g2[:, f * P:(f + 1) * P], m.lo_g[:, :])
            pe.wait_ge(kv_in, 64)
            pe.wait_ge(normed, 1)
            for f in range(FT):
                one(act_bank(), wkv[:, f * P:(f + 1) * P], m.ck[:, :])
            for t in range(TT):
                one(act_bank(), m.ck[:, t * P:(t + 1) * P], wkv[:, B_WIDTH:2 * B_WIDTH])
            pe.wait_ge(normed, 2)
            for u, (t, h) in enumerate(units):
                if u % RL == 0:
                    pe.wait_ge(bonus_in, u // RL + 1)
                    one(dve_bank(), c.headones[:, :], m.bonus[:, u // RL, :])
                q = slice((h % 2) * HD, (h % 2 + 1) * HD)
                one(act_bank(), m.qi[q, h // 2, t * P:(t + 1) * P], m.ki[q, 0:(t + 1) * P])

        @block.scalar
        def _(act):
            banks = bank_set(ps, sems)
            following = rounds(banks, ACT_BANKS)
            A_ = nc.scalar.activation
            A_(sq[:, FT, :], m.ck[:, :], ACT.Square).then_inc(sq_done, 1)
            A_(sq[:, FT + 1, :], m.ki[:, :], ACT.Square).then_inc(sq_done, 1)
            act.wait_ge(kk_in, 16)
            for f in range(FT):
                A_(sq[:, f, :], K[:, f, :], ACT.Square, scale=vec[:, 2, f:f + 1]).then_inc(sq_done, 1)

            act.wait_ge(clamped, 2)
            A_(norm[:, :], norm[:, :], ACT.Sqrt).then_inc(root, 1)
            act.wait_ge(vec_in, 16 * 4)

            def sigmoids(dest, i):
                for f in range(FT):
                    b = following()
                    out = b.read(act)
                    b.empty(A_(dest[:, f, :], out[:, :], ACT.Sigmoid, bias=vec[:, i, f:f + 1]))

            sigmoids(dec, 0)
            sigmoids(m.rate, 1)
            for b in ACT_BANKS:
                act.wait_ge(banks[b].emptied, 2)
            A_(dec[:, :, :], dec[:, :, :], ACT.Exp, scale=-DECAY).then_inc(decays, 1)
            act.wait_ge(less_made, 1)
            for f in range(FT):
                A_(m.kmod[:, f, :], m.rate[:, f, :], ACT.Identity, scale=vec[:, 3, f:f + 1],
                   bias=less_ka[:, f:f + 1]).then_inc(factor_done, 1)
            for dest in (m.gate, m.kb, m.vb):
                for f in range(FT):
                    b = following()
                    b.empty(A_(dest[:, f, :], b.read(act)[:, :], ACT.Copy))
            act.wait_ge(clamped, 2)
            for u, (t, h) in enumerate(units):
                L = (t + 1) * P
                b = following()
                if u >= RL:
                    act.wait_ge(added, u - RL + 1)
                b.empty(A_(rl[u % RL][:, 0:L], b.read(act)[:, 0:L], ACT.Relu))
                act.wait_ge(b.emptied, b.n)
                act.sem_inc(relu, 1)

        @block.gpsimd
        def _(pool):
            link = chain(pool, own_pool)
            link(G_.memset(sel[:, :, :], 0.0))
            for half in range(2):
                p = slice(half * HD, (half + 1) * HD)
                link(G_.affine_select(out=sel[p, 0:FT, :], in_=sel[p, 0:FT, :], compare_op=ALU.not_equal, fill=1.0,
                                      base=-half, pattern=[[-2, FT], [1, N_SUM]], channel_multiplier=0))
            for i in range(2):
                link(G_.memset(sel[:, FT + i, LAT + i:LAT + i + 1], 1.0 / P))
            pool.sem_inc(sel_made, 1)
            link(G_.memset(selT[:, :, :], 0.0))
            heads = selT[:, 0:FT, :].rearrange("h f (a n) -> h (f a) n", a=2)
            link(G_.affine_select(out=heads, in_=heads, compare_op=ALU.not_equal, fill=1.0, base=0,
                                  pattern=[[-1, A_HEADS], [0, HD]], channel_multiplier=1))
            link(G_.affine_select(out=selT[:, FT:, :], in_=selT[:, FT:, :], compare_op=ALU.not_equal, fill=1.0,
                                  base=-LAT, pattern=[[-1, 2], [0, P]], channel_multiplier=1))
            pool.sem_inc(sel_made, 1)
            link(G_.memset(restart[:, :, :], 0.0))
            pool.sem_inc(sel_made, 1)
            link(G_.memset(m.bias[:, 0, :], 0.0))
            link(G_.affine_select(out=m.bias[:, 0, 0:P], in_=m.bias[:, 0, 0:P], compare_op=ALU.is_ge, fill=NEG, base=0,
                                  pattern=[[-1, P]], channel_multiplier=1))
            pool.wait_ge(vec_in, 16 * 4)
            pool.wait_ge(W_done, 1)
            for f in range(FT):
                pool.wait_ge(km_done, f + 1)
                link(G_.tensor_tensor(m.bonus[:, f, :], R[:, f, :], m.kmod[:, f, :], ALU.mult))
                G_.tensor_scalar(m.bonus[:, f, :], m.bonus[:, f, :], vec[:, 4, f:f + 1], None,
                                 ALU.mult).then_inc(bonus_in, 1)
            pool.wait_ge(bonus_in, FT)
            for f in range(FT):
                pool.wait_ge(rated, f + 1)
                kkc = m.kk[:, f, :].rearrange("p (c i) -> p c i", i=CH)
                Wc = m.W[:, f, :].rearrange("p (c i) -> p c i", i=CH)
                G_.tensor_tensor(kkc[:, :, 1:CH], kkc[:, :, 1:CH], Wc[:, :, 0:CH - 1], ALU.mult)
                G_.tensor_tensor(R[:, f, :], R[:, f, :], m.W[:, f, :], ALU.mult)
                pool.wait_ge(inv_done, f + 1)
                G_.tensor_tensor(m.kmod[:, f, :], m.kmod[:, f, :], inv[:, f, :], ALU.mult)
            for i, t in enumerate(tiles):
                pool.wait_ge(scored, i + 1)
                part = m.bias[:, t, t * P:(t + 1) * P]
                G_.affine_select(out=part, in_=part, compare_op=ALU.is_ge, fill=NEG, base=0,
                                 pattern=[[-1, P]], channel_multiplier=1)

        @block.vector
        def _(dve):
            banks = bank_set(ps, sems)
            following = rounds(banks, DVE_BANKS)
            link = chain(dve, own)
            b = following()
            b.empty(V_.tensor_copy(m.wi[:, :, :], b.read(dve)[:, 0:TT * IDX_HEADS].rearrange("p (t h) -> p t h", t=TT)))
            b = following()
            out = b.read(dve)
            V_.tensor_scalar(norm[0:LAT, :], out[0:LAT, :], 1e-12, None, ALU.max).then_inc(clamped, 1)
            ins = V_.tensor_scalar(norm[LAT:N_SUM, :], out[LAT:N_SUM, :], RMS_EPS, None, ALU.add)
            b.empty(ins)
            dve.wait_ge(b.emptied, b.n)
            dve.sem_inc(clamped, 1)
            dve.wait_ge(root, 1)
            dve.wait_ge(sel_made, 2)
            V_.reciprocal(norm[:, :], norm[:, :]).then_inc(inverted, 1)
            dve.wait_ge(inverted, 1)
            dve.wait_ge(vec_in, 16 * 4)
            link(V_.tensor_scalar(less_ka[:, :], vec[:, 3, :], -1.0, 1.0, ALU.mult, ALU.add))
            dve.sem_inc(less_made, 1)
            dve.wait_ge(kv_in, 64)
            for x, g in ((m.ck, gkv), (m.ki, gki)):
                b = following()
                ins = V_.scalar_tensor_tensor(out=x[:, :], in0=x[:, :], scalar=g[:, 0:1], in1=b.read(dve)[:, :],
                                              op0=ALU.mult, op1=ALU.mult)
                b.empty(ins)
                dve.wait_ge(b.emptied, b.n)
                dve.sem_inc(normed, 1)
            for f in range(FT):
                b = following()
                b.empty(V_.scalar_tensor_tensor(out=m.kk[:, f, :], in0=K[:, f, :], scalar=vec[:, 2, f:f + 1],
                                                in1=b.read(dve)[:, :], op0=ALU.mult, op1=ALU.mult))
                dve.wait_ge(b.emptied, b.n)

            dve.wait_ge(decays, 1)
            dve.wait_ge(sel_made, 3)
            first = lambda t: t[:, :, :].rearrange("p f (c i) -> p (f c) i", i=CH)[:, :, 0:1]
            flat = lambda t: t[:, :, :].rearrange("p f n -> p (f n)")
            link(V_.tensor_copy(first(restart), first(dec)))
            link(V_.memset(first(dec), 0.0))
            link(V_.tensor_tensor_scan(flat(m.W), flat(dec), flat(restart), 0.0, ALU.mult, ALU.add))
            dve.sem_inc(W_done, 1)
            for f in range(FT):
                dve.wait_ge(factor_done, f + 1)
                V_.tensor_tensor(m.kmod[:, f, :], m.kmod[:, f, :], K[:, f, :], ALU.mult).then_inc(km_done, 1)
            for f in range(FT):
                V_.tensor_tensor(m.rate[:, f, :], m.rate[:, f, :], m.kk[:, f, :], ALU.mult).then_inc(rated, 1)

            def products(f):
                link(V_.reciprocal(inv[:, f, :], m.W[:, f, :]))
                dve.sem_inc(inv_done, 1)
                dve.wait_ge(rated, f + 1)
                link(V_.tensor_tensor(m.rate[:, f, :], m.rate[:, f, :], inv[:, f, :], ALU.mult))

            products(0)
            def bonus(f):
                b = following()
                b.empty(V_.tensor_tensor(m.bonus[:, f, :], b.read(dve)[:, :], V[:, f, :], ALU.mult))

            for u, (t, h) in enumerate(units):
                if u % RL == 0:
                    bonus(u // RL)
                if u % RL == 3 and u // RL + 1 < FT:
                    products(u // RL + 1)
                L = (t + 1) * P
                s, r = m.bias[:, t, 0:L], rl[u % RL][:, 0:L]
                dve.wait_ge(relu, u + 1)
                if h == 0:
                    V_.tensor_scalar(s, r, m.wi[:, t, h:h + 1], None, ALU.mult).then_inc(added, 1)
                else:
                    dve.wait_ge(added, u)
                    V_.scalar_tensor_tensor(out=s, in0=r, scalar=m.wi[:, t, h:h + 1], in1=s,
                                            op0=ALU.mult, op1=ALU.add).then_inc(added, 1)
                if h == IDX_HEADS - 1:
                    dve.wait_ge(added, u + 1)
                    dve.sem_inc(scored, 1)


PER_LEVEL, AT_LEVEL_4 = (4, 4, 5, 6), (1, 1, 2, 2)


class TopK:
    ROUNDS = TOPK // 8

    def __init__(self, nc, c, ctx, m):
        self.nc, self.m, self.r = nc, m, 0
        self.best = c.sb("best", [P, 8], ctx=ctx)
        self.own, self.done = c.sem("search_own"), 0

    def rounds(self, dve, n):
        V_ = self.nc.vector

        def link(ins):
            self.done += 1
            ins.then_inc(self.own, 1)
            dve.wait_ge(self.own, self.done)

        for _ in range(n):
            if self.r == (TT - 1) * self.ROUNDS:
                return
            t = TT - 1 - self.r // self.ROUNDS
            s = self.m.bias[:, t, 0:(t + 1) * P]
            link(V_.max(self.best[:, :], s))
            link(V_.match_replace(s, self.best[:, :], s, TAKEN))
            self.r += 1
            if self.r % self.ROUNDS == 0:
                link(V_.tensor_scalar(s, s, TAKEN / 2, NEG, ALU.is_gt, ALU.mult))

    def rest(self, dve):
        self.rounds(dve, (TT - 1) * self.ROUNDS)


class Finish:

    def __init__(self, nc, c, ctx, m, yT):
        self.nc, self.c, self.m, self.yT = nc, c, m, yT
        self.vec = c.sb("ln", [P, 2, FT], ctx=ctx)
        self.sq = c.sb("centred_square", [P, FT, P], ctx=ctx)
        self.std = c.sb("std", [P, FT, P], ctx=ctx)
        (self.vec_in, self.centred, self.squared, self.eps_added, self.rooted, self.inverted, self.own) = (
            c.sem(n) for n in ("ln_in", "centred", "squared", "eps_added", "rooted", "std_inverted", "finish_own"))
        self.linked, self.tile = 0, 0

    def y(self, t):
        return self.yT[:, 0:FT, t * P:(t + 1) * P]

    def load(self, sp, prm):
        for i, name in enumerate(("ln_g", "ln_b")):
            sp.dma_start(self.vec[:, i, :], prm[name].rearrange("(f p) -> p f", p=P),
                         allow_slow_non_contiguous=True).then_inc(self.vec_in, 16)

    def sums(self, pe, b, t):
        out = b.open(pe)
        b.close(self.nc.tensor.matmul(out[:, :], self.c.headones[:, :], self.y(t), start=True, stop=True))

    def centre(self, dve, b, n):
        o = b.read(dve)[:, :].rearrange("p (f n) -> p f n", f=FT)
        b.empty(self.nc.vector.scalar_tensor_tensor(out=self.y(n), in0=o, scalar=-1.0 / HD, in1=self.y(n),
                                                    op0=ALU.mult, op1=ALU.add))
        dve.wait_ge(b.emptied, b.n)
        dve.sem_inc(self.centred, 1)

    def square(self, pool, n, first=0):
        pool.wait_ge(self.centred, n - first + 1)
        self.nc.gpsimd.tensor_tensor(self.sq[:, :, :], self.y(n), self.y(n), ALU.mult).then_inc(self.squared, 1)

    def variances(self, pe, b, n, first=0):
        pe.wait_ge(self.squared, n - first + 1)
        out = b.open(pe)
        b.close(self.nc.tensor.matmul(out[:, :], self.c.headones[:, :], self.sq[:, :, :], start=True, stop=True))

    def add_eps(self, dve, b, n):
        o = b.read(dve)[:, :].rearrange("p (f n) -> p f n", f=FT)
        if self.linked:
            dve.wait_ge(self.own, self.linked)
        b.empty(self.nc.vector.tensor_scalar(self.std[:, :, :], o, 1.0 / HD, GN_EPS, ALU.mult, ALU.add))
        dve.wait_ge(b.emptied, b.n)
        dve.sem_inc(self.eps_added, 1)

    def root(self, act, n, first=0):
        act.wait_ge(self.eps_added, n - first + 1)
        self.nc.scalar.activation(self.std[:, :, :], self.std[:, :, :], ACT.Sqrt).then_inc(self.rooted, 1)

    def invert(self, dve, n, first=0):
        dve.wait_ge(self.rooted, n - first + 1)
        self.nc.vector.reciprocal(self.std[:, :, :], self.std[:, :, :]).then_inc(self.inverted, 1)
        self.linked += 5

    def scale(self, eng, n, first=0):
        op = (self.nc.gpsimd if eng.engine == self.nc.gpsimd.engine else self.nc.vector).tensor_tensor
        y, tok = self.y(n), slice(n * P, (n + 1) * P)
        eng.wait_ge(self.vec_in, 32)
        eng.wait_ge(self.inverted, n - first + 1)
        for i, (other, how) in enumerate(((self.std[:, :, :], ALU.mult), (self.wide(0), ALU.mult),
                                          (self.wide(1), ALU.add), (self.m.bonus[:, :, tok], ALU.add),
                                          (self.m.gate[:, :, tok], ALU.mult))):
            op(y, y, other, how).then_inc(self.own, 1)
            eng.wait_ge(self.own, 5 * (n - first) + i + 1)

    def wide(self, i):
        return self.vec[:, i, :].rearrange("p (f o) -> p f o", o=1).to_broadcast([P, FT, P])


@stage
def rwkv_chunks(nc, c, ctx, ps, m, yT, prm):
    fin = Finish(nc, c, ctx, m, yT)
    search = TopK(nc, c, ctx, m)
    al, be, ka, rho, V, W = m.kk, m.rate, m.kmod, m.rkv[0], m.rkv[2], m.W
    LEVELS = CH.bit_length() - 2
    mask = c.sb("mask", [P, 4, P], ctx=ctx)
    grams = ["AT", "QbT", "NT", "QkT", "A"]
    G = {g: c.sb(g, [P, 2, FT, P], ctx=ctx) for g in ("QbT", "NT", "QkT")}
    A = [c.sb(f"A{i}", [P, 2, FT, P], ctx=ctx) for i in range(2)]
    AT = [c.sb(f"AT{i}", [P, 2, FT, P], ctx=ctx) for i in range(2)]
    XT = c.sb("XT", [P, 2, FT, P], ctx=ctx)
    Cm = c.sb("Cm", [P, 2, FT, P], ctx=ctx)
    vt, kt, bt = (c.sb(n, [P, FT, P], ctx=ctx) for n in ("v_tok", "kappa_tok", "beta_tok"))
    U0, Wt, nU = (c.sb(n, [P, FT, P], ctx=ctx) for n in ("U0", "Walpha", "minusU"))
    WT = c.sb("WalphaT", [P, FT, P], ctx=ctx)
    Wend = [c.sb(f"W_end{s}", [P, FT, P], ctx=ctx) for s in range(2)]
    Wend_done, state_done = c.sem("Wend_done"), c.sem("state_done")
    S = c.sb("state", [P, FT, P], ctx=ctx)
    made, own, x_ready, mask_ready = c.sem("masks_made"), c.sem("dve_own"), c.sem("XT_ready"), c.sem("mask_ready")
    gram_out, s_ready, vt_out = c.sem("gram_out"), c.sem("state_ready"), c.sem("vt_out")
    sems = bank_sems(c, "chunk")

    def heads():
        return [(par, f) for par in range(2) for f in range(FT)]

    with nc.Block() as block:

        @block.sync
        def _(sp):
            fin.load(sp, prm)

        @block.gpsimd
        def _(pool):
            link = chain(pool, made)
            G_ = nc.gpsimd
            for i, (cmp, sign, chan) in enumerate(((ALU.is_gt, -1.0, -1), (ALU.is_gt, -1.0, 1),
                                                   (ALU.is_gt, 1.0, -1), (ALU.is_ge, 1.0, -1))):
                link(G_.memset(mask[:, i, :], sign))
                link(G_.affine_select(out=mask[:, i, :], in_=mask[:, i, :], compare_op=cmp, fill=0.0, base=0,
                                      pattern=[[-chan, P]], channel_multiplier=chan))
                link(G_.memset(mask[0:CH, i, CH:P], 0.0))
                link(G_.memset(mask[CH:P, i, 0:CH], 0.0))
            link(G_.memset(S[:, :, :], 0.0))
            pool.sem_inc(mask_ready, 1)
            for t in range(TT):
                for par in range(2):
                    pool.wait_ge(gram_out, 2 * t + par + 1)
                    G_.tensor_tensor(XT[:, par, :, :], AT[0][:, par, :, :],
                                     c.ident[:, :].rearrange("p (o n) -> p o n", o=1).to_broadcast([P, FT, P]),
                                     ALU.add).then_inc(x_ready, 1)
                if t:
                    pool.wait_ge(state_done, 2 * t)
                for s in range(2):
                    end = t * P + (s + 1) * CH - 1
                    G_.tensor_tensor(Wend[s][:, :, :], W[:, :, end:end + 1].to_broadcast([P, FT, P]),
                                     c.headones[:, :].rearrange("p (o n) -> p o n", o=1).to_broadcast([P, FT, P]),
                                     ALU.mult).then_inc(Wend_done, 1)
                if t:
                    fin.square(pool, t - 1)
                    fin.scale(pool, t - 1)

        @block.tensor
        def _(pe):
            B = bank_set(ps, sems)
            M = nc.tensor.matmul

            def four(b, one):
                out = b.open(pe)
                for f in range(FT):
                    last = one(out[:, f * P:(f + 1) * P], f)
                b.close(last)

            def mm(lhsT, rhs):
                return lambda out, f: M(out, lhsT(f), rhs(f), start=True, stop=True)

            pe.wait_ge(mask_ready, 1)
            for t in range(TT):
                tok = slice(t * P, (t + 1) * P)
                for b, src in ((B[0], V), (B[4], ka), (B[1], be), (B[5], al)):
                    four(b, lambda out, f: nc.tensor.transpose(out, src[:, f, tok], c.ident[:, :]))
                n = 0
                for par in range(2):
                    q = slice(par * HD, (par + 1) * HD)
                    for g in grams:
                        l, r = dict(AT=(be, al), QbT=(be, rho), NT=(ka, al), QkT=(ka, rho), A=(al, be))[g]
                        four(B[(2 + n) % 4], mm(lambda f: l[q, f, tok], lambda f: r[q, f, tok]))
                        n += 1
                if t:
                    B[5].copied(pe)
                    fin.sums(pe, B[2], t - 1)
                for b in (B[0], B[1], B[3]):
                    b.copied(pe)
                for lv in range(1, LEVELS + 1):
                    old, new = (lv - 1) % 2, lv % 2
                    for par in range(2):
                        four(B[4 + par], mm(lambda f: AT[old][:, par, f, :], lambda f: A[old][:, par, f, :]))
                        if lv < LEVELS:
                            four(B[6 + par], mm(lambda f: A[old][:, par, f, :], lambda f: AT[old][:, par, f, :]))
                    if t and lv == 2:
                        fin.variances(pe, B[3], t - 1)
                    if lv == 4:
                        for par in range(2):
                            four(B[2 + par], mm(lambda f: G["NT"][:, par, f, :], lambda f: vt[:, f, :]))
                    for par in range(2):
                        B[4 + par].copied(pe)
                        if lv == 1:
                            pe.wait_ge(x_ready, 2 * t + par + 1)
                        else:
                            B[par].copied(pe)
                        four(B[par], mm(lambda f: A[new][:, par, f, :], lambda f: XT[:, par, f, :]))
                        if lv < LEVELS:
                            B[6 + par].copied(pe)
                for par in range(2):
                    B[2 + par].copied(pe)
                    B[par].copied(pe)
                    B[5].copied(pe)
                    four(B[par], mm(lambda f: XT[:, par, f, :], lambda f: Cm[:, par, f, :]))
                y = B[5].open(pe)
                for par, f in heads():
                    q = slice(par * HD, (par + 1) * HD)
                    M(y[q, f * P:(f + 1) * P], vt[:, f, q], G["QkT"][:, par, f, :],
                      start=f == 0, stop=False, skip_group_check=True)
                B[0].copied(pe)
                B[1].copied(pe)
                four(B[4], lambda out, f: nc.tensor.transpose(out, Wt[:, f, :], c.ident[:, :]))
                B[4].copied(pe)
                for s in range(2):
                    p = slice(s * CH, (s + 1) * CH)
                    cur = slice(t * P + s * CH, t * P + (s + 1) * CH)
                    if t or s:
                        B[3].copied(pe)
                    out = B[2].open(pe)
                    for f in range(FT):
                        last = M(out[p, f * P:(f + 1) * P], WT[:, f, p], S[:, f, :], start=True, stop=True)
                    B[2].close(last)
                    for f in range(FT):
                        M(y[:, f * P + s * CH:f * P + (s + 1) * CH], S[:, f, :], rho[:, f, cur],
                          start=False, stop=False, skip_group_check=True)
                    out = B[3].open(pe)
                    B[2].copied(pe)
                    for f in range(FT):
                        M(out[:, f * P:(f + 1) * P], kt[p, f, :], vt[p, f, :], start=True, stop=False)
                        last = M(out[:, f * P:(f + 1) * P], bt[p, f, :], nU[p, f, :], start=False, stop=True)
                    B[3].close(last)
                for par, f in heads():
                    q = slice(par * HD, (par + 1) * HD)
                    last = M(y[q, f * P:(f + 1) * P], nU[:, f, q], G["QbT"][:, par, f, :],
                             start=False, stop=(par, f) == (1, FT - 1), skip_group_check=True)
                B[5].close(last)

        def view(out):
            return out[:, :].rearrange("p (f n) -> p f n", f=FT)

        @block.scalar
        def _(act):
            B = bank_set(ps, sems)
            cp = lambda out, in_: nc.scalar.activation(out, in_, ACT.Copy)
            for t in range(TT):
                o = view(B[4].read(act))
                B[4].empty(cp(kt[:, :, :], o))
                o = view(B[5].read(act))
                cp(Cm[:, 0, :, HD:P], o[:, :, 0:HD])
                B[5].empty(cp(Cm[:, 1, :, HD:P], o[:, :, HD:P]))
                for lv in range(1, LEVELS + 1):
                    if t and lv == 3:
                        fin.root(act, t - 1)
                    for par in range(2):
                        B[4 + par].empty(cp(A[lv % 2][:, par, :, :], view(B[4 + par].read(act))))
                        if lv < LEVELS:
                            B[6 + par].empty(cp(AT[lv % 2][:, par, :, :], view(B[6 + par].read(act))))
                B[4].empty(cp(WT[:, :, :], view(B[4].read(act))))
                B[5].empty(cp(yT[:, 0:FT, t * P:(t + 1) * P], view(B[5].read(act))))

        @block.vector
        def _(dve):
            B = bank_set(ps, sems)
            link = chain(dve, own)
            V_ = nc.vector
            dve.wait_ge(mask_ready, 1)
            dest = dict(AT=(AT[0], 0), QbT=(G["QbT"], 3), NT=(G["NT"], 2), QkT=(G["QkT"], 3), A=(A[0], 1))
            for t in range(TT):
                B[0].empty(V_.tensor_copy(vt[:, :, :], view(B[0].read(dve))))
                B[1].empty(V_.tensor_copy(bt[:, :, :], view(B[1].read(dve))))
                n = 0
                for par in range(2):
                    for g in grams:
                        b = B[(2 + n) % 4]
                        n += 1
                        out, i = dest[g]
                        ins = V_.tensor_tensor(out[:, par, :, :], view(b.read(dve)),
                                               mask[:, i:i + 1, :].to_broadcast([P, FT, P]), ALU.mult)
                        b.empty(ins)
                        if g == "AT":
                            dve.wait_ge(b.emptied, b.n)
                            dve.sem_inc(gram_out, 1)
                if t:
                    fin.centre(dve, B[2], t - 1)
                for lv in range(1, LEVELS + 1):
                    for par in range(2):
                        B[par].empty(V_.tensor_tensor(XT[:, par, :, :], view(B[par].read(dve)), XT[:, par, :, :],
                                                      ALU.add))
                    if t and lv == 2:
                        fin.add_eps(dve, B[3], t - 1)
                    if lv == 4:
                        for par in range(2):
                            B[2 + par].empty(V_.tensor_copy(Cm[:, par, :, 0:HD],
                                                            view(B[2 + par].read(dve))[:, :, par * HD:(par + 1) * HD]))
                    if t and lv == 3:
                        fin.invert(dve, t - 1)
                    elif lv <= 3:
                        search.rounds(dve, PER_LEVEL[t])
                    elif lv == 4:
                        search.rounds(dve, AT_LEVEL_4[t])
                for par in range(2):
                    q = slice(par * HD, (par + 1) * HD)
                    o = view(B[par].read(dve))
                    V_.tensor_copy(U0[:, :, q], o[:, :, 0:HD])
                    B[par].empty(V_.tensor_copy(Wt[:, :, q], o[:, :, HD:P]))
                for par in range(2):
                    dve.wait_ge(B[par].emptied, B[par].n)
                for s in range(2):
                    p = slice(s * CH, (s + 1) * CH)
                    o = view(B[2].read(dve))
                    B[2].empty(V_.scalar_tensor_tensor(out=nU[p, :, :], in0=o[p, :, :], scalar=-1.0, in1=U0[p, :, :],
                                                       op0=ALU.mult, op1=ALU.subtract))
                    o = view(B[3].read(dve))
                    link(V_.tensor_tensor(S[:, :, :], o, S[:, :, :], ALU.add))
                    dve.wait_ge(Wend_done, 2 * t + s + 1)
                    B[3].empty(V_.tensor_tensor(S[:, :, :], S[:, :, :], Wend[s][:, :, :], ALU.mult))
                    dve.wait_ge(B[3].emptied, B[3].n)
                    dve.sem_inc(state_done, 1)
            search.rest(dve)




@stage
def sparse_attend(nc, c, ctx, ps, m, yT, prm, w_out, wts):
    fin = Finish(nc, c, ctx, m, yT)
    LAST = TT - 1
    fin_sems = bank_sems(c, "finish")
    units = [(h, t) for h in range(B_HEADS) for t in range(TT)]
    N = len(units)
    RING, LT, LP = 6, 3, 5
    lg = [c.sb(f"prob{i}", [P, T], ctx=ctx) for i in range(RING)]
    pT = [c.sb(f"probT{i}", [P, T], ctx=ctx) for i in range(2)]
    nmax = c.sb("minus_max", [P, N], ctx=ctx)
    tot = c.sb("total", [P, N], ctx=ctx)
    inv = c.sb("inverse", [P, N], ctx=ctx)
    qk, biased, maxed, exped, inverted, scaled, turned, pT_out, pv, y_out = (
        c.sem(n) for n in ("qk", "biased", "maxed", "exped", "inverted", "scaled", "turned", "pT_out", "pv", "y_out"))
    ps_z, ps_t, ps_y = ps[0:3], ps[3:5], ps[5:7]
    with nc.Block() as block:

        @block.sync
        def _(sp):
            fin.load(sp, prm)
            wts.load_guest(sp, w_out)

        @block.tensor
        def _(pe):
            fin_bank = bank_set(ps, fin_sems)[7]
            fin.sums(pe, fin_bank, LAST)
            for i in range(N + LP):
                if i == 3:
                    fin.variances(pe, fin_bank, LAST, LAST)
                if i < N:
                    h, t = units[i]
                    q = slice((h % 2) * HD, (h % 2 + 1) * HD)
                    if i >= 3:
                        pe.wait_ge(biased, i - 2)
                    nc.tensor.matmul(ps_z[i % 3][:, 0:(t + 1) * P], m.qb[q, h // 2, t * P:(t + 1) * P],
                                     m.kb[q, h // 2, 0:(t + 1) * P], start=True, stop=True).then_inc(qk, 1)
                u = i - LT
                if 0 <= u < N:
                    pe.wait_ge(scaled, u + 1)
                    if u >= 2:
                        pe.wait_ge(pT_out, u - 1)
                    for b in range(units[u][1] + 1):
                        last = nc.tensor.transpose(ps_t[u % 2][:, b * P:(b + 1) * P],
                                                   lg[u % RING][:, b * P:(b + 1) * P], c.ident[:, :])
                    last.then_inc(turned, 1)
                u = i - LP
                if 0 <= u < N:
                    h, t = units[u]
                    q = slice((h % 2) * HD, (h % 2 + 1) * HD)
                    pair = h // 2
                    pe.wait_ge(pT_out, u + 1)
                    if h % 2 == 0 and t == 0 and pair >= 2:
                        pe.wait_ge(y_out, pair - 1)
                    for b in range(t + 1):
                        last = nc.tensor.matmul(ps_y[pair % 2][q, t * P:(t + 1) * P], m.vb[:, b, h * HD:(h + 1) * HD],
                                                pT[u % 2][:, b * P:(b + 1) * P], start=b == 0, stop=b == t)
                    last.then_inc(pv, 1)

        @block.vector
        def _(dve):
            V_ = nc.vector
            fin_bank = bank_set(ps, fin_sems)[7]
            fin.centre(dve, fin_bank, LAST)
            for i in range(N + 1):
                if i == 3:
                    fin.add_eps(dve, fin_bank, LAST)
                if i < N:
                    h, t = units[i]
                    L = (t + 1) * P
                    dve.wait_ge(qk, i + 1)
                    if i >= RING:
                        dve.wait_ge(turned, i - RING + 1)
                    V_.tensor_tensor(lg[i % RING][:, 0:L], ps_z[i % 3][:, 0:L], m.bias[:, t, 0:L],
                                     ALU.add).then_inc(biased, 1)
                    dve.wait_ge(biased, i + 1)
                    V_.tensor_reduce(nmax[:, i:i + 1], lg[i % RING][:, 0:L], AX.X, ALU.max,
                                     negate=True).then_inc(maxed, 1)
                if i >= 1:
                    u = i - 1
                    p = lg[u % RING][:, 0:(units[u][1] + 1) * P]
                    dve.wait_ge(exped, i)
                    V_.reciprocal(inv[:, u:i], tot[:, u:i]).then_inc(inverted, 1)
                    dve.wait_ge(inverted, i)
                    V_.tensor_scalar(p, p, inv[:, u:i], None, ALU.mult).then_inc(scaled, 1)
                if i == N // 2:
                    fin.invert(dve, LAST, LAST)

        @block.scalar
        def _(act):
            for i in range(N + LT):
                if i == 3:
                    fin.root(act, LAST, LAST)
                if i < N:
                    L = (units[i][1] + 1) * P
                    act.wait_ge(maxed, i + 1)
                    nc.scalar.activation(lg[i % RING][:, 0:L], lg[i % RING][:, 0:L], ACT.Exp,
                                         bias=nmax[:, i:i + 1], accum_out=tot[:, i:i + 1]).then_inc(exped, 1)
                u = i - LT
                if u >= 0:
                    L = (units[u][1] + 1) * P
                    act.wait_ge(turned, u + 1)
                    if u >= 2:
                        act.wait_ge(pv, u - 1)
                    nc.scalar.activation(pT[u % 2][:, 0:L], ps_t[u % 2][:, 0:L], ACT.Copy).then_inc(pT_out, 1)
                    if u % 8 == 2 and u > 8:
                        pair = u // 8 - 1
                        act.wait_ge(pv, 8 * (pair + 1))
                        nc.scalar.activation(yT[:, FT + pair, :], ps_y[pair % 2][:, :], ACT.Copy).then_inc(y_out, 1)
            pair = B_HEADS // 2 - 1
            act.wait_ge(pv, N)
            nc.scalar.activation(yT[:, FT + pair, :], ps_y[pair % 2][:, :], ACT.Copy).then_inc(y_out, 1)

        @block.gpsimd
        def _(pool):
            fin.square(pool, LAST, LAST)
            fin.scale(pool, LAST, LAST)


class Mixed:
    pass


def even_mixer(nc, c, ps, x, gain, w_in, w_out, prm, wts, slots, update):
    ctx = c.ctx.enter_context(ExitStack())
    yT = c.sb("yT", [P, KD, T], ctx=ctx)
    with ExitStack() as mid, ExitStack() as short:
        m = Mixed()
        m.qi = c.sb("q_idx", [P, FT, T], ctx=short, side="right")
        m.ck, m.ki, m.lo_da, m.lo_g = (c.sb(n, [P, T], ctx=short, side="right")
                                       for n in ("c_kv", "k_idx", "lora_da", "lora_g"))
        m.wiT = c.sb("w_idxT", [IDX_HEADS, T], ctx=short, side="right")
        m.qb = c.sb("q_b", [P, FT, T], ctx=mid)
        m.rkv = [c.sb(n, [P, FT, T], ctx=mid) for n in "rkv"]
        m.mu = c.sb("mu_rkv", [P, 3, FT], ctx=mid)
        with ExitStack() as proj:
            xn = c.sb("xn", [P, TT, D], ctx=proj)
            even_project(nc, c, proj, ps, x, xn, gain, w_in, m, prm, update)
        m.kb, m.vb, m.bias = (c.sb(n, [P, FT, T], ctx=mid) for n in ("k_b", "v_b", "bias"))
        m.wi = c.sb("w_idx", [P, TT, IDX_HEADS], ctx=mid)
        m.rate, m.gate, m.kk, m.kmod, m.bonus, m.W = (
            c.sb(n, [P, FT, T], ctx=mid) for n in ("rate", "gate", "kk", "k_mod", "bonus", "W"))
        with ExitStack() as prep:
            mixers_prepare(nc, c, prep, ps, m, prm)
        short.close()
        with ExitStack() as chunks:
            rwkv_chunks(nc, c, chunks, ps, m, yT, prm)
        wts.add_slot(slots, SLOTS - 1)
        with ExitStack() as inner:
            sparse_attend(nc, c, inner, ps, m, yT, prm, w_out, wts)
    for j in range(SLOTS - 1):
        wts.add_slot(slots, j)
    return yT, ctx


@stage
def final_norm(nc, c, x, gain, out_dram, combine):
    with ExitStack() as ctx:
        g = c.sb("final_gain", [P, D], ctx=ctx)
        sq = c.sb("squares", [P, TT, D], ctx=ctx)
        ss = c.sb("ss", [P, 2 * TT], ctx=ctx)
        update = combine([c.sb(f"got{j}", [P, TT, D], ctx=ctx) for j in range(2)])
        g_in, summed, root, own, ready, stored = (c.sem(n) for n in ("final_gain_in", "summed", "root", "dve_own",
                                                                     "out_ready", "out_stored"))
        with nc.Block() as block:

            @block.sync
            def _(sp):
                sp.dma_start(g[:, :], gain.rearrange("(o d) -> o d", o=1).to_broadcast([P, D])).then_inc(g_in, 16)
                for t in range(TT):
                    sp.wait_ge(ready, t + 1)
                    sp.dma_start(out_dram[t * P:(t + 1) * P, :], sq[:, t, :]).then_inc(stored, 16)
                sp.wait_ge(stored, 16 * TT)

            update.start(block)

            @block.scalar
            def _(act):
                for t in range(TT):
                    update.wait_tile(act, t)
                    nc.scalar.activation(sq[:, t, :], x[:, t, :], ACT.Square,
                                         accum_out=ss[:, t:t + 1]).then_inc(summed, 1)
                    act.wait_ge(summed, t + 1)
                    nc.scalar.activation(ss[:, TT + t:TT + t + 1], ss[:, t:t + 1], ACT.Sqrt, scale=1.0 / D,
                                         bias=c.eps[:, 0:1]).then_inc(root, 1)

            @block.vector
            def _(dve):
                link = chain(dve, own)
                dve.wait_ge(g_in, 16)
                for t in range(TT + 1):
                    if t < TT:
                        update.add_tile(dve, link, t)
                    if t >= 1:
                        u = t - 1
                        std = ss[:, TT + u:TT + u + 1]
                        dve.wait_ge(root, u + 1)
                        link(nc.vector.reciprocal(std, std))
                        nc.vector.scalar_tensor_tensor(out=sq[:, u, :], in0=x[:, u, :], scalar=std, in1=g[:, :],
                                                       op0=ALU.mult, op1=ALU.mult).then_inc(ready, 1)


def build(nc, a, out):
    with ExitStack() as ctx:
        c = Core(nc, ctx)
        x = c.sb("x", [P, TT, D])
        ps = [ctx.enter_context(nc.psum_tensor(f"ps{i}", [P, BANK], F32)) for i in range(8)]
        xrows = nc.dram_tensor("sorted_rows", [N_ROWS, D], F32).ap()
        yrows = nc.dram_tensor("expert_rows", [N_ROWS, D], F32).ap()
        arriving = Arriving(c, x, a["x"][0])
        constants(nc, c, arriving.load)
        prm = {n: a["a_" + n][0] for n in ("mu_lora", "mu_rkv", "w0", "w1", "w2", "a0", "a1", "a2", "g1", "g2",
                                           "k_k", "k_a", "ln_g", "ln_b")}
        prm["r_k"] = a["a_r_k"][0].rearrange("h d -> (h d)")
        prm.update({n: a["b_" + n][0] for n in ("kv_norm", "w_kv_up", "idx_k_norm")})
        wts = ExpertWeights(c)
        r = Routes(c, ctx)

        def combine(got):
            return Combine(nc, c, x, yrows, r, got)

        depth = a["moe_norm"].shape[0]
        assert depth == 2
        for layer in range(depth):
            wts.start_layer(a["moe_w1"][layer], a["moe_w3"][layer], a["moe_w2"][layer])
            slots = ctx.enter_context(ExitStack())
            if layer % 2 == 0:
                yT = even_mixer(nc, c, ps, x, a["ev_norm"][layer // 2], a["ev_w_in"][layer // 2],
                           a["ev_w_out"][layer // 2], prm, wts, slots, arriving)
            else:
                yT = odd_mixer(nc, c, ps, x, a["od_norm"][layer // 2], a["od_w_qkv"][layer // 2],
                          a["od_w_out"][layer // 2], wts, slots, combine)
            moe(nc, c, ps, x, yT, xrows, yrows, a["moe_norm"][layer], a["moe_router_group"][layer],
                a["moe_router_expert"][layer], wts, slots, r)
        final_norm(nc, c, x, a["final_norm"], out[0], combine)


_INS = ["x", "ev_norm", "ev_w_in", "ev_w_out", "a_mu_rkv", "a_mu_lora", "a_w0", "a_w1", "a_w2", "a_a0", "a_a1",
        "a_a2", "a_g1", "a_g2", "a_k_k", "a_k_a", "a_r_k", "a_ln_g", "a_ln_b", "b_kv_norm", "b_w_kv_up",
        "b_idx_k_norm", "od_norm", "od_w_qkv", "od_w_out", "moe_norm", "moe_router_group", "moe_router_expert",
        "moe_w1", "moe_w3", "moe_w2", "final_norm"]


def kernel(**inputs):
    import numpy as np
    import concourse.bacc as bacc
    from concourse.bass_utils import run_bass_kernel_spmd

    nc = bacc.Bacc("TRN2", target_bir_lowering=False, num_devices=1)
    arrays, args = {}, {}
    for name in _INS:
        arrays[f"in_{name}"] = np.ascontiguousarray(inputs[name])
        args[name] = nc.dram_tensor(f"in_{name}", arrays[f"in_{name}"].shape, F32, kind="ExternalInput").ap()
    shape = inputs["x"].shape
    out = nc.dram_tensor("out_x", shape, F32, kind="ExternalOutput").ap()
    build(nc, args, out)
    r = run_bass_kernel_spmd(nc, [arrays], core_ids=[0])
    return r.results[0]["out_x"]
```
